# Optimizing a Trainium2 kernel written in Bass

```python
import math
import jax, jax.numpy as jnp
from jax import lax
import numpy as np

D_MODEL = 1024
BATCH = 1
SEQ = 1024
DEPTH = 1
DEC_BATCH = 8
DEC_SEQ = 8
PAST_LEN = 8192
PAGE_SIZE = 128

GMLP_W = D_MODEL
GMLP_GROUPS = 4
GMLP_GROUP_DIM = GMLP_W // GMLP_GROUPS
GMLP_CHUNK = 128
MLSTM_W = D_MODEL
MLSTM_HEADS = 4
MLSTM_HEAD_DIM = MLSTM_W // MLSTM_HEADS
MLSTM_CHUNK = 128
CONV_W = 4
D_FF = 2816
N_ADA = 9
EPS = 1e-6
IN_COLS = 2 * GMLP_W + 4 * MLSTM_W + 2 * MLSTM_HEADS + 2 * D_MODEL

kernel_name = 'gated_gmlp_mlstm_macaron_adaln_decoder_step'

def rmsnorm(x, g):
    xf = x.astype(jnp.float32)
    y = xf * lax.rsqrt(jnp.mean(xf * xf, axis=-1, keepdims=True) + EPS)
    return (y * g.astype(jnp.float32)).astype(x.dtype)

def layernorm(x, g, b):
    xf = x.astype(jnp.float32)
    mu = jnp.mean(xf, axis=-1, keepdims=True)
    var = jnp.mean(jnp.square(xf - mu), axis=-1, keepdims=True)
    y = (xf - mu) * lax.rsqrt(var + EPS) * g.astype(jnp.float32) + b.astype(jnp.float32)
    return y.astype(x.dtype)

def modulate(h, shift, scale):
    return h * (1 + scale[:, None, :]) + shift[:, None, :]

def swiglu(h, w_in, w_out):
    a, b = jnp.split(h @ w_in, 2, axis=-1)
    return (jax.nn.silu(a) * b) @ w_out

def causal_conv(x, buf, w, b):
    T = x.shape[1]
    xp = jnp.concatenate([buf.astype(x.dtype), x], axis=1)
    y = b
    for j in range(CONV_W):
        y = y + xp[:, j:j + T] * w[j]
    return y, xp[:, T:]

def gmlp_spatial(u, v, ws, bs):
    B, T, _ = v.shape
    L = min(T, GMLP_CHUNK)
    NC = T // L
    w = jnp.tril(ws[:, :L, :L])
    vg = v.reshape(B, NC, L, GMLP_GROUPS, GMLP_GROUP_DIM)
    bias = jnp.swapaxes(bs[:, :L], 0, 1)[None, None, :, :, None]
    mixed = jnp.einsum('gts,bcsgd->bctgd', w, vg) + bias
    return u * mixed.reshape(B, T, GMLP_W)

def mlstm_chunked(q, k, v, i_pre, f_pre, C0, n0, m0):
    B, T, H, DH = q.shape
    L = math.gcd(T, MLSTM_CHUNK)
    NC = T // L

    def to_chunks(a):
        return jnp.moveaxis(a.reshape(B, NC, L, *a.shape[2:]), 1, 0)

    xs = (to_chunks(q), to_chunks(k), to_chunks(v), to_chunks(i_pre),
          to_chunks(jax.nn.log_sigmoid(f_pre)))
    causal = jnp.tril(jnp.ones((L, L), dtype=bool))

    def step(carry, inp):
        C, n, m = carry
        qb, kb, vb, ib, lfb = inp
        b = jnp.swapaxes(jnp.cumsum(lfb, axis=1), 1, 2)
        ih = jnp.swapaxes(ib, 1, 2)
        inter = b + m[..., None]
        Dm = b[..., :, None] - b[..., None, :] + ih[..., None, :]
        Dm = jnp.where(causal, Dm, -jnp.inf)
        m_t = jnp.maximum(inter, jnp.max(Dm, axis=-1))
        w_inter = jnp.exp(inter - m_t)
        s = jnp.einsum('blhd,bshd->bhls', qb, kb) * jnp.exp(Dm - m_t[..., None])
        num = (w_inter[..., None] * jnp.einsum('blhd,bhde->bhle', qb, C)
               + jnp.einsum('bhls,bshe->bhle', s, vb))
        den = w_inter * jnp.einsum('blhd,bhd->bhl', qb, n) + jnp.sum(s, axis=-1)
        h = num / jnp.maximum(jnp.abs(den), jnp.exp(-m_t))[..., None]
        bL = b[..., -1]
        g = bL[..., None] - b + ih
        m_new = jnp.maximum(bL + m, jnp.max(g, axis=-1))
        a_prev = jnp.exp(bL + m - m_new)
        kw = kb * jnp.swapaxes(jnp.exp(g - m_new[..., None]), 1, 2)[..., None]
        C_new = a_prev[..., None, None] * C + jnp.einsum('bshd,bshe->bhde', kw, vb)
        n_new = a_prev[..., None] * n + jnp.sum(kw, axis=1)
        return (C_new, n_new, m_new), jnp.swapaxes(h, 1, 2)

    (C, n, m), hs = lax.scan(step, (C0, n0, m0), xs)
    return jnp.moveaxis(hs, 0, 1).reshape(B, T, H, DH), C, n, m

def token_mixer(h, conv_buf, C0, n0, m0, w_in, b_gates, conv_w, conv_b, ln_g, ln_b,
                ws, bs, norm_g, w_out):
    B, T, _ = h.shape
    H, DH = MLSTM_HEADS, MLSTM_HEAD_DIM
    z = h @ w_in
    u = jax.nn.gelu(z[..., :GMLP_W])
    v = layernorm(jax.nn.gelu(z[..., GMLP_W:2 * GMLP_W]), ln_g, ln_b)
    y_a = gmlp_spatial(u, v, ws, bs)
    s0 = 2 * GMLP_W
    qk, new_buf = causal_conv(z[..., s0:s0 + 2 * MLSTM_W], conv_buf, conv_w, conv_b)
    qk = jax.nn.silu(qk)
    s0 += 2 * MLSTM_W
    vm = z[..., s0:s0 + MLSTM_W]
    s0 += MLSTM_W
    o = z[..., s0:s0 + MLSTM_W]
    s0 += MLSTM_W
    gif = (z[..., s0:s0 + 2 * H] + b_gates).astype(jnp.float32)
    s0 += 2 * H
    g_a = z[..., s0:s0 + D_MODEL]
    g_b = z[..., s0 + D_MODEL:s0 + 2 * D_MODEL]

    def heads(a):
        return a.astype(jnp.float32).reshape(B, T, H, DH)

    q = heads(qk[..., :MLSTM_W])
    k = heads(qk[..., MLSTM_W:]) * (DH ** -0.5)
    ht, C, n, m = mlstm_chunked(q, k, heads(vm), gif[..., :H], gif[..., H:],
                                C0.astype(jnp.float32), n0.astype(jnp.float32),
                                m0.astype(jnp.float32))
    mu = jnp.mean(ht, axis=-1, keepdims=True)
    var = jnp.mean(jnp.square(ht - mu), axis=-1, keepdims=True)
    hn = (ht - mu) * lax.rsqrt(var + EPS) * norm_g.astype(jnp.float32).reshape(H, DH)
    y_b = jax.nn.sigmoid(o) * hn.reshape(B, T, MLSTM_W).astype(h.dtype)
    mix = jax.nn.sigmoid(g_a) * y_a + jax.nn.sigmoid(g_b) * y_b
    return mix @ w_out, new_buf, C, n, m, v

def run_trunk(x, c, conv0, C0, n0, m0, w_ada, b_ada, g_ffn1, w_ffn1_in, w_ffn1_out, g_mix,
              w_in, b_gates, conv_w, conv_b, gmlp_ln_g, gmlp_ln_b, gmlp_ws, gmlp_bs,
              mlstm_norm_g, w_out, g_ffn2, w_ffn2_in, w_ffn2_out, w_ada_final, b_ada_final,
              g_final):
    B = x.shape[0]
    cs = jax.nn.silu(c)
    outs = []
    for l in range(DEPTH):
        ada = (cs @ w_ada[l] + b_ada[l]).reshape(B, N_ADA, D_MODEL)
        sh1, sc1, gt1, sh2, sc2, gt2, sh3, sc3, gt3 = [ada[:, j] for j in range(N_ADA)]
        h = modulate(rmsnorm(x, g_ffn1[l]), sh1, sc1)
        x = x + 0.5 * gt1[:, None] * swiglu(h, w_ffn1_in[l], w_ffn1_out[l])
        h = modulate(rmsnorm(x, g_mix[l]), sh2, sc2)
        out, buf, C, n, m, v = token_mixer(h, conv0[l], C0[l], n0[l], m0[l], w_in[l], b_gates[l],
                                           conv_w[l], conv_b[l], gmlp_ln_g[l], gmlp_ln_b[l],
                                           gmlp_ws[l], gmlp_bs[l], mlstm_norm_g[l], w_out[l])
        x = x + gt2[:, None] * out
        h = modulate(rmsnorm(x, g_ffn2[l]), sh3, sc3)
        x = x + 0.5 * gt3[:, None] * swiglu(h, w_ffn2_in[l], w_ffn2_out[l])
        outs.append((buf, C.astype(x.dtype), n.astype(x.dtype), m.astype(x.dtype), v))
    fin = cs @ w_ada_final + b_ada_final
    shf, scf = jnp.split(fin, 2, axis=-1)
    y = modulate(rmsnorm(x, g_final), shf, scf)
    buf_s = jnp.stack([o[0] for o in outs])
    C_s = jnp.stack([o[1] for o in outs])
    n_s = jnp.stack([o[2] for o in outs])
    m_s = jnp.stack([o[3] for o in outs])
    v_s = jnp.stack([o[4] for o in outs])
    return y, buf_s, C_s, n_s, m_s, v_s

def setup_inputs(seed: int = 0) -> dict:
    key = jax.random.key(seed)
    ks = iter(jax.random.split(key, 48))

    def nrm(shape, s):
        return s * jax.random.normal(next(ks), shape, jnp.float32)

    D, H, DH = D_MODEL, MLSTM_HEADS, MLSTM_HEAD_DIM
    f_bias = jnp.linspace(3.0, 6.0, H, dtype=jnp.float32)
    b_gates = jnp.concatenate([nrm((DEPTH, H), 0.1), f_bias[None] + nrm((DEPTH, H), 0.1)], axis=-1)
    return {
        'x_prompt': nrm((BATCH, SEQ, D), 1.0),
        'x_sample': nrm((DEC_BATCH, DEC_SEQ, D), 1.0),
        'c_prompt': nrm((BATCH, D), 1.0),
        'c_sample': nrm((DEC_BATCH, D), 1.0),
        'state_mlstm_C': nrm((DEPTH, DEC_BATCH, H, DH, DH), 0.1),
        'state_mlstm_n': nrm((DEPTH, DEC_BATCH, H, DH), 1.0),
        'state_mlstm_m': nrm((DEPTH, DEC_BATCH, H), 0.5),
        'state_conv': nrm((DEPTH, DEC_BATCH, CONV_W - 1, 2 * MLSTM_W), 1.0),
        'w_ada': nrm((DEPTH, D, N_ADA * D), 0.5 * D ** -0.5),
        'b_ada': nrm((DEPTH, N_ADA * D), 0.1),
        'g_ffn1': 1.0 + nrm((DEPTH, D), 0.1),
        'w_ffn1_in': nrm((DEPTH, D, 2 * D_FF), D ** -0.5),
        'w_ffn1_out': nrm((DEPTH, D_FF, D), D_FF ** -0.5),
        'g_mix': 1.0 + nrm((DEPTH, D), 0.1),
        'w_in': nrm((DEPTH, D, IN_COLS), D ** -0.5),
        'b_gates': b_gates,
        'conv_w': nrm((DEPTH, CONV_W, 2 * MLSTM_W), CONV_W ** -0.5),
        'conv_b': nrm((DEPTH, 2 * MLSTM_W), 0.02),
        'gmlp_ln_g': 1.0 + nrm((DEPTH, GMLP_W), 0.1),
        'gmlp_ln_b': nrm((DEPTH, GMLP_W), 0.02),
        'gmlp_ws': nrm((DEPTH, GMLP_GROUPS, GMLP_CHUNK, GMLP_CHUNK), 0.05),
        'gmlp_bs': 1.0 + nrm((DEPTH, GMLP_GROUPS, GMLP_CHUNK), 0.1),
        'mlstm_norm_g': 1.0 + nrm((DEPTH, MLSTM_W), 0.1),
        'w_out': nrm((DEPTH, D, D), D ** -0.5),
        'g_ffn2': 1.0 + nrm((DEPTH, D), 0.1),
        'w_ffn2_in': nrm((DEPTH, D, 2 * D_FF), D ** -0.5),
        'w_ffn2_out': nrm((DEPTH, D_FF, D), D_FF ** -0.5),
        'w_ada_final': nrm((D, 2 * D), 0.5 * D ** -0.5),
        'b_ada_final': nrm((2 * D,), 0.1),
        'g_final': 1.0 + nrm((D,), 0.1),
    }

def reference(x_prompt, x_sample, c_prompt, c_sample, state_mlstm_C, state_mlstm_n,
              state_mlstm_m, state_conv, w_ada, b_ada, g_ffn1, w_ffn1_in, w_ffn1_out, g_mix,
              w_in, b_gates, conv_w, conv_b, gmlp_ln_g, gmlp_ln_b, gmlp_ws, gmlp_bs,
              mlstm_norm_g, w_out, g_ffn2, w_ffn2_in, w_ffn2_out, w_ada_final, b_ada_final,
              g_final):
    weights = (w_ada, b_ada, g_ffn1, w_ffn1_in, w_ffn1_out, g_mix, w_in, b_gates, conv_w,
               conv_b, gmlp_ln_g, gmlp_ln_b, gmlp_ws, gmlp_bs, mlstm_norm_g, w_out, g_ffn2,
               w_ffn2_in, w_ffn2_out, w_ada_final, b_ada_final, g_final)
    Bp = x_prompt.shape[0]
    H, DH = MLSTM_HEADS, MLSTM_HEAD_DIM
    conv0 = jnp.zeros((DEPTH, Bp, CONV_W - 1, 2 * MLSTM_W), x_prompt.dtype)
    C0 = jnp.zeros((DEPTH, Bp, H, DH, DH), jnp.float32)
    n0 = jnp.zeros((DEPTH, Bp, H, DH), jnp.float32)
    m0 = jnp.zeros((DEPTH, Bp, H), jnp.float32)
    y_prompt, conv_p, C_p, n_p, m_p, _ = run_trunk(x_prompt, c_prompt, conv0, C0, n0, m0,
                                                   *weights)
    y_sample, conv_s, C_s, n_s, m_s, v_s = run_trunk(x_sample, c_sample, state_conv,
                                                     state_mlstm_C, state_mlstm_n,
                                                     state_mlstm_m, *weights)
    return (y_prompt, y_sample, C_p, n_p, m_p, conv_p, C_s, n_s, m_s, conv_s, v_s)


_drawn_inputs = setup_inputs


def setup_inputs(seed=0):
    import zlib

    import numpy as np

    out = dict(_drawn_inputs(seed))
    spreads = {}
    factors = {'gmlp_ln_b': 2.956, 'gmlp_bs': 4.544, 'mlstm_norm_g': 6.4, 'g_ffn2': 3.81}
    for name, (base, spread) in spreads.items():
        noise = np.random.default_rng([zlib.crc32(name.encode()), seed]).standard_normal(out[name].shape)
        drawn = base * np.exp(spread * noise) if base else spread * noise
        out[name] = __import__('jax').numpy.asarray(drawn.astype(out[name].dtype))
    for name, factor in factors.items():
        out[name] = (out[name] * factor).astype(out[name].dtype)
    return out
```

```python
from contextlib import ExitStack

import concourse.bass as bass
from concourse import mybir

F32 = mybir.dt.float32
F32R = mybir.dt.float32r
ALU = mybir.AluOpType
ACT = mybir.ActivationFunctionType

P = 128
D = 1024
KT = D // P
SEQ = 1024
NSEQ = 8
STOK = 8
T = SEQ + NSEQ * STOK
UNITS = [(0, 384), (384, 384), (768, T - 768)]
TAIL_P = SEQ - 768
DFF = 2816
FB = DFF // 256
H = 4
DH = 256
CW = 4
CHUNK = 128
NCH = SEQ // CHUNK
NTT = NCH + 1
ADA_T = 9 * KT
ALL_T = ADA_T + 2 * KT
EPS = 1e-6
HEAD_STEPS = 162
BIG = 1.0e30
GELU_COLS, V_COLS, Q_COLS, K_COLS, VM_COLS, O_COLS, GATE_COLS = 0, 1024, 2048, 3072, 4096, 5120, 6144
GA_COLS, GB_COLS = 6152, 7176


class Count:

    def __init__(self, ctx, nc, name):
        self.sem = ctx.enter_context(nc.semaphore(name))
        self.base = 0

    def __call__(self, n):
        return self.sem, n + self.base


class Steps:

    def __init__(self, ctx, nc, name):
        self.sem = ctx.enter_context(nc.semaphore(name))
        self.n = 0
        self.turn = None

    def one(self):
        self.n += 1
        return self.sem, 1

    def now(self):
        if self.turn is None:
            return self.sem, self.n
        return self.sem, self.turn * self.stride + self.n

    def enter(self, turn, stride, first=0):
        self.turn, self.stride, self.start, self.first = turn, stride, self.n, first
        self.n -= first * stride

    def leave(self, turns):
        n = self.n + self.first * self.stride
        assert n - self.start == self.stride, (n - self.start, self.stride)
        self.n = self.start + self.stride * turns
        self.turn = None


class Arena:

    def __init__(self, nc):
        self.nc, self.at, self.end = nc, -(-nc.sbuf_base // 32) * 32, nc.sbuf_usable_end
        self.fence = None

    def put(self, name, shape, dtype=F32, at=None):
        size = 4
        for s in shape[1:]:
            size *= s
        size = -(-size // 32) * 32
        offset = self.at if at is None else at
        if at is None:
            self.at += size
        assert offset + size <= self.end, (name, offset + size - self.end)
        t = self.nc.alloc_sbuf_tensor_at(name, shape, dtype, offset=offset)
        return t


def bc(ap, axis, n):
    a = ap.unsqueeze(axis)
    shape = list(a.shape)
    shape[axis] = n
    return a.broadcast_to(shape)


def layer(nc, dbg, stop, I, O):
    with ExitStack() as ctx:
        ar = Arena(nc)

        def cnt(name):
            return Count(ctx, nc, name)

        ps = ctx.enter_context(nc.psum_tensor("ps", [P, 8, 512], F32))

        xT = ar.put("xT", [P, KT, T])
        hi_at = ar.at
        hhi = ar.put("hhi", [P, KT, T], F32R)
        hlo = ar.put("hlo", [P, KT, T], F32R)
        ada = ar.put("ada", [P, ALL_T, 9])
        ident = ar.put("ident", [P, P])
        mean = ar.put("mean", [P, P])
        eps_col = ar.put("eps_col", [P, 1])
        vT = ar.put("vT", [P, 120])
        gp = ar.put("gp", [P, KT])
        gs = ar.put("gs", [P, KT, NSEQ])
        gate_p = ar.put("gate_p", [P, KT])
        gate_s = ar.put("gate_s", [P, KT, NSEQ])
        V_FFN1, V_MIX, V_FFN2, V_FINAL, V_NORM, V_CB, V_CW = 0, 8, 16, 24, 32, 40, 56
        work = ar.at
        dve_steps, act_steps, pool_steps = (Steps(ctx, nc, n) for n in ("dve_steps", "act_steps", "pool_steps"))

        def bring_in():
            ar.at = work
            xtok = ar.put("xtok", [P, NTT, D])
            crow = ar.put("crow", [9, D])
            crow2 = ar.put("crow2", [9, D])
            csT = ar.put("csT", [P, KT, 9], at=hi_at)
            bT = ar.put("bT", [P, ALL_T], at=hi_at + 32 * 9)
            brow = ar.put("brow", [ALL_T, P])
            vrow = ar.put("vrow", [120, P])
            x_in = [cnt(f"x_in{u}") for u in range(3)]
            small_in, made, x_turned, x_kept, c_silu, v_turned, v_kept = (
                cnt(n) for n in ("small_in", "made", "x_turned", "x_kept", "c_silu", "v_turned", "v_kept"))
            x_kept_a = cnt("x_kept_a")
            with nc.Block() as block:
                @block.sync
                def _(sp):
                    sp.dma_start(crow[0:1, :], I["c_prompt"]).then_inc(small_in.sem, 16)
                    sp.dma_start(crow[1:9, :], I["c_sample"]).then_inc(small_in.sem, 16)
                    for u, (t0, n) in enumerate(UNITS):
                        for tt in range(3 * u, 3 * u + (3 if u < 2 else 2)):
                            sp.dma_start(xtok[:, tt, :], I["x_prompt"][0, 128 * tt:128 * tt + 128, :]).then_inc(x_in[u].sem, 16)
                    sp.dma_start(xtok[0:64, 8, :], I["x_sample"].rearrange("b t d -> (b t) d")).then_inc(x_in[2].sem, 16)

                @block.scalar
                def _(act):
                    act.dma_start(brow[0:ADA_T, :], I["b_ada"].rearrange("l (t p) -> (l t) p", p=P)).then_inc(small_in.sem, 16)
                    act.dma_start(brow[ADA_T:ALL_T, :], I["b_ada_final"].rearrange("(t p) -> t p", p=P)).then_inc(small_in.sem, 16)
                    for at, n, src in ((V_FFN1, 8, I["g_ffn1"].rearrange("l (t p) -> (l t) p", p=P)),
                                       (V_MIX, 8, I["g_mix"].rearrange("l (t p) -> (l t) p", p=P)),
                                       (V_FFN2, 8, I["g_ffn2"].rearrange("l (t p) -> (l t) p", p=P)),
                                       (V_FINAL, 8, I["g_final"].rearrange("(t p) -> t p", p=P)),
                                       (V_NORM, 8, I["mlstm_norm_g"].rearrange("l (t p) -> (l t) p", p=P)),
                                       (V_CB, 16, I["conv_b"].rearrange("l (t p) -> (l t) p", p=P)),
                                       (V_CW, 64, I["conv_w"].rearrange("l j (t p) -> (l j t) p", p=P))):
                        act.dma_start(vrow[at:at + n, :], src).then_inc(small_in.sem, 16)
                    act.wait_ge(*small_in(16 * 11))
                    act.activation(crow2[:, :], crow[:, :], ACT.Silu).then_inc(c_silu.sem, 1)
                    act.wait_ge(*v_turned(1))
                    act.activation(csT[:, :, :], ps[:, 6, 0:72], ACT.Copy).then_inc(v_kept.sem, 1)
                    act.wait_ge(*v_turned(2))
                    act.activation(bT[:, :], ps[:, 7, 0:ALL_T], ACT.Copy).then_inc(v_kept.sem, 1)
                    act.activation(vT[:, :], ps[:, 7, 128:248], ACT.Copy).then_inc(v_kept.sem, 1)
                    for g in range(1, 3 * KT, 2):
                        u, k = divmod(g, KT)
                        t0, n = UNITS[u]
                        act.wait_ge(*x_turned(g + 1))
                        act.activation(xT[:, k, t0:t0 + n], ps[:, g % 6, 0:n], ACT.Copy).then_inc(x_kept_a.sem, 1)

                @block.gpsimd
                def _(pool):
                    pool.memset(ident[:, :], 0.0).then_inc(made.sem, 1)
                    pool.memset(mean[:, :], 1.0 / D).then_inc(made.sem, 1)
                    pool.memset(eps_col[:, :], EPS).then_inc(made.sem, 1)
                    pool.wait_ge(*made(3))
                    pool.affine_select(out=ident[:, :], in_=ident[:, :], compare_op=ALU.not_equal, fill=1.0,
                                       base=0, pattern=[[-1, P]], channel_multiplier=1).then_inc(made.sem, 1)

                @block.vector
                def _(dve):
                    for g in range(0, 3 * KT, 2):
                        u, k = divmod(g, KT)
                        t0, n = UNITS[u]
                        dve.wait_ge(*x_turned(g + 1))
                        dve.tensor_copy(xT[:, k, t0:t0 + n], ps[:, g % 6, 0:n]).then_inc(x_kept.sem, 1)

                @block.tensor
                def _(pe):
                    pe.wait_ge(*made(4))
                    pe.wait_ge(*c_silu(1))
                    for k in range(KT):
                        ins = pe.transpose(ps[:, 6, 9 * k:9 * k + 9], crow2[:, 128 * k:128 * k + 128], ident[0:9, 0:9])
                    ins.then_inc(v_turned.sem, 1)
                    pe.transpose(ps[:, 7, 0:ALL_T], brow[:, :], ident[0:ALL_T, 0:ALL_T])
                    pe.transpose(ps[:, 7, 128:248], vrow[:, :], ident[0:120, 0:120]).then_inc(v_turned.sem, 1)
                    for g in range(3 * KT):
                        u, k = divmod(g, KT)
                        if g % KT == 0:
                            pe.wait_ge(*x_in[u](48))
                        if g >= 6:
                            e, m = (x_kept, (g - 6) // 2 + 1) if g % 2 == 0 else (x_kept_a, (g - 7) // 2 + 1)
                            pe.wait_ge(*e(m))
                        for c in range(3):
                            tt = 3 * u + c
                            rows = 64 if tt == 8 else P
                            ins = pe.transpose(ps[:, g % 6, 128 * c:128 * c + rows],
                                               xtok[0:rows, tt, 128 * k:128 * k + 128], ident[0:rows, 0:rows])
                        ins.then_inc(x_turned.sem, 1)
            return csT, bT

        def ada_vectors(csT, bT):
            ar.at = work
            RING = 4
            GROUPS = ALL_T // (2 * RING)
            wa = ar.put("wa", [P, RING, KT, 256])
            w_in = [cnt(f"ada_w_in{s}") for s in range(RING)]
            w_used, done, kept = cnt("ada_w_used"), cnt("ada_done"), cnt("ada_kept")
            wa_d = I["w_ada"][0].rearrange("(k p) n -> p k n", p=P)
            wf_d = I["w_ada_final"].rearrange("(k p) n -> p k n", p=P)
            with nc.Block() as block:
                @block.sync
                def _(sp):
                    def load(s, src):
                        sp.dma_start(wa[:, s, :, :], src).then_inc(w_in[s].sem, 16)
                    for s in range(RING):
                        load(s, wa_d[:, :, 256 * s:256 * s + 256])
                    with sp.Fori(1, GROUPS - 2) as g:
                        for s in range(RING):
                            sp.wait_ge(*w_used(g * RING + (s - RING + 1)))
                            load(s, wa_d[:, :, bass.ds(g * (256 * RING) + 256 * s, 256)])
                    for g in range(2):
                        for s in range(RING):
                            sp.wait_ge(*w_used((g + GROUPS - 3) * RING + s + 1))
                            load(s, wf_d[:, :, 256 * (g * RING + s):256 * (g * RING + s) + 256])

                @block.tensor
                def _(pe):
                    def group(g, bank):
                        for s in range(RING):
                            pe.wait_ge(*w_in[s](g * 16 + 16))
                            for i in range(2):
                                for k in range(KT):
                                    ins = pe.matmul(ps[:, bank, 9 * (2 * s + i):9 * (2 * s + i) + 9],
                                                    wa[:, s, k, 128 * i:128 * i + 128], csT[:, k, :],
                                                    start=(k == 0), stop=(k == KT - 1))
                            ins.then_inc(w_used.sem, 1)
                    group(0, 0)
                    with pe.Fori(1, GROUPS) as g:
                        pe.wait_ge(*kept(g))
                        group(g, 0)

                @block.vector
                def _(dve):
                    with dve.Fori(0, GROUPS) as g:
                        dve.wait_ge(*w_used(g * RING + RING))
                        dve.tensor_tensor(ada[:, bass.ds(g * 8, 8), :],
                                          ps[:, 0, 0:72].rearrange("p (j s) -> p j s", s=9),
                                          bc(bT[:, bass.ds(g * 8, 8)], 2, 9), ALU.add).then_inc(kept.sem, 1)

        NS = {}

        def norm(g_at, shift, scale, final=False):
            ar.at = work
            tag = f"n{len(NS)}_"
            NS[tag] = 1
            RINGS = 4
            sq = ar.put(tag + "sq", [P, RINGS, 384])
            tt = ar.put(tag + "t", [P, RINGS, 384])
            rr = ar.put(tag + "r", [P, T])
            ts = ar.put(tag + "ts", [P, KT, NSEQ, STOK])
            y = ar.put(tag + "y", [P, KT, T], at=hi_at) if final else None
            sq_done, ss_step, rms_done, t_done, hi_done, lo_done = (
                norm_counts[n] for n in ("sq_done", "ss_step", "rms_done", "t_done", "hi_done", "lo_done"))
            with nc.Block() as block:
                @block.scalar
                def _(act):
                    def root(n):
                        t0, w = UNITS[n]
                        act.wait_ge(*ss_step(n * KT + KT))
                        act.activation(rr[:, t0:t0 + w], ps[:, n, 0:w], ACT.Sqrt, bias=eps_col[:, 0:1]).then_inc(rms_done.sem, 1)

                    for n, (t0, w) in enumerate(UNITS):
                        for k in range(KT):
                            j = n * KT + k
                            if j >= RINGS:
                                act.wait_ge(*ss_step(j - RINGS + 1))
                            act.activation(sq[:, j % RINGS, 0:w], xT[:, k, t0:t0 + w], ACT.Square).then_inc(sq_done.sem, 1)
                        if n:
                            root(n - 1)
                    root(2)
                    for n, (t0, w) in enumerate(UNITS):
                        wp = w if n < 2 else TAIL_P
                        for k in range(KT):
                            j = n * KT + k
                            act.wait_ge(*t_done(j + 1))
                            dst = y if final else hhi
                            act.activation(dst[:, k, t0:t0 + wp], tt[:, j % RINGS, 0:wp], ACT.Identity,
                                           bias=ada[:, shift + k, 0:1]).then_inc(hi_done.sem, 1)
                    act.wait_ge(*t_done(3 * KT + 1))
                    act.activation((y if final else hhi)[:, :, SEQ:T], ts[:, :, :, :].rearrange("p k s t -> p k (s t)"),
                                   ACT.Copy).then_inc(hi_done.sem, 1)

                @block.tensor
                def _(pe):
                    for n, (t0, w) in enumerate(UNITS):
                        for k in range(KT):
                            j = n * KT + k
                            pe.wait_ge(*sq_done(j + 1))
                            pe.matmul(ps[:, n, 0:w], mean[:, :], sq[:, j % RINGS, 0:w],
                                      start=(k == 0), stop=(k == KT - 1)).then_inc(ss_step.sem, 1)

                @block.vector
                def _(dve):
                    own = dve_steps
                    dve.scalar_tensor_tensor(out=gp[:, :], in0=ada[:, scale:scale + KT, 0], scalar=1.0,
                                             in1=vT[:, g_at:g_at + KT], op0=ALU.add, op1=ALU.mult).then_inc(*own.one())
                    dve.scalar_tensor_tensor(out=gs[:, :, :], in0=ada[:, scale:scale + KT, 1:9], scalar=1.0,
                                             in1=bc(vT[:, g_at:g_at + KT], 2, NSEQ), op0=ALU.add,
                                             op1=ALU.mult).then_inc(*own.one())

                    def low(j):
                        n, k = divmod(j, KT)
                        t0, w = UNITS[n]
                        wp = w if n < 2 else TAIL_P
                        dve.wait_ge(*hi_done(j + 1))
                        dve.scalar_tensor_tensor(out=hlo[:, k, t0:t0 + wp], in0=tt[:, j % RINGS, 0:wp],
                                                 scalar=ada[:, shift + k, 0:1],
                                                 in1=hhi[:, k, t0:t0 + wp].bitcast(F32),
                                                 op0=ALU.add, op1=ALU.subtract).then_inc(lo_done.sem, 1)

                    for n, (t0, w) in enumerate(UNITS):
                        wp = w if n < 2 else TAIL_P
                        dve.wait_ge(*rms_done(n + 1))
                        dve.reciprocal(rr[:, t0:t0 + w], rr[:, t0:t0 + w]).then_inc(*own.one())
                        dve.wait_ge(*own.now())
                        for k in range(KT):
                            j = n * KT + k
                            if j >= RINGS:
                                dve.wait_ge(*(hi_done if final else lo_done)(j - RINGS + 1))
                            dve.scalar_tensor_tensor(out=tt[:, j % RINGS, 0:wp], in0=xT[:, k, t0:t0 + wp],
                                                     scalar=gp[:, k:k + 1], in1=rr[:, t0:t0 + wp],
                                                     op0=ALU.mult, op1=ALU.mult).then_inc(t_done.sem, 1)
                            if not final and j >= 2:
                                low(j - 2)
                    if not final:
                        low(3 * KT - 2)
                        low(3 * KT - 1)
                    xs = xT[:, :, SEQ:T].rearrange("p k (s t) -> p k s t", t=STOK)
                    dve.tensor_tensor(ts[:, :, :, :], xs, bc(gs[:, :, :], 3, STOK), ALU.mult).then_inc(*own.one())
                    dve.wait_ge(*own.now())
                    tsf = ts[:, :, :, :].rearrange("p k s t -> p k (s t)")
                    dve.tensor_tensor(tsf, tsf, bc(rr[:, SEQ:T], 1, KT), ALU.mult).then_inc(*own.one())
                    dve.wait_ge(*own.now())
                    dve.tensor_tensor(ts[:, :, :, :], ts[:, :, :, :], bc(ada[:, shift:shift + KT, 1:9], 3, STOK),
                                      ALU.add).then_inc(t_done.sem, 1)
                    if not final:
                        dve.wait_ge(*hi_done(3 * KT + 1))
                        dve.wait_ge(*t_done(3 * KT + 1))
                        dve.tensor_tensor(hlo[:, :, SEQ:T], tsf, hhi[:, :, SEQ:T].bitcast(F32), ALU.subtract).then_inc(*own.one())
            sq_done.base += 3 * KT
            rms_done.base += 3
            ss_step.base += 3 * KT
            t_done.base += 3 * KT + 1
            hi_done.base += 3 * KT + 1
            lo_done.base += 0 if final else 3 * KT
            return y

        norm_counts = {n: cnt(n) for n in ("sq_done", "ss_step", "rms_done", "t_done", "hi_done", "lo_done")}

        ffn_counts = {n: cnt("ffn_" + n) for n in (
            "a_in", "b_in", "o_in", "a_hi", "b_hi", "o_hi", "a_lo", "b_lo", "o_lo",
            "a_unit", "b_unit", "out_unit", "silu", "hidden", "hid_hi", "hid_lo", "x_added")}
        ffn_mem = {}

        def residual_gates(gate, factor):
            with nc.Block() as block:
                @block.vector
                def _(dve):
                    dve.tensor_scalar(gate_p[:, :], ada[:, gate:gate + KT, 0], factor, None, ALU.mult).then_inc(*dve_steps.one())
                    dve.tensor_scalar(gate_s[:, :, :], ada[:, gate:gate + KT, 1:9], factor, None, ALU.mult).then_inc(*dve_steps.one())
                    dve.wait_ge(*dve_steps.now())

        OUT_ORDER = [(0, 0), (0, 1), (1, 0), (1, 1), (0, 2), (1, 2)] + [(m, n) for m in range(2, KT) for n in range(3)]

        def add_out(dve, own, m, n, bank, tmp, x_added):
            t0, w = UNITS[n]
            wp = w if n < 2 else TAIL_P
            ins = dve.scalar_tensor_tensor(out=xT[:, m, t0:t0 + wp], in0=ps[:, bank, 0:wp], scalar=gate_p[:, m:m + 1],
                                           in1=xT[:, m, t0:t0 + wp], op0=ALU.mult, op1=ALU.add)
            if n < 2:
                ins.then_inc(x_added.sem, 1)
                return
            dve.tensor_tensor(tmp, ps[:, bank, TAIL_P:w].rearrange("p (s t) -> p s t", t=STOK),
                              bc(gate_s[:, m, :], 2, STOK), ALU.mult).then_inc(*own.one())
            dve.wait_ge(*own.now())
            xs = xT[:, m, SEQ:T].rearrange("p (s t) -> p s t", t=STOK)
            dve.tensor_tensor(xs, xs, tmp, ALU.add).then_inc(x_added.sem, 1)

        def ffn(w_up, w_down):
            if not ffn_mem:
                ar.at = work
                for nm in ("a", "b", "o"):
                    ffn_mem[nm + "_raw"] = None
                    ffn_mem[nm + "_hi"] = ar.put(f"w{nm}_hi", [P, 2048], F32R)
                    at = ar.at
                    ffn_mem[nm + "_lo"] = ar.put(f"w{nm}_lo", [P, 2048], F32R)
                    ffn_mem[nm + "_raw"] = ar.put(f"w{nm}_raw", [P, 2048], at=at)
                ffn_mem["g_hi"] = ar.put("g_hi", [P, 2, T], F32R)
                ffn_mem["g_lo"] = ar.put("g_lo", [P, 2, T], F32R)
                ffn_mem["st"] = ar.put("st", [P, 3, 384])
                ffn_mem["hf"] = ar.put("hf", [P, 3, 384])
                ffn_mem["tmp"] = ar.put("ffn_tmp", [P, 4, NSEQ, STOK])
            M = ffn_mem
            C = ffn_counts
            up_d = w_up.rearrange("(k p) n -> p k n", p=P)
            down_d = w_down.rearrange("(b k p) n -> p b k n", k=2, p=P)

            def part(nm, kind, i):
                t = M[f"{nm}_{kind}"]
                if nm == "o":
                    return t[:, 1024 * i:1024 * i + 1024]
                return t[:, :].rearrange("p (k n) -> p k n", n=256)[:, :, 128 * i:128 * i + 128]

            with nc.Block() as block:
                @block.sync
                def _(sp):
                    def load(nm, b):
                        dst = M[f"{nm}_raw"]
                        if nm == "o":
                            src = down_d[:, b, :, :] if isinstance(b, int) else down_d[:, bass.ds(b, 1), :, :].squeeze(1)
                            sp.dma_start(dst[:, :].rearrange("p (k n) -> p k n", k=2), src).then_inc(C["o_in"].sem, 16)
                        else:
                            off = 0 if nm == "a" else DFF
                            sp.dma_start(dst[:, :].rearrange("p (k n) -> p k n", k=KT),
                                         up_d[:, :, bass.ds(b * 256 + off, 256)]).then_inc(C[nm + "_in"].sem, 16)
                    load("a", 0)
                    load("b", 0)
                    load("o", 0)
                    with sp.Fori(1, FB) as b:
                        sp.wait_ge(*C["a_unit"](b * 6))
                        load("a", b)
                        sp.wait_ge(*C["b_unit"](b * 6))
                        load("b", b)
                        sp.wait_ge(*C["out_unit"](b * 24))
                        load("o", b)

                def blocks(eng, body):
                    body(0, True, False)
                    with eng.Fori(1, FB - 1) as b:
                        body(b, False, False)
                    body(FB - 1, False, True)

                @block.scalar
                def _(act):
                    def split(nm, i, b):
                        if i == 0:
                            act.wait_ge(*C[nm + "_in"](b * 16 + 16))
                        act.activation(part(nm, "hi", i), part(nm, "raw", i), ACT.Copy).then_inc(C[nm + "_hi"].sem, 1)

                    def silu(i, n, b):
                        act.wait_ge(*C["a_unit"](b * 6 + 3 * i + n + 1))
                        if i == 1:
                            act.wait_ge(*C["hidden"](b * 6 + n + 1))
                        w = UNITS[n][1]
                        act.activation(M["st"][:, n, 0:w], ps[:, n, 0:w], ACT.Silu).then_inc(C["silu"].sem, 1)

                    def hid(i, n, b):
                        t0, w = UNITS[n]
                        act.wait_ge(*C["hidden"](b * 6 + 3 * i + n + 1))
                        act.activation(M["g_hi"][:, i, t0:t0 + w], M["hf"][:, n, 0:w], ACT.Copy).then_inc(C["hid_hi"].sem, 1)

                    def body(b, first, last):
                        for n in range(3):
                            silu(0, n, b)
                        split("b", 1, b)
                        for n in range(3):
                            hid(0, n, b)
                        split("o", 0, b)
                        for n in range(3):
                            silu(1, n, b)
                        split("o", 1, b)
                        for n in range(3):
                            hid(1, n, b)
                        if not last:
                            split("a", 0, b + 1)
                            split("b", 0, b + 1)
                            split("a", 1, b + 1)

                    split("a", 0, 0)
                    split("b", 0, 0)
                    split("a", 1, 0)
                    blocks(act, body)

                @block.vector
                def _(dve):
                    own = dve_steps

                    def split(nm, i, b):
                        dve.wait_ge(*C[nm + "_hi"](b * 2 + i + 1))
                        dve.tensor_tensor(part(nm, "lo", i), part(nm, "raw", i), part(nm, "hi", i).bitcast(F32),
                                          ALU.subtract).then_inc(C[nm + "_lo"].sem, 1)

                    def hidden(i, n, b):
                        w = UNITS[n][1]
                        dve.wait_ge(*C["b_unit"](b * 6 + 3 * i + n + 1))
                        dve.wait_ge(*C["silu"](b * 6 + 3 * i + n + 1))
                        if i == 1:
                            dve.wait_ge(*C["hid_lo"](b * 6 + n + 1))
                            dve.wait_ge(*C["hid_hi"](b * 6 + n + 1))
                        dve.tensor_tensor(M["hf"][:, n, 0:w], M["st"][:, n, 0:w], ps[:, 3 + n, 0:w],
                                          ALU.mult).then_inc(C["hidden"].sem, 1)

                    def low(i, n, b):
                        t0, w = UNITS[n]
                        dve.wait_ge(*C["hid_hi"](b * 6 + 3 * i + n + 1))
                        dve.tensor_tensor(M["g_lo"][:, i, t0:t0 + w], M["hf"][:, n, 0:w],
                                          M["g_hi"][:, i, t0:t0 + w].bitcast(F32), ALU.subtract).then_inc(C["hid_lo"].sem, 1)

                    def body(b, first, last):
                        split("b", 1, b)
                        hidden(0, 0, b)
                        hidden(0, 1, b)
                        low(0, 0, b)
                        hidden(0, 2, b)
                        low(0, 1, b)
                        low(0, 2, b)
                        split("o", 0, b)
                        split("o", 1, b)
                        hidden(1, 0, b)
                        low(1, 0, b)
                        hidden(1, 1, b)
                        low(1, 1, b)
                        hidden(1, 2, b)
                        low(1, 2, b)
                        for u, (m, n) in enumerate(OUT_ORDER):
                            dve.wait_ge(*C["out_unit"](b * 24 + u + 1))
                            add_out(dve, own, m, n, u % 6, M["tmp"][:, m % 4, :, :], C["x_added"])
                            if not last and u in (3, 9, 15):
                                split(*{3: ("a", 0), 9: ("b", 0), 15: ("a", 1)}[u], b + 1)

                    split("a", 0, 0)
                    split("b", 0, 0)
                    split("a", 1, 0)
                    body(0, True, False)
                    with dve.Fori(1, FB - 1) as b:
                        own.enter(b, KT, first=1)
                        body(b, False, False)
                        own.leave(FB - 2)
                    body(FB - 1, False, True)

                @block.tensor
                def _(pe):
                    def three(bank, w, pairs):
                        last = len(pairs) - 1
                        for j, (wh, wl, xh, xl) in enumerate(pairs):
                            pe.matmul(ps[:, bank, 0:w], wh, xh, start=(j == 0), stop=False)
                            pe.matmul(ps[:, bank, 0:w], wh, xl, start=False, stop=False)
                            ins = pe.matmul(ps[:, bank, 0:w], wl, xh, start=False, stop=(j == last))
                        return ins

                    def up(nm, i, b, first):
                        pe.wait_ge(*C[nm + "_lo"](b * 2 + i + 1))
                        for n, (t0, w) in enumerate(UNITS):
                            bank = n if nm == "a" else 3 + n
                            if i == 1:
                                pe.wait_ge(*C["silu" if nm == "a" else "hidden"](b * 6 + n + 1))
                            elif not first:
                                pe.wait_ge(*C["x_added"](b * 24 - 6 + bank + 1))
                            wh, wl = part(nm, "hi", i), part(nm, "lo", i)
                            ins = three(bank, w, [(wh[:, k, :], wl[:, k, :], hhi[:, k, t0:t0 + w], hlo[:, k, t0:t0 + w])
                                                  for k in range(KT)])
                            ins.then_inc(C[nm + "_unit"].sem, 1)

                    def body(b, first, last):
                        up("a", 0, b, first)
                        up("b", 0, b, first)
                        up("a", 1, b, first)
                        up("b", 1, b, first)
                        pe.wait_ge(*C["o_lo"](b * 2 + 2))
                        for u, (m, n) in enumerate(OUT_ORDER):
                            t0, w = UNITS[n]
                            if u < 3:
                                pe.wait_ge(*C["silu"](b * 6 + 3 + u + 1))
                            elif u < 6:
                                pe.wait_ge(*C["hidden"](b * 6 + u + 1))
                            else:
                                pe.wait_ge(*C["x_added"](b * 24 + u - 6 + 1))
                            if m == 0:
                                pe.wait_ge(*C["hid_lo"](b * 6 + 3 + n + 1))
                            ms = slice(128 * m, 128 * m + 128)
                            ins = three(u % 6, w, [(part("o", "hi", i)[:, ms], part("o", "lo", i)[:, ms],
                                                    M["g_hi"][:, i, t0:t0 + w], M["g_lo"][:, i, t0:t0 + w])
                                                   for i in range(2)])
                            ins.then_inc(C["out_unit"].sem, 1)

                    blocks(pe, body)

            for n, c in C.items():
                c.base += {"a_in": 16, "b_in": 16, "o_in": 16, "a_hi": 2, "b_hi": 2, "o_hi": 2, "a_lo": 2, "b_lo": 2,
                           "o_lo": 2, "a_unit": 6, "b_unit": 6, "out_unit": 24,
                           "silu": 6, "hidden": 6, "hid_hi": 6, "hid_lo": 6, "x_added": 24}[n] * FB

        def mixer_memory():
            ar.at = work
            m = {}
            m["m_rows"] = ar.put("m_rows", [H, T])
            m["tok"] = ar.put("tok", [P, NTT, 4, H])
            m["a_prev"] = ar.put("a_prev", [H, 16])
            m["m_new"] = ar.put("m_new", [H, 16])
            m["conv_in"] = ar.put("conv_in", [P, 2, KT, NSEQ * 3])
            m["n_in"] = ar.put("n_in", [P, 2, NSEQ, H])
            m["tails"] = ar.put("tails", [P, 2 * KT, 27])
            m["n_out"] = ar.put("n_out", [P, 2, NSEQ, H])
            m["np_out"] = ar.put("np_out", [P, 2, H])
            m["neg_mask"] = ar.put("neg_mask", [P, P])
            m["neg_diag"] = ar.put("neg_diag", [64, 64])
            m["seq_mask"] = ar.put("seq_mask", [64, NSEQ])
            m["half"] = ar.put("half", [P, NTT])
            m["w_hi"], m["w_lo"], m["w_raw"] = [], [], []
            m["ring_at"] = ar.at
            for s in range(2):
                m["w_hi"].append(ar.put(f"mw{s}_hi", [P, 2048], F32R))
                at = ar.at
                m["w_lo"].append(ar.put(f"mw{s}_lo", [P, 2048], F32R))
                m["w_raw"].append(ar.put(f"mw{s}_raw", [P, 2048], at=at))
            return m, ar.at

        def pair_part(M, kind, slot, i, rows=False):
            t = M["w_" + kind][slot]
            if rows:
                return t[:, 1024 * i:1024 * i + 1024]
            return t[:, :].rearrange("p (k n) -> p k n", n=256)[:, :, 128 * i:128 * i + 128]

        def three(pe, out, operands):
            last = len(operands) - 1
            for j, (wh, wl, xh, xl) in enumerate(operands):
                pe.matmul(out, wh, xh, start=(j == 0), stop=False)
                pe.matmul(out, wh, xl, start=False, stop=False)
                ins = pe.matmul(out, wl, xh, start=False, stop=(j == last))
            return ins

        def split_counts():
            return cnt("mw_hi_done"), cnt("mw_lo_done")

        w_d = I["w_in"][0].rearrange("(k p) n -> p k n", p=P)

        def gates_and_v(M, free, v_raw):
            ar.at = free
            rows_i = ar.put("rows_i", [H, T])
            rows_l = ar.put("rows_l", [H, T])
            rows_k = ar.put("rows_k", [H, T])
            rows_q = ar.put("rows_q", [P, T])
            bias_i = ar.put("bias_i", [H, 1])
            bias_f = ar.put("bias_f", [H, 1])
            m0 = ar.put("m0", [H, NSEQ])
            b_last = ar.put("b_last", [H, 16])
            a_max = ar.put("a_max", [H, 16])
            m_prev = ar.put("m_prev", [H, 16])
            m_last = ar.put("m_last", [H, 16])
            m_rows, tok, a_prev, m_new = M["m_rows"], M["tok"], M["a_prev"], M["m_new"]
            zeroed, gate_in, small, v_in = cnt("g_zeroed"), cnt("gate_in"), cnt("gate_small"), [cnt(f"v_in{p}") for p in range(4)]
            g_unit, v_unit, v_kept = cnt("gate_unit"), cnt("v_unit"), cnt("gelu_v_kept")
            hi_done, lo_done = cnt("gv_hi_done"), cnt("gv_lo_done")
            abs_ready, log_ready, e_ready, e_done = cnt("abs_ready"), cnt("log_ready"), cnt("e_ready"), cnt("e_done")
            q_turned, tok_done, m_out = cnt("q_turned"), cnt("tok_done"), cnt("m_out")
            PRO, SAM = slice(0, SEQ), slice(SEQ, T)

            def chunks(row):
                return (row[:, PRO].rearrange("h (c t) -> h c t", t=CHUNK), row[:, SAM].rearrange("h (c t) -> h c t", t=STOK))

            with nc.Block() as block:
                @block.sync
                def _(sp):
                    sp.wait_ge(*zeroed(1))
                    gw = pair_part(M, "raw", 0, 0)
                    sp.dma_start(gw[:, :, 0:4], w_d[:, :, GATE_COLS:GATE_COLS + 4]).then_inc(gate_in.sem, 16)
                    sp.dma_start(gw[:, :, 32:36], w_d[:, :, GATE_COLS + 4:GATE_COLS + 8]).then_inc(gate_in.sem, 16)
                    for p in range(4):
                        if p == 1:
                            sp.wait_ge(*g_unit(3))
                        if p > 1:
                            sp.wait_ge(*v_unit(9 * (p - 1)))
                        sp.dma_start(M["w_raw"][(p + 1) % 2][:, :].rearrange("p (k n) -> p k n", k=KT),
                                     w_d[:, :, V_COLS + 256 * p:V_COLS + 256 * p + 256]).then_inc(v_in[p].sem, 16)
                    sp.wait_ge(*tok_done(NTT + 1))
                    sp.dma_start(O["m_prompt"].rearrange("l b h -> h (l b)"), m_new[:, 7:8]).then_inc(m_out.sem, 16)
                    with nc.allow_non_contiguous_dma(reason="32 numbers"):
                        sp.dma_start(O["m_sample"].rearrange("l b h -> h (l b)"), m_new[:, 8:16]).then_inc(m_out.sem, 16)
                    sp.wait_ge(*m_out(32))

                @block.gpsimd
                def _(pool):
                    pool.memset(pair_part(M, "raw", 0, 0), 0.0).then_inc(zeroed.sem, 1)
                    with nc.allow_non_contiguous_dma(reason="a few numbers"):
                        pool.dma_start(bias_i[:, :], I["b_gates"][0:1, 0:H].rearrange("l h -> h l")).then_inc(small.sem, 16)
                        pool.dma_start(bias_f[:, :], I["b_gates"][0:1, H:2 * H].rearrange("l h -> h l")).then_inc(small.sem, 16)
                        pool.dma_start(m0[:, :], I["state_mlstm_m"].rearrange("l b h -> h (l b)")).then_inc(small.sem, 16)
                    pool.memset(rows_k[:, :], 1.0).then_inc(*pool_steps.one())
                    pool.memset(m_prev[:, :], 0.0).then_inc(*pool_steps.one())
                    pool.memset(rows_q[:, :], 0.0).then_inc(*pool_steps.one())
                    pool.wait_ge(*pool_steps.now())
                    kp, ks = chunks(rows_k)
                    pool.memset(kp[:, :, 0:1], 0.0).then_inc(*pool_steps.one())
                    pool.memset(ks[:, :, 0:1], 0.0).then_inc(zeroed.sem, 1)

                @block.scalar
                def _(act):
                    act.wait_ge(*gate_in(32))
                    act.activation(pair_part(M, "hi", 0, 0), pair_part(M, "raw", 0, 0), ACT.Copy).then_inc(hi_done.sem, 1)

                    def split(p):
                        act.wait_ge(*v_in[p](16))
                        for i in range(2):
                            s = (p + 1) % 2
                            act.activation(pair_part(M, "hi", s, i), pair_part(M, "raw", s, i), ACT.Copy).then_inc(hi_done.sem, 1)

                    split(0)
                    for p in range(4):
                        for t in range(NTT):
                            rows = 64 if t == 8 else P
                            act.wait_ge(*v_unit(9 * p + t + 1))
                            r0 = 64 if t == 8 else 0
                            act.activation(v_raw[0:rows, t, 256 * p:256 * p + 256], ps[r0:r0 + rows, 3 + t % 3, 0:256],
                                           ACT.Gelu_apprx_tanh).then_inc(v_kept.sem, 1)
                            if t == 1 and p < 3:
                                split(p + 1)
                            if (p, t) == (0, 2):
                                act.wait_ge(*abs_ready(1))
                                act.activation(rows_l[:, :], rows_l[:, :], ACT.Exp, scale=-1.0).then_inc(*act_steps.one())
                                act.wait_ge(*act_steps.now())
                                act.activation(rows_l[:, :], rows_l[:, :], ACT.Ln, bias=1.0).then_inc(log_ready.sem, 1)
                            if (p, t) == (1, 6):
                                act.wait_ge(*e_ready(1))
                                act.activation(a_prev[:, :], m_last[:, :], ACT.Exp).then_inc(*act_steps.one())
                                act.activation(rows_q[32:36, :], rows_k[:, :], ACT.Exp).then_inc(e_done.sem, 1)
                                act.wait_ge(*e_ready(2))
                                act.activation(rows_q[64:68, :], rows_k[:, :], ACT.Exp).then_inc(e_done.sem, 1)
                                act.wait_ge(*e_ready(3))
                                act.activation(rows_q[96:100, :], rows_k[:, :], ACT.Exp, scale=-1.0).then_inc(e_done.sem, 1)

                @block.vector
                def _(dve):
                    own = dve_steps

                    def low(n, s, i):
                        dve.wait_ge(*hi_done(n))
                        dve.tensor_tensor(pair_part(M, "lo", s, i), pair_part(M, "raw", s, i),
                                          pair_part(M, "hi", s, i).bitcast(F32), ALU.subtract).then_inc(lo_done.sem, 1)

                    def split(p):
                        for i in range(2):
                            low(2 * p + i + 2, (p + 1) % 2, i)

                    def link(ins):
                        ins.then_inc(*own.one())
                        dve.wait_ge(*own.now())

                    low(1, 0, 0)
                    split(0)
                    dve.wait_ge(*small(48))
                    dve.wait_ge(*zeroed(2))
                    for n, (t0, w) in enumerate(UNITS):
                        dve.wait_ge(*g_unit(n + 1))
                        dve.tensor_scalar(rows_i[:, t0:t0 + w], ps[0:4, n, 0:w], bias_i[:, 0:1], None, ALU.add).then_inc(*own.one())
                        link(dve.tensor_scalar(m_rows[:, t0:t0 + w], ps[32:36, n, 0:w], bias_f[:, 0:1], None, ALU.add))
                    dve.scalar_tensor_tensor(out=rows_l[:, :], in0=m_rows[:, :], scalar=-1.0, in1=m_rows[:, :],
                                             op0=ALU.mult, op1=ALU.max).then_inc(abs_ready.sem, 1)
                    dve.wait_ge(*log_ready(1))
                    link(dve.scalar_tensor_tensor(out=m_rows[:, :], in0=m_rows[:, :], scalar=0.0, in1=rows_l[:, :],
                                                  op0=ALU.min, op1=ALU.subtract))
                    link(dve.tensor_tensor_scan(rows_l[:, :], rows_k[:, :], m_rows[:, :], 0.0, ALU.mult, ALU.add))
                    dve.tensor_tensor(rows_i[:, :], rows_i[:, :], rows_l[:, :], ALU.subtract).then_inc(*own.one())
                    link(dve.tensor_scalar(rows_k[:, :], rows_k[:, :], -1.0, BIG, ALU.add, ALU.mult))
                    link(dve.tensor_tensor_scan(m_rows[:, :], rows_k[:, :], rows_i[:, :], -BIG, ALU.add, ALU.max))
                    split(1)
                    for dst, src in ((b_last, rows_l), (a_max, m_rows)):
                        sp_, ss_ = chunks(src)
                        dve.tensor_copy(dst[:, 0:8], sp_[:, :, CHUNK - 1]).then_inc(*own.one())
                        link(dve.tensor_copy(dst[:, 8:16], ss_[:, :, STOK - 1]))
                    dve.tensor_copy(m_prev[:, 8:16], m0[:, :]).then_inc(*own.one())
                    dve.tensor_tensor(m_new[:, 8:16], a_max[:, 8:16], m0[:, :], ALU.max).then_inc(*own.one())
                    link(dve.tensor_tensor_scan(m_new[:, 0:8], a_max[:, 0:8], b_last[:, 0:8], 0.0, ALU.max, ALU.add))
                    link(dve.tensor_tensor(m_new[:, 8:16], m_new[:, 8:16], b_last[:, 8:16], ALU.add))
                    link(dve.tensor_copy(m_prev[:, 1:8], m_new[:, 0:7]))
                    link(dve.tensor_tensor(a_max[:, :], m_prev[:, :], a_max[:, :], ALU.max))
                    link(dve.tensor_tensor(m_last[:, :], m_prev[:, :], a_max[:, :], ALU.subtract))
                    for mr, c0, L in zip(chunks(m_rows), (0, 8), (CHUNK, STOK)):
                        link(dve.tensor_tensor(mr, mr, bc(m_prev[:, c0:c0 + 8], 2, L), ALU.max))
                    dve.tensor_copy(rows_q[0:4, :], rows_i[:, :]).then_inc(*own.one())
                    for n, (kr, ir, c0, L) in enumerate(zip(chunks(rows_k), chunks(rows_i), (0, 8), (CHUNK, STOK))):
                        ins = dve.tensor_tensor(kr, ir, bc(a_max[:, c0:c0 + 8], 2, L), ALU.subtract)
                        ins.then_inc(*(own.one() if n == 0 else (e_ready.sem, 1)))
                    dve.wait_ge(*e_done(1))
                    split(2)
                    for n, (kr, mr, c0, L) in enumerate(zip(chunks(rows_k), chunks(m_rows), (0, 8), (CHUNK, STOK))):
                        ins = dve.tensor_tensor(kr, bc(m_prev[:, c0:c0 + 8], 2, L), mr, ALU.subtract)
                        ins.then_inc(*(own.one() if n == 0 else (e_ready.sem, 1)))
                    dve.wait_ge(*e_done(2))
                    dve.tensor_tensor(rows_k[:, :], rows_l[:, :], m_rows[:, :], ALU.add).then_inc(e_ready.sem, 1)
                    split(3)
                    for t in range(NTT):
                        rows = 64 if t == 8 else P
                        dve.wait_ge(*q_turned(t + 1))
                        dve.tensor_copy(tok[0:rows, t, :, :],
                                        ps[0:rows, 6 + t % 2, 0:P].rearrange("p (q h) -> p q h", h=32)[:, :, 0:H]
                                        ).then_inc(tok_done.sem, 1)
                    dve.wait_ge(*tok_done(NTT))
                    dve.tensor_scalar(tok[:, 0:8, 1, :], tok[:, 0:8, 1, :], 1.0 / 16, None, ALU.mult).then_inc(*own.one())
                    dve.tensor_scalar(tok[0:64, 8, 1, :], tok[0:64, 8, 1, :], 1.0 / 16, None, ALU.mult).then_inc(tok_done.sem, 1)

                @block.tensor
                def _(pe):
                    pe.wait_ge(*lo_done(1))
                    wh, wl = pair_part(M, "hi", 0, 0), pair_part(M, "lo", 0, 0)
                    for n, (t0, w) in enumerate(UNITS):
                        three(pe, ps[:, n, 0:w], [(wh[:, k, :], wl[:, k, :], hhi[:, k, t0:t0 + w], hlo[:, k, t0:t0 + w])
                                                  for k in range(KT)]).then_inc(g_unit.sem, 1)
                    for p in range(4):
                        pe.wait_ge(*lo_done(2 * p + 3))
                        s = (p + 1) % 2
                        wh = M["w_hi"][s][:, :].rearrange("p (k n) -> p k n", k=KT)
                        wl = M["w_lo"][s][:, :].rearrange("p (k n) -> p k n", k=KT)
                        for t in range(NTT):
                            rows = 64 if t == 8 else P
                            if 9 * p + t >= 3:
                                pe.wait_ge(*v_kept(9 * p + t - 2))
                            a, b = (128 * t, 128 * t + 128) if t < 8 else (T - 128, T)
                            three(pe, ps[:, 3 + t % 3, 0:256],
                                  [(hhi[:, k, a:b], hlo[:, k, a:b], wh[:, k, :], wl[:, k, :]) for k in range(KT)]
                                  ).then_inc(v_unit.sem, 1)
                    pe.wait_ge(*e_done(3))
                    for t in range(NTT):
                        rows = 64 if t == 8 else P
                        if t >= 2:
                            pe.wait_ge(*tok_done(t - 1))
                        pe.transpose(ps[0:rows, 6 + t % 2, 0:P], rows_q[:, 128 * t:128 * t + rows],
                                     ident[:, :]).then_inc(q_turned.sem, 1)

        def spatial(M, free, v, mixed_d):
            ar.at = M["ring_at"]
            ln_g = ar.put("ln_g", [P, D])
            ln_b = ar.put("ln_b", [P, D])
            stage = ar.put("stage", [P, 2, KT, P])
            crow = ar.put("conv_rows", [NSEQ * 3, 2 * D])
            nrow = ar.put("n_rows", [NSEQ * H, DH])
            ar.at = free
            w_rows = ar.put("w_rows", [P, H, P])
            w_diag = ar.put("w_diag", [64, H, 64])
            w_t = ar.put("w_t", [P, H, P])
            w_dt = ar.put("w_dt", [64, H, 64])
            b_s = ar.put("b_s", [P, H, P])
            stats = ar.put("stats", [P, NTT, 2, 6])
            mv = ar.put("mv", [P, NTT, 2])
            rstd = ar.put("rstd", [P, NTT])
            names = ("ln_in", "w_in_", "diag_zero", "diag_in", "states_in", "consts", "w_turned", "w_copied", "w_masked",
                     "stats_done", "rstd_done", "scaled", "gained", "v_ready", "mix_unit", "mix_kept", "mix_out", "v_out",
                     "s_turned", "s_kept")
            (ln_in, w_in_, diag_zero, diag_in, states_in, consts, w_turned, w_copied, w_masked, stats_done, rstd_done,
             scaled, gained, v_ready, mix_unit, mix_kept, mix_out, v_out, s_turned, s_kept) = (cnt("sp_" + n) for n in names)
            mix_out = [mix_out, cnt("sp_mix_out1")]
            with nc.Block() as block:
                @block.sync
                def _(sp):
                    sp.dma_start(ln_g[:, :], I["gmlp_ln_g"].broadcast_to([P, D])).then_inc(ln_in.sem, 16)
                    sp.dma_start(ln_b[:, :], I["gmlp_ln_b"].broadcast_to([P, D])).then_inc(ln_in.sem, 16)
                    sp.dma_start(w_rows[:, :, :], I["gmlp_ws"][0].rearrange("g t s -> t g s")).then_inc(w_in_.sem, 16)
                    sp.dma_start(b_s[:, :, :], I["gmlp_bs"].broadcast_to([P, H, P])).then_inc(w_in_.sem, 16)
                    sp.dma_start(crow[:, :], I["state_conv"].rearrange("l b j c -> (l b j) c")).then_inc(states_in.sem, 16)
                    sp.dma_start(nrow[:, :], I["state_mlstm_n"].rearrange("l b h d -> (l b h) d")).then_inc(states_in.sem, 16)
                    sp.wait_ge(*diag_zero(1))
                    for b in range(NSEQ):
                        sp.dma_start(w_diag[8 * b:8 * b + 8, :, 8 * b:8 * b + 8],
                                     I["gmlp_ws"][0, :, 0:8, 0:8].rearrange("g t s -> t g s")).then_inc(diag_in.sem, 16)
                    md = mixed_d.rearrange("(f p) t -> p f t", p=P)
                    for t in range(NTT):
                        n = 64 if t == 8 else P
                        sp.wait_ge(*mix_kept(2 * t + 2))
                        sp.dma_start(md[:, :, 128 * t:128 * t + n], stage[:, t % 2, :, 0:n]).then_inc(mix_out[t % 2].sem, 16)
                    sp.wait_ge(*v_ready(NTT))
                    sp.dma_start(O["v_sample"].rearrange("l b t d -> (l b t) d"), v[0:64, 8, :]).then_inc(v_out.sem, 16)
                    sp.wait_ge(*v_out(16))
                    sp.wait_ge(*mix_out[0](80))
                    sp.wait_ge(*mix_out[1](64))

                @block.gpsimd
                def _(pool):
                    own = pool_steps
                    pool.memset(w_diag[:, :, :], 0.0).then_inc(diag_zero.sem, 1)
                    pool.memset(M["half"][:, :], -0.5).then_inc(consts.sem, 1)
                    pool.memset(M["neg_mask"][:, :], 0.0).then_inc(*own.one())
                    pool.memset(M["neg_diag"][:, :], 0.0).then_inc(*own.one())
                    pool.memset(M["seq_mask"][:, :], 1.0).then_inc(*own.one())
                    pool.wait_ge(*own.now())
                    pool.affine_select(out=M["neg_mask"][:, :], in_=M["neg_mask"][:, :], compare_op=ALU.is_ge, fill=-BIG,
                                       base=0, pattern=[[1, P]], channel_multiplier=-1).then_inc(*own.one())
                    pool.affine_select(out=M["neg_diag"][:, :], in_=M["neg_diag"][:, :], compare_op=ALU.is_ge, fill=-BIG,
                                       base=0, pattern=[[1, 64]], channel_multiplier=-1).then_inc(*own.one())
                    pool.affine_select(out=M["seq_mask"][:, :], in_=M["seq_mask"][:, :], compare_op=ALU.is_ge, fill=0.0,
                                       base=0, pattern=[[-8, NSEQ]], channel_multiplier=1).then_inc(*own.one())
                    pool.wait_ge(*own.now())
                    nd = M["neg_diag"][:, :].rearrange("s (b t) -> s b t", t=STOK)
                    pool.affine_select(out=nd, in_=nd, compare_op=ALU.is_ge, fill=-BIG, base=0,
                                       pattern=[[-8, NSEQ], [0, STOK]], channel_multiplier=1).then_inc(*own.one())
                    pool.affine_select(out=M["seq_mask"][:, :], in_=M["seq_mask"][:, :], compare_op=ALU.is_ge, fill=0.0,
                                       base=7, pattern=[[8, NSEQ]], channel_multiplier=-1).then_inc(consts.sem, 1)
                    pool.wait_ge(*w_copied(2))
                    for n, (w, L) in enumerate(((w_t, P), (w_dt, 64))):
                        pool.affine_select(out=w[:, :, :], in_=w[:, :, :], compare_op=ALU.is_ge, fill=0.0, base=0,
                                           pattern=[[0, H], [1, L]], channel_multiplier=-1).then_inc(w_masked.sem, 1)
                    pool.wait_ge(*stats_done(NTT))
                    pool.tensor_scalar(rstd[:, :], mv[:, :, 1], EPS, None, ALU.add).then_inc(*own.one())
                    pool.wait_ge(*own.now())
                    pool.tensor_tensor(rstd[:, :], rstd[:, :], M["half"][:, :], ALU.pow).then_inc(rstd_done.sem, 1)
                    pool.wait_ge(*ln_in(32))
                    for t in range(NTT):
                        rows = 64 if t == 8 else P
                        pool.wait_ge(*scaled(t + 1))
                        pool.tensor_tensor(v[0:rows, t, :], v[0:rows, t, :], ln_g[0:rows, :], ALU.mult).then_inc(gained.sem, 1)

                @block.scalar
                def _(act):
                    act.wait_ge(*s_turned(1))
                    act.activation(M["conv_in"][:, :, :, :].rearrange("p a t n -> p (a t n)"), ps[:, 6, 0:384], ACT.Copy).then_inc(s_kept.sem, 1)
                    act.wait_ge(*s_turned(2))
                    act.activation(M["n_in"][:, :, :, :].rearrange("p i b h -> p (i b h)"), ps[:, 7, 0:64], ACT.Copy).then_inc(s_kept.sem, 1)
                    act.wait_ge(*w_turned(1))
                    act.activation(w_t[:, :, :].rearrange("p g t -> p (g t)"), ps[:, 0, 0:512], ACT.Copy).then_inc(w_copied.sem, 1)
                    act.wait_ge(*w_turned(2))
                    act.activation(w_dt[:, :, :].rearrange("p g t -> p (g t)"), ps[0:64, 1, 0:256], ACT.Copy).then_inc(w_copied.sem, 1)

                @block.vector
                def _(dve):
                    own = dve_steps
                    dve.memset(mv[:, 8, :], 1.0).then_inc(*own.one())
                    dve.wait_ge(*own.now())
                    for t in range(NTT):
                        rows = 64 if t == 8 else P
                        for i in range(2):
                            dve.bn_stats(stats[0:rows, t, i, :], v[0:rows, t, 512 * i:512 * i + 512]).then_inc(*own.one())
                        dve.wait_ge(*own.now())
                        dve.bn_aggr(mv[0:rows, t, :], stats[0:rows, t, :, :].rearrange("p a b -> p (a b)")).then_inc(stats_done.sem, 1)
                    dve.wait_ge(*rstd_done(1))

                    def scale(t):
                        rows = 64 if t == 8 else P
                        dve.tensor_scalar(v[0:rows, t, :], v[0:rows, t, :], mv[0:rows, t, 0:1], rstd[0:rows, t:t + 1],
                                          ALU.subtract, ALU.mult).then_inc(scaled.sem, 1)

                    def shift(t):
                        rows = 64 if t == 8 else P
                        dve.wait_ge(*gained(t + 1))
                        dve.tensor_tensor(v[0:rows, t, :], v[0:rows, t, :], ln_b[0:rows, :], ALU.add).then_inc(v_ready.sem, 1)

                    def keep(t):
                        for hf in range(2):
                            dve.wait_ge(*mix_unit(2 * t + hf + 1))
                            if t >= 2 and hf == 0:
                                dve.wait_ge(*mix_out[t % 2](16 * (t // 2)))
                            bank = 2 + (2 * t + hf) % 6
                            if t < 8:
                                dve.tensor_tensor(stage[:, t % 2, 4 * hf:4 * hf + 4, :].rearrange("p (g f) t -> p g f t", f=2),
                                                  ps[:, bank, 0:512].rearrange("p (g f t) -> p g f t", g=2, f=2),
                                                  bc(b_s[:, 2 * hf:2 * hf + 2, :], 2, 2), ALU.add).then_inc(mix_kept.sem, 1)
                            else:
                                for g in range(2):
                                    f0 = 4 * hf + 2 * g
                                    ins = dve.tensor_tensor(
                                        stage[:, 0, f0:f0 + 2, 0:64].rearrange("p f (b t) -> p f b t", t=STOK),
                                        ps[:, bank, 128 * g:128 * g + 128].rearrange("p (f b t) -> p f b t", f=2, t=STOK),
                                        bc(bc(b_s[:, 2 * hf + g, 0:STOK], 1, NSEQ), 1, 2), ALU.add)
                                ins.then_inc(mix_kept.sem, 1)

                    scale(0)
                    scale(1)
                    for t in range(NTT):
                        if t + 2 < NTT:
                            scale(t + 2)
                        shift(t)
                        if t >= 1:
                            keep(t - 1)
                    keep(8)

                @block.tensor
                def _(pe):
                    pe.wait_ge(*states_in(32))
                    for j in range(16):
                        ins = pe.transpose(ps[:, 6, 24 * j:24 * j + 24], crow[:, 128 * j:128 * j + 128], ident[0:24, 0:24])
                    ins.then_inc(s_turned.sem, 1)
                    for i in range(2):
                        ins = pe.transpose(ps[:, 7, 32 * i:32 * i + 32], nrow[:, 128 * i:128 * i + 128], ident[0:32, 0:32])
                    ins.then_inc(s_turned.sem, 1)
                    pe.wait_ge(*w_in_(32))
                    for g in range(H):
                        ins = pe.transpose(ps[:, 0, 128 * g:128 * g + 128], w_rows[:, g, :], ident[:, :])
                    ins.then_inc(w_turned.sem, 1)
                    pe.wait_ge(*diag_in(16 * NSEQ))
                    for g in range(H):
                        ins = pe.transpose(ps[0:64, 1, 64 * g:64 * g + 64], w_diag[:, g, :], ident[0:64, 0:64])
                    ins.then_inc(w_turned.sem, 1)
                    pe.wait_ge(*w_masked(2))
                    pe.wait_ge(*s_kept(2))
                    for t in range(NTT):
                        rows = 64 if t == 8 else P
                        pe.wait_ge(*v_ready(t + 1))
                        for hf in range(2):
                            u = 2 * t + hf
                            if u >= 6:
                                pe.wait_ge(*mix_kept(u - 5))
                            w = w_t if t < 8 else w_dt
                            for f in range(4):
                                ft = 4 * hf + f
                                ins = pe.matmul(ps[:, 2 + u % 6, rows * f:rows * f + rows], v[0:rows, t, 128 * ft:128 * ft + 128],
                                                w[:, ft // 2, :], start=True, stop=True)
                            ins.then_inc(mix_unit.sem, 1)

        def heads(M, free, mixed_d):
            ar.at = free
            q = ar.put("q", [P, 2, T], at=None)
            q_at = ar.at - 2 * T * 4
            k_at = ar.at
            kk = ar.put("kk", [P, 2, T])
            mix_hi = ar.put("mix_hi", [P, 2, T], F32R, at=q_at)
            mix_lo = ar.put("mix_lo", [P, 2, T], F32R, at=k_at)
            vx = ar.put("vx", [P, NTT, DH + 1])
            ob = ar.put("ob", [P, 2, T])
            ub = ar.put("ub", [P, 2, T])
            zc_at = ar.at
            ZP, ZS = SEQ + 3, NSEQ * (STOK + 3)
            zc = ar.put("zc", [P, ZP + ZS])
            zc_end = ar.at
            ar.at = zc_at
            ex = ar.put("ex", [P, P])
            st = ar.put("s_t", [P, P])
            kw = ar.put("kw", [P, DH])
            inter = ar.put("inter", [P, DH + 1])
            ar.at = max(ar.at, zc_end)
            num = ar.put("num", [P, DH + 1])
            tmp = ar.put("gate_tmp", [P, 2, 384])
            C = ar.put("C", [P, 2, DH + 1])
            cs = ar.put("cs", [P, 2, 2, DH + 1])
            kws = ar.put("kws", [64, DH])
            inter_s = ar.put("inter_s", [64, DH + 1])
            vb = ar.put("vb", [64, DH + 1])
            otmp = ar.put("otmp", [P, 4, NSEQ, STOK])
            cw = ar.put("cw", [P, CW, 2, 2])
            cb = ar.put("cb", [P, 2, 2])
            ng = ar.put("ng", [P, 2])
            pads = ar.put("pads", [P, 2, 2, 24])
            tk = ar.put("tk", [P, NTT, 4])
            sel = ar.put("sel", [H, P])
            ap_ = ar.put("ap_", [P, 16])
            hn0 = ar.put("hn0", [P, 2, NSEQ])
            w_mask = ar.put("w_mask", [64, NSEQ])
            den = ar.put("den", [P, 2])
            hst = ar.put("hst", [P, 6])
            hmv = ar.put("hmv", [P, 2])
            var = ar.put("var", [P, 2])
            x_added = ffn_counts["x_added"]
            names = ("hi", "lo", "qk_unit", "zc_kept", "conv", "qk_ready", "vm_unit", "vm_kept", "step_unit",
                     "step_act", "step_mul", "mix_sum", "mix_hi", "mix_lo", "out_unit", "staged", "ap_mm", "ap_kept", "kT", "kw_done",
                     "s0", "e_ready", "e_done", "st_done", "inter_mm", "inter_done", "s1", "b5_read", "c_upd", "var_ready",
                     "rs_ready", "h_ready", "s2", "h_kept", "prep", "seq_mm", "seq_upd", "ub_in", "cp_out", "ones_made", "passed")
            K = {n: cnt("h_" + n) for n in names}
            w_in_ = [cnt("h_w_in0"), cnt("h_w_in1")]
            c_in = [cnt("h_c_in0"), cnt("h_c_in1")]
            c_out = [cnt("h_c_out0"), cnt("h_c_out1")]
            JOBS = [0, 1, 2, 3, "S", 4, 5, 6, 7]
            NJ = len(JOBS)
            EVENTS, unit = [], 0
            for gap in range(3 * NJ):
                EVENTS.append(("stage", gap // 3, gap % 3))
                while unit < (gap + 1) * 24 // (3 * NJ):
                    EVENTS.append(("unit", unit, None))
                    unit += 1

            def place(p):
                c = JOBS[p]
                return (False, None, SEQ, 64, 8) if c == "S" else (True, c, c * CHUNK, CHUNK, c)

            def seq_at(p, stage):
                return 2 * p + stage // 2 if p < 4 and stage != 1 else None

            def zc_out(n, w):
                t0 = UNITS[n][0]
                return zc[:, 3 + t0:3 + t0 + w]

            zs = zc[:, ZP:ZP + ZS].rearrange("p (b t) -> p b t", t=STOK + 3)

            with nc.Block() as block:
                @block.sync
                def _(sp):
                    DOWN = I["w_out"][0].rearrange("(h k p) n -> p h k n", k=2, p=P)

                    def load(h, pair):
                        dst = M["w_raw"][pair % 2]
                        sp.sem_inc(K["passed"].sem, 1)
                        if pair == 7:
                            src = DOWN[:, bass.ds(h, 1), :, :].squeeze(1)
                            sp.dma_start(dst[:, :].rearrange("p (k n) -> p k n", k=2), src).then_inc(w_in_[1].sem, 16)
                            return
                        col = (Q_COLS, K_COLS, VM_COLS, GB_COLS, O_COLS, GA_COLS, GELU_COLS)[pair]
                        sp.dma_start(dst[:, :].rearrange("p (k n) -> p k n", k=KT),
                                     w_d[:, :, bass.ds(h * 256 + col, 256)]).then_inc(w_in_[pair % 2].sem, 16)

                    def load_state(h, b):
                        src = I["state_mlstm_C"][0, b].rearrange("h (i p) e -> p h i e", p=P)[:, bass.ds(h, 1), :, :].squeeze(1)
                        sp.dma_start(cs[:, b % 2, :, 0:DH], src).then_inc(c_in[b % 2].sem, 16)

                    def body(h, last):
                        sp.wait_ge(*x_added(h * 24))
                        sp.dma_start(ub[:, :, :], mixed_d.rearrange("(h i p) t -> p h i t", i=2, p=P)[:, bass.ds(h, 1), :, :]
                                     .squeeze(1)).then_inc(K["ub_in"].sem, 16)
                        load_state(h, 0)
                        load_state(h, 1)
                        for pair in range(3):
                            sp.wait_ge(*(K["qk_unit"](h * 12 + 6 * pair + 6) if pair < 2 else K["vm_unit"](h * NTT + NTT)))
                            load(h, pair + 2)
                        for kind, a, stage in EVENTS:
                            if kind == "stage" and seq_at(a, stage) is not None:
                                b = seq_at(a, stage)
                                sp.wait_ge(*K["seq_upd"](h * 8 + b + 1))
                                dst = O["C_sample"][0, b].rearrange("h (i p) e -> p h i e", p=P)[:, bass.ds(h, 1), :, :].squeeze(1)
                                sp.dma_start(dst, cs[:, b % 2, :, 0:DH]).then_inc(c_out[b % 2].sem, 16)
                                if b + 2 < NSEQ:
                                    sp.wait_ge(*c_out[b % 2](h * 64 + 16 * (b // 2 + 1)))
                                    load_state(h, b + 2)
                            if kind == "unit" and a % 6 == 5:
                                pair = 3 + a // 6
                                sp.wait_ge(*K["step_unit"](h * 24 + a + 1))
                                if pair < 6:
                                    load(h, pair + 2)
                                elif not last:
                                    load(h + 1, 0)
                        for s in range(2):
                            sp.wait_ge(*c_out[s](h * 64 + 64))
                        sp.wait_ge(*K["c_upd"](h * 8 + 8))
                        dst = O["C_prompt"][0, 0].rearrange("h (i p) e -> p h i e", p=P)[:, bass.ds(h, 1), :, :].squeeze(1)
                        sp.dma_start(dst, C[:, :, 0:DH]).then_inc(K["cp_out"].sem, 16)
                        sp.wait_ge(*K["cp_out"](h * 16 + 16))
                        if not last:
                            sp.wait_ge(*K["out_unit"](h * 24 + 24))
                            load(h + 1, 1)

                    load(0, 0)
                    load(0, 1)
                    with sp.Fori(0, H - 1) as h:
                        body(h, False)
                    body(H - 1, True)

                @block.gpsimd
                def _(pool):
                    own = pool_steps
                    pool.memset(vx[:, :, DH:DH + 1], 1.0).then_inc(K["ones_made"].sem, 1)
                    with pool.Fori(0, H) as h:
                        own.enter(h, NJ)
                        for p in range(NJ):
                            rows = place(p)[3]
                            pool.wait_ge(*K["var_ready"](h * NJ + p + 1))
                            pool.sem_inc(K["passed"].sem, 1)
                            pool.tensor_scalar(var[0:rows, 1:2], var[0:rows, 0:1], EPS, None, ALU.add).then_inc(*own.one())
                            pool.wait_ge(*own.now())
                            pool.tensor_tensor(var[0:rows, 1:2], var[0:rows, 1:2], M["half"][0:rows, 0:1], ALU.pow
                                               ).then_inc(K["rs_ready"].sem, 1)
                        own.leave(H)

                @block.scalar
                def _(act):
                    def split(h, j):
                        pair, i = j // 2, j % 2
                        if i == 0:
                            act.wait_ge(*w_in_[pair % 2](h * 64 + 16 * (pair // 2) + 16))
                        rows = pair == 7
                        act.activation(pair_part(M, "hi", pair % 2, i, rows), pair_part(M, "raw", pair % 2, i, rows),
                                       ACT.Copy).then_inc(K["hi"].sem, 1)

                    def silu(h, j):
                        act.wait_ge(*K["conv"](h * 4 + j + 1))
                        t = (q, kk)[j // 2][:, j % 2, :]
                        act.activation(t, t, ACT.Silu).then_inc(K["qk_ready"].sem, 1)

                    def unit(h, u):
                        tile, n = divmod(u, 3)
                        t0, w = UNITS[n]
                        i = tile % 2
                        act.wait_ge(*K["step_unit"](h * 24 + u + 1))
                        if tile < 2:
                            dst = ob[:, i, t0:t0 + w]
                        else:
                            dst = tmp[:, u % 2, 0:w]
                            if u >= 8:
                                act.wait_ge(*K["step_mul"](h * 18 + u - 7))
                        f = ACT.Gelu_apprx_tanh if tile >= 6 else ACT.Sigmoid
                        act.activation(dst, ps[:, u % 3, 0:w], f).then_inc(K["step_act"].sem, 1)

                    def stage0(h, p):
                        chunk, c, t0, L, tt = place(p)
                        if chunk:
                            act.wait_ge(*K["kT"](h * NJ + c + 2))
                            if p:
                                act.wait_ge(*K["s1"](h * NJ + p))
                            act.activation(kw[:, :], ps[:, 4, 0:DH], ACT.Copy, scale=tk[:, tt, 1:2]).then_inc(K["kw_done"].sem, 1)
                        act.wait_ge(*K["e_ready"](h * NJ + p + 1))
                        act.activation(ex[0:L, 0:L], ex[0:L, 0:L], ACT.Exp, bias=tk[0:L, tt, 0:1]).then_inc(K["e_done"].sem, 1)

                    def stage1(h, p):
                        chunk, c, t0, L, tt = place(p)
                        if chunk:
                            act.wait_ge(*K["inter_mm"](h * 8 + c + 1))
                            act.activation(inter[:, :], ps[:, 4, 0:DH + 1], ACT.Copy, scale=tk[:, tt, 2:3]
                                           ).then_inc(K["inter_done"].sem, 1)

                    def stage2(h, p):
                        chunk, c, t0, L, tt = place(p)
                        act.wait_ge(*K["s2"](h * NJ + p + 1))
                        for i in range(2):
                            ins = act.activation(q[:, i, t0:t0 + L], ps[:, 4, 128 * i:128 * i + L], ACT.Copy, scale=ng[:, i:i + 1])
                        ins.then_inc(K["h_kept"].sem, 1)

                    with act.Fori(0, H) as h:
                        split(h, 0)
                        split(h, 1)
                        for j in range(4):
                            for n, (t0, w) in enumerate(UNITS):
                                act.wait_ge(*K["qk_unit"](h * 12 + 3 * j + n + 1))
                                if n == 0 and j:
                                    act.wait_ge(*K["conv"](h * 4 + j))
                                if n < 2:
                                    act.activation(zc_out(n, w), ps[:, n, 0:w], ACT.Copy).then_inc(K["zc_kept"].sem, 1)
                                else:
                                    act.activation(zc_out(n, TAIL_P), ps[:, n, 0:TAIL_P], ACT.Copy)
                                    act.activation(zs[:, :, 3:3 + STOK], ps[:, n, TAIL_P:w].rearrange("p (b t) -> p b t", t=STOK),
                                                   ACT.Copy).then_inc(K["zc_kept"].sem, 1)
                                if n == 0:
                                    split(h, j + 2)
                                if n == 1 and j:
                                    silu(h, j - 1)
                        for t in range(NTT):
                            rows, r0 = (64, 64) if t == 8 else (P, 0)
                            act.wait_ge(*K["vm_unit"](h * NTT + t + 1))
                            act.activation(vx[0:rows, t, 0:DH], ps[r0:r0 + rows, t % 3, 0:DH], ACT.Copy).then_inc(K["vm_kept"].sem, 1)
                            if t == 1:
                                silu(h, 3)
                            if t in (3, 4):
                                split(h, t + 3)
                        act.wait_ge(*K["kT"](h * NJ + 1))
                        act.activation(kws[:, :], ps[0:64, 4, 0:DH], ACT.Copy, scale=tk[0:64, 8, 1:2]).then_inc(K["kw_done"].sem, 1)
                        for kind, a, s in EVENTS:
                            if kind == "stage":
                                (stage0, stage1, stage2)[s](h, a)
                            else:
                                unit(h, a)
                                if a % 3 == 1:
                                    split(h, a // 3 + 8)
                        for n in range(3):
                            t0, w = UNITS[n]
                            for i in range(2):
                                act.wait_ge(*K["mix_sum"](h * 6 + 2 * n + i + 1))
                                act.activation(mix_hi[:, i, t0:t0 + w], ub[:, i, t0:t0 + w], ACT.Copy).then_inc(K["mix_hi"].sem, 1)

                @block.vector
                def _(dve):
                    own = dve_steps

                    def link(ins):
                        ins.then_inc(*own.one())
                        dve.wait_ge(*own.now())

                    def split(h, j):
                        pair, i = j // 2, j % 2
                        rows = pair == 7
                        dve.wait_ge(*K["hi"](h * 16 + j + 1))
                        dve.tensor_tensor(pair_part(M, "lo", pair % 2, i, rows), pair_part(M, "raw", pair % 2, i, rows),
                                          pair_part(M, "hi", pair % 2, i, rows).bitcast(F32), ALU.subtract).then_inc(K["lo"].sem, 1)

                    def stage_head(h):
                        cwv = vT[:, V_CW:V_CW + 64].rearrange("p (j a t) -> p (j a) t", j=CW, a=2)
                        dve.tensor_copy(cw[:, :, :, :].rearrange("p j a i -> p (j a) i"), cwv[:, :, bass.ds(h * 2, 2)]).then_inc(*own.one())
                        dve.tensor_copy(cb[:, :, :], vT[:, V_CB:V_CB + 16].rearrange("p (a t) -> p a t", a=2)[:, :, bass.ds(h * 2, 2)]).then_inc(*own.one())
                        dve.tensor_copy(ng[:, :], vT[:, V_NORM:V_NORM + 8][:, bass.ds(h * 2, 2)]).then_inc(*own.one())
                        dve.tensor_copy(pads[:, :, :, :], M["conv_in"][:, :, bass.ds(h * 2, 2), :]).then_inc(*own.one())
                        dve.tensor_copy(tk[:, 0:8, :], M["tok"][:, 0:8, :, bass.ds(h, 1)].squeeze(3)).then_inc(*own.one())
                        dve.tensor_copy(tk[0:64, 8, :], M["tok"][0:64, 8, :, bass.ds(h, 1)].squeeze(2)).then_inc(*own.one())
                        dve.tensor_copy(sel[:, :], ident[0:H, bass.ds(h, 1)].broadcast_to([H, P])).then_inc(*own.one())
                        dve.tensor_copy(hn0[:, :, :], M["n_in"][:, :, :, bass.ds(h, 1)].squeeze(3)).then_inc(*own.one())
                        dve.memset(C[:, :, :], 0.0).then_inc(*own.one())
                        dve.wait_ge(*own.now())
                        dve.tensor_scalar(w_mask[:, :], M["seq_mask"][:, :], tk[0:64, 8, 2:3], None, ALU.mult).then_inc(K["staged"].sem, 1)

                    def conv(h, j):
                        a, i = divmod(j, 2)
                        dst = (q, kk)[a]
                        dve.tensor_copy(zs[:, :, 0:3], pads[:, a, i, :].rearrange("p (b t) -> p b t", t=3)).then_inc(*own.one())
                        link(dve.memset(zc[:, 0:3], 0.0))
                        dve.wait_ge(*K["zc_kept"](h * 12 + 3 * j + 3))
                        ds = dst[:, i, SEQ:T].rearrange("p (b t) -> p b t", t=STOK)
                        tails = M["tails"][:, bass.ds(h * 2 + (8 * a + i), 1), :].squeeze(1)
                        dve.tensor_copy(tails[:, 0:3], zc[:, SEQ:SEQ + 3]).then_inc(*own.one())
                        dve.tensor_copy(tails[:, 3:27].rearrange("p (b t) -> p b t", t=3), zs[:, :, STOK:STOK + 3]).then_inc(*own.one())
                        for w in range(CW):
                            for out, src in ((dst[:, i, 0:SEQ], zc[:, w:w + SEQ]), (ds, zs[:, :, w:w + STOK])):
                                if w == 0:
                                    ins = dve.tensor_scalar(out, src, cw[:, 0, a, i:i + 1], cb[:, a, i:i + 1], ALU.mult, ALU.add)
                                else:
                                    ins = dve.scalar_tensor_tensor(out=out, in0=src, scalar=cw[:, w, a, i:i + 1], in1=out,
                                                                   op0=ALU.mult, op1=ALU.add)
                                if w == CW - 1 and out is ds:
                                    ins.then_inc(K["conv"].sem, 1)
                                else:
                                    ins.then_inc(*own.one())
                            if w < CW - 1:
                                dve.wait_ge(*own.now())

                    def prep(h, b):
                        dve.tensor_copy(cs[:, b % 2, :, DH:DH + 1], hn0[:, :, b:b + 1]).then_inc(*own.one())
                        dve.tensor_scalar(vb[:, :], vx[0:64, 8, :], M["seq_mask"][:, b:b + 1], None, ALU.mult).then_inc(K["prep"].sem, 1)

                    def sequence(h, b):
                        dve.wait_ge(*K["seq_mm"](h * 8 + b + 1))
                        if b == 0:
                            dve.tensor_scalar(inter_s[:, :], ps[0:64, 7, 0:DH + 1], w_mask[:, 0:1], None, ALU.mult).then_inc(*own.one())
                        else:
                            dve.scalar_tensor_tensor(out=inter_s[:, :], in0=ps[0:64, 7, 0:DH + 1], scalar=w_mask[:, b:b + 1],
                                                     in1=inter_s[:, :], op0=ALU.mult, op1=ALU.add).then_inc(*own.one())
                        s = b % 2
                        dve.scalar_tensor_tensor(out=cs[:, s, :, DH:DH + 1], in0=cs[:, s, :, DH:DH + 1], scalar=ap_[:, 8 + b:9 + b],
                                                 in1=ps[:, 3, 300:302].unsqueeze(2), op0=ALU.mult, op1=ALU.add).then_inc(*own.one())
                        dve.scalar_tensor_tensor(out=cs[:, s, :, 0:DH], in0=cs[:, s, :, 0:DH], scalar=ap_[:, 8 + b:9 + b],
                                                 in1=ps[:, 6, 0:512].rearrange("p (i e) -> p i e", i=2), op0=ALU.mult,
                                                 op1=ALU.add).then_inc(K["seq_upd"].sem, 1)
                        dve.wait_ge(*own.now())
                        dve.tensor_copy(M["n_out"][:, :, b, bass.ds(h, 1)], cs[:, s, :, DH:DH + 1]).then_inc(*own.one())
                        if b + 1 < NSEQ:
                            prep(h, b + 1)

                    def stage0(h, p):
                        chunk, c, t0, L, tt = place(p)
                        dve.wait_ge(*K["s0"](h * NJ + p + 1))
                        mask = M["neg_mask"] if chunk else M["neg_diag"]
                        dve.tensor_tensor(ex[0:L, 0:L], mask[:, :], ps[0:L, 3, 128:128 + L], ALU.subtract).then_inc(K["e_ready"].sem, 1)
                        b = seq_at(p, 0)
                        if b is not None:
                            sequence(h, b)
                        dve.wait_ge(*K["e_done"](h * NJ + p + 1))
                        dve.scalar_tensor_tensor(out=st[0:L, 0:L], in0=ps[0:L, 3, 0:L], scalar=1.0 / 16, in1=ex[0:L, 0:L],
                                                 op0=ALU.mult, op1=ALU.mult).then_inc(K["st_done"].sem, 1)

                    def stage1(h, p):
                        chunk, c, t0, L, tt = place(p)
                        dve.wait_ge(*K["s1"](h * NJ + p + 1))
                        if chunk:
                            dve.wait_ge(*K["inter_done"](h * 8 + c + 1))
                        if p:
                            dve.wait_ge(*K["s2"](h * NJ + p))
                        src = inter if chunk else inter_s
                        ins = dve.tensor_tensor(num[0:L, :], src[0:L, :], ps[0:L, 5, 0:DH + 1], ALU.add)
                        if chunk:
                            ins.then_inc(*own.one())
                            dve.scalar_tensor_tensor(out=C[:, :, DH:DH + 1], in0=C[:, :, DH:DH + 1], scalar=ap_[:, c:c + 1],
                                                     in1=ps[:, 5, 300:302].unsqueeze(2), op0=ALU.mult, op1=ALU.add
                                                     ).then_inc(K["b5_read"].sem, 1)
                            dve.scalar_tensor_tensor(out=C[:, :, 0:DH], in0=C[:, :, 0:DH], scalar=ap_[:, c:c + 1],
                                                     in1=ps[:, 6, 0:512].rearrange("p (i e) -> p i e", i=2), op0=ALU.mult,
                                                     op1=ALU.add).then_inc(K["c_upd"].sem, 1)
                            dve.wait_ge(*own.now())
                        else:
                            ins.then_inc(K["b5_read"].sem, 1)
                            dve.wait_ge(*K["b5_read"](h * NJ + p + 1))
                        dve.tensor_scalar(den[0:L, 0:1], num[0:L, DH:DH + 1], -1.0, tk[0:L, tt, 3:4], ALU.mult, ALU.max
                                          ).then_inc(*own.one())
                        link(dve.bn_stats(hst[0:L, :], num[0:L, 0:DH]))
                        link(dve.tensor_scalar(den[0:L, 0:1], den[0:L, 0:1], num[0:L, DH:DH + 1], None, ALU.max))
                        dve.reciprocal(den[0:L, 1:2], den[0:L, 0:1]).then_inc(*own.one())
                        link(dve.bn_aggr(hmv[0:L, :], hst[0:L, :]))
                        dve.tensor_scalar(var[0:L, 0:1], hmv[0:L, 1:2], den[0:L, 1:2], den[0:L, 1:2], ALU.mult, ALU.mult
                                          ).then_inc(K["var_ready"].sem, 1)
                        dve.wait_ge(*K["rs_ready"](h * NJ + p + 1))
                        link(dve.tensor_scalar(den[0:L, 0:1], var[0:L, 1:2], den[0:L, 1:2], None, ALU.mult))
                        dve.tensor_scalar(num[0:L, 0:DH], num[0:L, 0:DH], hmv[0:L, 0:1], den[0:L, 0:1], ALU.subtract, ALU.mult
                                          ).then_inc(K["h_ready"].sem, 1)

                    def stage2(h, p):
                        b = seq_at(p, 2)
                        if b is not None:
                            sequence(h, b)

                    def unit(h, u):
                        tile, n = divmod(u, 3)
                        t0, w = UNITS[n]
                        i = tile % 2
                        if tile < 2:
                            return
                        dst = (ob, ub)[tile >= 4][:, i, t0:t0 + w]
                        dve.wait_ge(*K["step_act"](h * 24 + u + 1))
                        if u == 12:
                            dve.wait_ge(*K["ub_in"](h * 16 + 16))
                        dve.tensor_tensor(dst, dst, tmp[:, u % 2, 0:w], ALU.mult).then_inc(K["step_mul"].sem, 1)

                    dve.wait_ge(*K["ones_made"](1))
                    with dve.Fori(0, H) as h:
                        own.enter(h, HEAD_STEPS)
                        split(h, 0)
                        split(h, 1)
                        stage_head(h)
                        for j in range(4):
                            split(h, j + 2)
                            conv(h, j)
                        dve.wait_ge(*K["vm_kept"](h * NTT + 4))
                        split(h, 6)
                        split(h, 7)
                        dve.wait_ge(*K["ap_mm"](h + 1))
                        dve.tensor_copy(ap_[:, :], ps[:, 3, 0:16]).then_inc(K["ap_kept"].sem, 1)
                        dve.wait_ge(*K["ap_kept"](h + 1))
                        dve.wait_ge(*K["vm_kept"](h * NTT + NTT))
                        prep(h, 0)
                        for kind, a, s in EVENTS:
                            if kind == "stage":
                                (stage0, stage1, stage2)[s](h, a)
                            else:
                                unit(h, a)
                                if a % 3 == 1:
                                    split(h, a // 3 + 8)
                        dve.wait_ge(*K["h_kept"](h * NJ + NJ))
                        dve.tensor_copy(M["np_out"][:, :, bass.ds(h, 1)], C[:, :, DH:DH + 1]).then_inc(*own.one())

                        def low(j):
                            n, i = divmod(j, 2)
                            t0, w = UNITS[n]
                            dve.wait_ge(*K["mix_hi"](h * 6 + j + 1))
                            dve.tensor_tensor(mix_lo[:, i, t0:t0 + w], ub[:, i, t0:t0 + w], mix_hi[:, i, t0:t0 + w].bitcast(F32),
                                              ALU.subtract).then_inc(K["mix_lo"].sem, 1)

                        for j in range(6):
                            n, i = divmod(j, 2)
                            t0, w = UNITS[n]
                            dve.wait_ge(*K["step_mul"](h * 18 + 18))
                            link(dve.tensor_tensor(ob[:, i, t0:t0 + w], ob[:, i, t0:t0 + w], q[:, i, t0:t0 + w], ALU.mult))
                            dve.tensor_tensor(ub[:, i, t0:t0 + w], ub[:, i, t0:t0 + w], ob[:, i, t0:t0 + w], ALU.add
                                              ).then_inc(K["mix_sum"].sem, 1)
                            if j:
                                low(j - 1)
                        low(5)
                        for u, (m, n) in enumerate(OUT_ORDER):
                            dve.wait_ge(*K["out_unit"](h * 24 + u + 1))
                            add_out(dve, own, m, n, u % 6, otmp[:, m % 4, :, :], x_added)
                        dve.wait_ge(*K["cp_out"](h * 16 + 16))
                        own.leave(H)

                @block.tensor
                def _(pe):
                    def operands(pair, i, t0, w):
                        wh, wl = (pair_part(M, kd, pair % 2, i) for kd in ("hi", "lo"))
                        return [(wh[:, k, :], wl[:, k, :], hhi[:, k, t0:t0 + w], hlo[:, k, t0:t0 + w]) for k in range(KT)]

                    def sequence(h, p, stage):
                        b = seq_at(p, stage)
                        if b is None:
                            return
                        s = b % 2
                        if stage == 2:
                            pe.wait_ge(*K["st_done"](h * NJ + p + 1))
                            pe.wait_ge(*K["seq_upd"](h * 8 + b))
                            state_n(h, b)
                        pe.wait_ge(*c_in[s](h * 64 + 16 * (b // 2 + 1)))
                        if b:
                            pe.wait_ge(*K["seq_upd"](h * 8 + b))
                        if stage == 0 and p:
                            pe.wait_ge(*K["c_upd"](h * 8 + p))
                        if stage == 2:
                            pe.wait_ge(*K["c_upd"](h * 8 + p + 1))
                        for i in range(2):
                            pe.matmul(ps[0:64, 7, 0:DH + 1], q[:, i, SEQ:T], cs[:, s, i, :], start=(i == 0), stop=(i == 1))
                        for i in range(2):
                            ins = pe.matmul(ps[:, 6, 256 * i:256 * i + 256], kws[:, 128 * i:128 * i + 128], vb[:, 0:DH],
                                            start=True, stop=True)
                        ins.then_inc(K["seq_mm"].sem, 1)

                    def state_n(h, b):
                        pe.wait_ge(*K["prep"](h * 8 + b + 1))
                        pe.wait_ge(*K["kw_done"](h * NJ + 1))
                        for i in range(2):
                            ins = pe.matmul(ps[:, 3, 300 + i:301 + i], kws[:, 128 * i:128 * i + 128], vb[:, DH:DH + 1],
                                            start=True, stop=True)
                        return ins

                    def stage0(h, p):
                        chunk, c, t0, L, tt = place(p)
                        if chunk:
                            if p:
                                pe.wait_ge(*K["h_kept"](h * NJ + p))
                            else:
                                pe.wait_ge(*K["kw_done"](h * NJ + 1))
                            for i in range(2):
                                ins = pe.transpose(ps[:, 4, 128 * i:128 * i + 128], kk[:, i, t0:t0 + L], ident[:, :])
                            ins.then_inc(K["kT"].sem, 1)
                        if p:
                            pe.wait_ge(*K["st_done"](h * NJ + p))
                            if p <= 4:
                                pe.wait_ge(*K["seq_upd"](h * 8 + 2 * p))
                        else:
                            pe.wait_ge(*K["ap_kept"](h + 1))
                        if not chunk:
                            pe.sem_inc(K["passed"].sem, 1)
                        for i in range(2):
                            pe.matmul(ps[0:L, 3, 0:L], kk[:, i, t0:t0 + L], q[:, i, t0:t0 + L], start=(i == 0), stop=(i == 1))
                        ins = pe.matmul(ps[0:L, 3, 128:128 + L], sel[:, 0:L], M["m_rows"][:, t0:t0 + L], start=True, stop=True)
                        if seq_at(p, 0) is not None:
                            ins = state_n(h, seq_at(p, 0))
                        ins.then_inc(K["s0"].sem, 1)
                        sequence(h, p, 0)

                    def stage1(h, p):
                        chunk, c, t0, L, tt = place(p)
                        if chunk:
                            pe.wait_ge(*K["kw_done"](h * NJ + c + 2))
                            if c:
                                pe.wait_ge(*K["c_upd"](h * 8 + c))
                            for i in range(2):
                                ins = pe.matmul(ps[:, 4, 0:DH + 1], q[:, i, t0:t0 + L], C[:, i, :], start=(i == 0), stop=(i == 1))
                            ins.then_inc(K["inter_mm"].sem, 1)
                        pe.wait_ge(*K["st_done"](h * NJ + p + 1))
                        if p:
                            pe.wait_ge(*K["b5_read"](h * NJ + p))
                        if not chunk:
                            pe.sem_inc(K["passed"].sem, 1)
                        ins = pe.matmul(ps[0:L, 5, 0:DH + 1], st[0:L, 0:L], vx[0:L, tt, :], start=True, stop=True)
                        if chunk:
                            for i in range(2):
                                pe.matmul(ps[:, 5, 300 + i:301 + i], kw[:, 128 * i:128 * i + 128], vx[:, tt, DH:DH + 1],
                                          start=True, stop=True)
                            if p < 4:
                                pe.wait_ge(*K["seq_upd"](h * 8 + 2 * p + 1))
                            for i in range(2):
                                ins = pe.matmul(ps[:, 6, 256 * i:256 * i + 256], kw[:, 128 * i:128 * i + 128], vx[:, tt, 0:DH],
                                                start=True, stop=True)
                        ins.then_inc(K["s1"].sem, 1)

                    def stage2(h, p):
                        chunk, c, t0, L, tt = place(p)
                        pe.wait_ge(*K["h_ready"](h * NJ + p + 1))
                        if chunk:
                            pe.wait_ge(*K["inter_done"](h * 8 + c + 1))
                        else:
                            pe.wait_ge(*K["h_kept"](h * NJ + p))
                        if not chunk:
                            pe.sem_inc(K["passed"].sem, 1)
                        for i in range(2):
                            ins = pe.transpose(ps[:, 4, 128 * i:128 * i + L], num[0:L, 128 * i:128 * i + 128], ident[0:L, 0:L])
                        ins.then_inc(K["s2"].sem, 1)
                        sequence(h, p, 2)

                    def unit(h, u):
                        tile, n = divmod(u, 3)
                        t0, w = UNITS[n]
                        if n == 0:
                            pe.wait_ge(*K["lo"](h * 16 + 6 + tile + 1))
                        if u < 3:
                            pe.wait_ge(*K["vm_kept"](h * NTT + 6 + u + 1))
                        else:
                            pe.wait_ge(*K["step_act"](h * 24 + u - 2))
                        ins = three(pe, ps[:, n, 0:w], operands(3 + tile // 2, tile % 2, t0, w))
                        ins.then_inc(K["step_unit"].sem, 1)

                    with pe.Fori(0, H) as h:
                        pe.wait_ge(*x_added(h * 24))
                        for j in range(4):
                            pe.wait_ge(*K["lo"](h * 16 + j + 1))
                            for n, (t0, w) in enumerate(UNITS):
                                if j:
                                    pe.wait_ge(*K["zc_kept"](h * 12 + 3 * (j - 1) + n + 1))
                                three(pe, ps[:, n, 0:w], operands(j // 2, j % 2, t0, w)).then_inc(K["qk_unit"].sem, 1)
                        pe.wait_ge(*K["lo"](h * 16 + 6))
                        wh, wl = (M["w_" + kd][0][:, :].rearrange("p (k n) -> p k n", k=KT) for kd in ("hi", "lo"))
                        for t in range(NTT):
                            if t < 3:
                                pe.wait_ge(*K["zc_kept"](h * 12 + 9 + t + 1))
                            else:
                                pe.wait_ge(*K["vm_kept"](h * NTT + t - 2))
                            a = 128 * t if t < 8 else T - P
                            three(pe, ps[:, t % 3, 0:DH], [(hhi[:, k, a:a + P], hlo[:, k, a:a + P], wh[:, k, :], wl[:, k, :])
                                                           for k in range(KT)]).then_inc(K["vm_unit"].sem, 1)
                        pe.wait_ge(*K["staged"](h + 1))
                        pe.matmul(ps[:, 3, 0:16], sel[:, :], M["a_prev"][:, :], start=True, stop=True).then_inc(K["ap_mm"].sem, 1)
                        pe.wait_ge(*K["qk_ready"](h * 4 + 4))
                        pe.sem_inc(K["passed"].sem, 1)
                        for i in range(2):
                            ins = pe.transpose(ps[0:64, 4, 128 * i:128 * i + 128], kk[:, i, SEQ:T], ident[:, :])
                        ins.then_inc(K["kT"].sem, 1)
                        pe.wait_ge(*K["vm_kept"](h * NTT + NTT))
                        for kind, a, s in EVENTS:
                            if kind == "stage":
                                (stage0, stage1, stage2)[s](h, a)
                            else:
                                unit(h, a)
                        pe.wait_ge(*K["lo"](h * 16 + 16))
                        for u, (m, n) in enumerate(OUT_ORDER):
                            t0, w = UNITS[n]
                            if u < 3:
                                pe.wait_ge(*K["step_act"](h * 24 + 21 + u + 1))
                            elif u >= 6:
                                pe.wait_ge(*x_added(h * 24 + (u - 5)))
                            if m == 0:
                                pe.wait_ge(*K["mix_lo"](h * 6 + 2 * n + 2))
                            ms = slice(128 * m, 128 * m + 128)
                            three(pe, ps[:, u % 6, 0:w], [(pair_part(M, "hi", 1, i, True)[:, ms], pair_part(M, "lo", 1, i, True)[:, ms],
                                                           mix_hi[:, i, t0:t0 + w], mix_lo[:, i, t0:t0 + w]) for i in range(2)]
                                  ).then_inc(K["out_unit"].sem, 1)
            x_added.base += 24 * H

        def states_out(M, free):
            ar.at = free
            crow = ar.put("conv_rows_out", [27, 2 * D])
            nrow = ar.put("n_rows_out", [NSEQ * H, DH])
            nprow = ar.put("np_rows_out", [H, DH])
            turned, kept, out = cnt("so_turned"), cnt("so_kept"), cnt("so_out")
            with nc.Block() as block:
                @block.tensor
                def _(pe):
                    for j in range(16):
                        ins = pe.transpose(ps[0:27, j // 4, 128 * (j % 4):128 * (j % 4) + 128], M["tails"][:, j, :], ident[:, :])
                    ins.then_inc(turned.sem, 1)
                    for i in range(2):
                        pe.transpose(ps[0:32, 4, 128 * i:128 * i + 128], M["n_out"][:, i, :, :].rearrange("p b h -> p (b h)"), ident[:, :])
                        ins = pe.transpose(ps[0:H, 5, 128 * i:128 * i + 128], M["np_out"][:, i, :], ident[:, :])
                    ins.then_inc(turned.sem, 1)

                @block.vector
                def _(dve):
                    dve.wait_ge(*turned(1))
                    for j in range(4):
                        dve.tensor_copy(crow[:, 512 * j:512 * j + 512], ps[0:27, j, :]).then_inc(kept.sem, 1)
                    dve.wait_ge(*turned(2))
                    dve.tensor_copy(nrow[:, :], ps[0:32, 4, 0:DH]).then_inc(kept.sem, 1)
                    dve.tensor_copy(nprow[:, :], ps[0:H, 5, 0:DH]).then_inc(kept.sem, 1)

                @block.sync
                def _(sp):
                    sp.wait_ge(*kept(6))
                    sp.dma_start(O["conv_prompt"][0, 0], crow[0:3, :]).then_inc(out.sem, 16)
                    sp.dma_start(O["conv_sample"].rearrange("l b j c -> (l b j) c"), crow[3:27, :]).then_inc(out.sem, 16)
                    sp.dma_start(O["n_sample"].rearrange("l b h d -> (l b h) d"), nrow[:, :]).then_inc(out.sem, 16)
                    sp.dma_start(O["n_prompt"].rearrange("l b h d -> (l b h) d"), nprow[:, :]).then_inc(out.sem, 16)
                    sp.wait_ge(*out(64))

        def store_y(y):
            ar.at = work
            row = ar.put("y_row", [P, 2, D])
            turned, kept, out = cnt("y_turned"), [cnt("y_kept_v"), cnt("y_kept_a")], [cnt("y_out0"), cnt("y_out1")]
            with nc.Block() as block:
                @block.tensor
                def _(pe):
                    for t in range(NTT):
                        n = 64 if t == 8 else P
                        for hf in range(2):
                            u = 2 * t + hf
                            if t >= 4:
                                pe.wait_ge(*kept[hf](t - 3))
                            for f in range(4):
                                ins = pe.transpose(ps[0:n, u % 8, 128 * f:128 * f + 128], y[:, 4 * hf + f, 128 * t:128 * t + n], ident[:, :])
                            ins.then_inc(turned.sem, 1)

                @block.vector
                def _(dve):
                    for t in range(NTT):
                        n = 64 if t == 8 else P
                        dve.wait_ge(*turned(2 * t + 1))
                        if t >= 2:
                            dve.wait_ge(*out[t % 2](16 * (t // 2)))
                        dve.tensor_copy(row[0:n, t % 2, 0:512], ps[0:n, (2 * t) % 8, :]).then_inc(kept[0].sem, 1)

                @block.scalar
                def _(act):
                    for t in range(NTT):
                        n = 64 if t == 8 else P
                        act.wait_ge(*turned(2 * t + 2))
                        if t >= 2:
                            act.wait_ge(*out[t % 2](16 * (t // 2)))
                        act.activation(row[0:n, t % 2, 512:1024], ps[0:n, (2 * t + 1) % 8, :], ACT.Copy).then_inc(kept[1].sem, 1)

                @block.sync
                def _(sp):
                    for t in range(NTT):
                        n = 64 if t == 8 else P
                        sp.wait_ge(*kept[0](t + 1))
                        sp.wait_ge(*kept[1](t + 1))
                        dst = O["y_prompt"][0, 128 * t:128 * t + P, :] if t < 8 else O["y_sample"].rearrange("b t d -> (b t) d")
                        sp.dma_start(dst, row[0:n, t % 2, :]).then_inc(out[t % 2].sem, 16)
                    sp.wait_ge(*out[0](80))
                    sp.wait_ge(*out[1](64))

        csT, bT = bring_in()
        ada_vectors(csT, bT)
        if stop == 1:
            return dump(nc, ctx, dbg, xT, T * KT)
        norm(V_FFN1, 0, 8)
        residual_gates(16, 0.5)
        ffn(I["w_ffn1_in"][0], I["w_ffn1_out"][0])
        if stop == 2:
            return dump(nc, ctx, dbg, xT, T * KT)
        norm(V_MIX, 24, 32)
        residual_gates(40, 1.0)
        M, after = mixer_memory()
        ar.at = after
        v = ar.put("v", [P, NTT, D])
        mixed_d = nc.dram_tensor("mixed", [D, T], F32, kind="Internal").ap()
        gates_and_v(M, ar.at, v)
        spatial(M, after + NTT * D * 4, v, mixed_d)
        heads(M, after, mixed_d)
        states_out(M, after)
        if stop == 3:
            return dump(nc, ctx, dbg, xT, T * KT)
        norm(V_FFN2, 48, 56)
        residual_gates(64, 0.5)
        ffn(I["w_ffn2_in"][0], I["w_ffn2_out"][0])
        store_y(norm(V_FINAL, ADA_T, ADA_T + KT, final=True))


def dump(nc, ctx, dbg, t, n):
    s = ctx.enter_context(nc.semaphore("dumped"))
    with nc.Block() as block:
        @block.sync
        def _(sp):
            sp.dma_start(dbg, t[:, :, :]).then_inc(s, 16)
            sp.wait_ge(s, 16)


_INS = ['x_prompt', 'x_sample', 'c_prompt', 'c_sample', 'state_mlstm_C', 'state_mlstm_n', 'state_mlstm_m', 'state_conv',
        'w_ada', 'b_ada', 'g_ffn1', 'w_ffn1_in', 'w_ffn1_out', 'g_mix', 'w_in', 'b_gates', 'conv_w', 'conv_b',
        'gmlp_ln_g', 'gmlp_ln_b', 'gmlp_ws', 'gmlp_bs', 'mlstm_norm_g', 'w_out', 'g_ffn2', 'w_ffn2_in', 'w_ffn2_out',
        'w_ada_final', 'b_ada_final', 'g_final']
_OUTS = [("y_prompt", (1, SEQ, D)), ("y_sample", (NSEQ, STOK, D)), ("C_prompt", (1, 1, H, DH, DH)), ("n_prompt", (1, 1, H, DH)),
         ("m_prompt", (1, 1, H)), ("conv_prompt", (1, 1, CW - 1, 2 * D)), ("C_sample", (1, NSEQ, H, DH, DH)),
         ("n_sample", (1, NSEQ, H, DH)), ("m_sample", (1, NSEQ, H)), ("conv_sample", (1, NSEQ, CW - 1, 2 * D)),
         ("v_sample", (1, NSEQ, STOK, D))]
STOP = 0
DBG = (P, KT, T)


def kernel(**inputs):
    import numpy as _np
    import concourse.bacc as _bacc
    from concourse.bass_utils import run_bass_kernel_spmd as _run

    nc = _bacc.Bacc("TRN2", target_bir_lowering=False, num_devices=1, dynamic_dma_scratch_size=4096)
    arrays = {f"in_{n}": _np.ascontiguousarray(inputs[n]) for n in _INS}
    ins = {n: nc.dram_tensor(f"in_{n}", arrays[f"in_{n}"].shape, F32, kind="ExternalInput").ap() for n in _INS}
    dbg = None
    if STOP:
        dbg = nc.dram_tensor("dbg", DBG, F32, kind="ExternalOutput").ap()
        outs = {}
    else:
        outs = {n: nc.dram_tensor(f"out_{n}", s, F32, kind="ExternalOutput").ap() for n, s in _OUTS}
    layer(nc, dbg, STOP, ins, outs)
    r = _run(nc, [arrays], core_ids=[0])
    if STOP:
        return r.results[0]["dbg"]
    return tuple(r.results[0][f"out_{n}"] for n, _ in _OUTS)
```

```python
from contextlib import ExitStack

import concourse.bass as bass
from concourse import mybir

F32 = mybir.dt.float32
F32R = mybir.dt.float32r
ALU = mybir.AluOpType
ACT = mybir.ActivationFunctionType

P = 128
D = 1024
KT = D // P
SEQ = 1024
NSEQ = 8
STOK = 8
T = SEQ + NSEQ * STOK
UNITS = [(0, 384), (384, 384), (768, T - 768)]
TAIL_P = SEQ - 768
DFF = 2816
FB = DFF // 256
H = 4
DH = 256
CW = 4
CHUNK = 128
NCH = SEQ // CHUNK
NTT = NCH + 1
ADA_T = 9 * KT
ALL_T = ADA_T + 2 * KT
EPS = 1e-6
HEAD_STEPS = 170
BIG = 1.0e30
GELU_COLS, V_COLS, Q_COLS, K_COLS, VM_COLS, O_COLS, GATE_COLS = 0, 1024, 2048, 3072, 4096, 5120, 6144
GA_COLS, GB_COLS = 6152, 7176


class Count:

    def __init__(self, ctx, nc, name):
        self.sem = ctx.enter_context(nc.semaphore(name))
        self.base = 0

    def __call__(self, n):
        return self.sem, n + self.base


class Steps:

    def __init__(self, ctx, nc, name):
        self.sem = ctx.enter_context(nc.semaphore(name))
        self.n = 0
        self.turn = None

    def one(self):
        self.n += 1
        return self.sem, 1

    def now(self):
        if self.turn is None:
            return self.sem, self.n
        return self.sem, self.turn * self.stride + self.n

    def enter(self, turn, stride, first=0):
        self.turn, self.stride, self.start, self.first = turn, stride, self.n, first
        self.n -= first * stride

    def leave(self, turns):
        n = self.n + self.first * self.stride
        assert n - self.start == self.stride, (n - self.start, self.stride)
        self.n = self.start + self.stride * turns
        self.turn = None


class Arena:

    def __init__(self, nc):
        self.nc, self.at, self.end = nc, -(-nc.sbuf_base // 32) * 32, nc.sbuf_usable_end
        self.fence = None

    def put(self, name, shape, dtype=F32, at=None):
        size = 4
        for s in shape[1:]:
            size *= s
        size = -(-size // 32) * 32
        offset = self.at if at is None else at
        if at is None:
            self.at += size
        assert offset + size <= self.end, (name, offset + size - self.end)
        t = self.nc.alloc_sbuf_tensor_at(name, shape, dtype, offset=offset)
        return t


def bc(ap, axis, n):
    a = ap.unsqueeze(axis)
    shape = list(a.shape)
    shape[axis] = n
    return a.broadcast_to(shape)


def layer(nc, dbg, stop, I, O):
    with ExitStack() as ctx:
        ar = Arena(nc)

        def cnt(name):
            return Count(ctx, nc, name)

        ps = ctx.enter_context(nc.psum_tensor("ps", [P, 8, 512], F32))

        xT = ar.put("xT", [P, KT, T])
        hi_at = ar.at
        hhi = ar.put("hhi", [P, KT, T], F32R)
        hlo = ar.put("hlo", [P, KT, T], F32R)
        ada = ar.put("ada", [P, ALL_T, 9])
        ident = ar.put("ident", [P, P])
        mean = ar.put("mean", [P, P])
        eps_col = ar.put("eps_col", [P, 1])
        vT = ar.put("vT", [P, 120])
        gp = ar.put("gp", [P, KT])
        gs = ar.put("gs", [P, KT, NSEQ])
        gate_p = ar.put("gate_p", [P, KT])
        gate_s = ar.put("gate_s", [P, KT, NSEQ])
        V_FFN1, V_MIX, V_FFN2, V_FINAL, V_NORM, V_CB, V_CW = 0, 8, 16, 24, 32, 40, 56
        cs_r = ar.put("cs_r", [P, KT, 18], F32R)
        bT = ar.put("bT", [P, ALL_T])
        work = ar.at
        y_out = ar.put("y", [P, KT, T], at=hi_at)
        RINGS = 4
        ar.at = top = ar.end // 32 * 32 - 4 * (RINGS * 384 + T + KT * NSEQ * STOK) - 3 * 8192
        ring = ar.put("norm_ring", [P, RINGS, 384])
        rr = ar.put("rr", [P, T])
        ts = ar.put("norm_samples", [P, KT, NSEQ, STOK])
        ada_raw = [ar.put("ada_raw0", [P, KT, 256])] + [
            ar.put(f"ada_raw{s}", [P, KT, 256], at=hi_at + 8192 * (s - 1)) for s in range(1, 4)]
        ada_hi = [ar.put("ada_hi0", [P, KT, 256], F32R), ar.put("ada_hi1", [P, KT, 256], F32R, at=hi_at + 3 * 8192)]
        ada_lo = [ar.put("ada_lo0", [P, KT, 256], F32R), ar.put("ada_lo1", [P, KT, 256], F32R, at=hi_at + 4 * 8192)]
        ada_in = [cnt(f"ada_in{s}") for s in range(4)]
        ada_hi_done, ada_lo_done, ada_mm, ada_kept = (cnt("ada_" + n) for n in ("hi_done", "lo_done", "mm", "kept"))
        squared, squares_added, mean_done, rms_done, t_done, hi_done, lo_done = (
            cnt("norm_" + n) for n in ("squared", "squares_added", "mean_done", "rms_done", "t_done", "hi_done", "lo_done"))
        dve_steps, act_steps, pool_steps = (Steps(ctx, nc, n) for n in ("dve_steps", "act_steps", "pool_steps"))

        class Squares:

            def __init__(self, order):
                self.order, self.add_of, self.before, last = order, [], [], {}
                for k, n in order:
                    if k == 0:
                        self.add_of.append(None)
                        self.before.append(None)
                    else:
                        self.before.append(last.get(n))
                        last[n] = sum(a is not None for a in self.add_of)
                        self.add_of.append(last[n])

            def square(self, act, s):
                k, n = self.order[s]
                t0, w = UNITS[n]
                if k == 0:
                    dst = rr[:, t0:t0 + w]
                else:
                    r = self.add_of[s]
                    if r >= RINGS:
                        act.wait_ge(*squares_added(r - RINGS + 1))
                    dst = ring[:, r % RINGS, 0:w]
                act.activation(dst, xT[:, k, t0:t0 + w], ACT.Square).then_inc(squared.sem, 1)

            def add(self, eng, s):
                k, n = self.order[s]
                if k == 0:
                    return
                t0, w = UNITS[n]
                eng.wait_ge(*squared(s + 1))
                if self.before[s] is not None:
                    eng.wait_ge(*squares_added(self.before[s] + 1))
                eng.tensor_tensor(rr[:, t0:t0 + w], rr[:, t0:t0 + w], ring[:, self.add_of[s] % RINGS, 0:w],
                                  ALU.add).then_inc(squares_added.sem, 1)

            def close(self):
                squared.base += 3 * KT
                squares_added.base += 3 * (KT - 1)

        wa_d = I["w_ada"][0].rearrange("(k p) n -> p k n", p=P)
        wf_d = I["w_ada_final"].rearrange("(k p) n -> p k n", p=P)

        def ada_load(sp, g, slot=0):
            if isinstance(g, int) and g >= ADA_T // 2:
                src = wf_d[:, :, 256 * g - P * ADA_T:256 * g - P * ADA_T + 256]
            else:
                src = wa_d[:, :, bass.ds(g * 256, 256)]
            sp.dma_start(ada_raw[slot][:, :, :], src).then_inc(ada_in[slot].sem, 16)

        def ada_high(act, turn, halves_free, slot=0, half=0):
            act.wait_ge(*ada_in[slot](turn * 16 + 16))
            if halves_free is not None:
                act.wait_ge(*ada_mm(halves_free))
            for i in range(2):
                act.activation(ada_hi[half][:, :, 128 * i:128 * i + 128], ada_raw[slot][:, :, 128 * i:128 * i + 128],
                               ACT.Copy).then_inc(ada_hi_done.sem, 1)

        def ada_low(dve, g, slot=0, half=0):
            for i in range(2):
                c = slice(128 * i, 128 * i + 128)
                dve.wait_ge(*ada_hi_done(g * 2 + (i + 1)))
                dve.tensor_tensor(ada_lo[half][:, :, c], ada_raw[slot][:, :, c], ada_hi[half][:, :, c].bitcast(F32),
                                  ALU.subtract).then_inc(ada_lo_done.sem, 1)

        def ada_product(pe, g, bank, half=0, reused=True):
            pe.wait_ge(*ada_lo_done(g * 2 + 2))
            if reused:
                pe.wait_ge(*ada_kept(g - 1))
            for i in range(2):
                out = ps[:, bank, 18 * i:18 * i + 18]
                for k in range(KT):
                    pe.matmul(out, ada_hi[half][:, k, 128 * i:128 * i + 128], cs_r[:, k, :], start=(k == 0), stop=False)
                    ins = pe.matmul(out, ada_lo[half][:, k, 128 * i:128 * i + 128], cs_r[:, k, :], start=False,
                                    stop=(k == KT - 1))
            ins.then_inc(ada_mm.sem, 1)

        def ada_keep(dve, g, bank):
            dve.wait_ge(*ada_mm(g + 1))
            dst = ada[:, bass.ds(g * 2, 2), :]
            out = ps[:, bank, 0:36].rearrange("p (j s) -> p j s", s=18)
            dve.tensor_tensor(dst, out[:, :, 0:9], bc(bT[:, bass.ds(g * 2, 2)], 2, 9), ALU.add).then_inc(*dve_steps.one())
            dve.wait_ge(*dve_steps.now())
            dve.tensor_tensor(dst, dst, out[:, :, 9:18], ALU.add).then_inc(ada_kept.sem, 1)

        def bring_in():
            ar.at = work
            xtok = ar.put("xtok", [P, NTT, D])
            crow = ar.put("crow", [9, D])
            crow2 = ar.put("crow2", [9, D])
            csT = ar.put("csT", [P, KT, 9])
            brow = ar.put("brow", [ALL_T, P])
            vrow = ar.put("vrow", [120, P])
            assert ar.at <= top
            x_in = [cnt(f"x_in{u}") for u in range(3)]
            c_in, small_in, made, x_turned, x_kept, c_silu, v_turned, v_kept, cs_ready = (
                cnt(n) for n in ("c_in", "small_in", "made", "x_turned", "x_kept", "c_silu", "v_turned", "v_kept", "cs_ready"))
            x_kept_a = cnt("x_kept_a")
            sq = Squares([(k, u) for u in range(3) for k in range(KT)])
            with nc.Block() as block:
                @block.sync
                def _(sp):
                    for u in range(3):
                        for tt in range(3 * u, 3 * u + (3 if u < 2 else 2)):
                            sp.dma_start(xtok[:, tt, :], I["x_prompt"][0, 128 * tt:128 * tt + 128, :]).then_inc(x_in[u].sem, 16)
                        if u == 2:
                            sp.dma_start(xtok[0:64, 8, :], I["x_sample"].rearrange("b t d -> (b t) d")).then_inc(x_in[2].sem, 16)
                        for g in range(4 * u, 4 * u + 4):
                            if g >= 4:
                                sp.wait_ge(*ada_lo_done(2 * (g - 4) + 2))
                            ada_load(sp, g, g % 4)

                @block.scalar
                def _(act):
                    act.dma_start(crow[0:1, :], I["c_prompt"]).then_inc(c_in.sem, 16)
                    act.dma_start(crow[1:9, :], I["c_sample"]).then_inc(c_in.sem, 16)
                    act.dma_start(brow[0:ADA_T, :], I["b_ada"].rearrange("l (t p) -> (l t) p", p=P)).then_inc(small_in.sem, 16)
                    act.dma_start(brow[ADA_T:ALL_T, :], I["b_ada_final"].rearrange("(t p) -> t p", p=P)).then_inc(small_in.sem, 16)
                    for at, n, src in ((V_FFN1, 8, I["g_ffn1"].rearrange("l (t p) -> (l t) p", p=P)),
                                       (V_MIX, 8, I["g_mix"].rearrange("l (t p) -> (l t) p", p=P)),
                                       (V_FFN2, 8, I["g_ffn2"].rearrange("l (t p) -> (l t) p", p=P)),
                                       (V_FINAL, 8, I["g_final"].rearrange("(t p) -> t p", p=P)),
                                       (V_NORM, 8, I["mlstm_norm_g"].rearrange("l (t p) -> (l t) p", p=P)),
                                       (V_CB, 16, I["conv_b"].rearrange("l (t p) -> (l t) p", p=P)),
                                       (V_CW, 64, I["conv_w"].rearrange("l j (t p) -> (l j t) p", p=P))):
                        act.dma_start(vrow[at:at + n, :], src).then_inc(small_in.sem, 16)
                    act.wait_ge(*c_in(32))
                    act.activation(crow2[:, :], crow[:, :], ACT.Silu).then_inc(c_silu.sem, 1)
                    act.wait_ge(*v_turned(1))
                    act.activation(csT[:, :, :], ps[:, 6, 0:72], ACT.Copy).then_inc(v_kept.sem, 1)
                    act.wait_ge(*v_kept(1))
                    act.activation(cs_r[:, :, 0:9], csT[:, :, :], ACT.Copy).then_inc(v_kept.sem, 1)
                    act.wait_ge(*v_turned(2))
                    act.activation(bT[:, :], ps[:, 7, 0:ALL_T], ACT.Copy).then_inc(v_kept.sem, 1)
                    act.activation(vT[:, :], ps[:, 7, 128:248], ACT.Copy).then_inc(v_kept.sem, 1)
                    for u, (t0, n) in enumerate(UNITS):
                        for k in range(1, KT, 2):
                            g = KT * u + k
                            act.wait_ge(*x_turned(g + 1))
                            act.activation(xT[:, k, t0:t0 + n], ps[:, g % 6, 0:n], ACT.Copy).then_inc(x_kept_a.sem, 1)
                        for k in range(KT):
                            if k % 2 == 0:
                                act.wait_ge(*x_kept(4 * u + k // 2 + 1))
                            else:
                                act.wait_ge(*x_kept_a(4 * u + k // 2 + 1))
                            sq.square(act, KT * u + k)
                            if k % 2 == 1:
                                g = 4 * u + k // 2
                                ada_high(act, g // 4, g - 1 if g >= 2 else None, g % 4, g % 2)

                @block.gpsimd
                def _(pool):
                    pool.memset(ident[:, :], 0.0).then_inc(made.sem, 1)
                    pool.memset(mean[:, :], 1.0 / D).then_inc(made.sem, 1)
                    pool.memset(eps_col[:, :], EPS).then_inc(made.sem, 1)
                    pool.wait_ge(*made(3))
                    pool.affine_select(out=ident[:, :], in_=ident[:, :], compare_op=ALU.not_equal, fill=1.0,
                                       base=0, pattern=[[-1, P]], channel_multiplier=1).then_inc(made.sem, 1)
                    for s in range(3 * KT):
                        sq.add(pool, s)

                @block.vector
                def _(dve):
                    dve.wait_ge(*v_kept(2))
                    dve.tensor_tensor(cs_r[:, :, 9:18], csT[:, :, :], cs_r[:, :, 0:9].bitcast(F32), ALU.subtract).then_inc(cs_ready.sem, 1)
                    for u, (t0, n) in enumerate(UNITS):
                        for k in range(0, KT, 2):
                            g = KT * u + k
                            dve.wait_ge(*x_turned(g + 1))
                            dve.tensor_copy(xT[:, k, t0:t0 + n], ps[:, g % 6, 0:n]).then_inc(x_kept.sem, 1)
                        for g in range(4 * u, 4 * u + 4):
                            ada_low(dve, g, g % 4, g % 2)
                            if g == 1:
                                dve.wait_ge(*v_kept(4))
                            if g:
                                ada_keep(dve, g - 1, 6 + (g - 1) % 2)
                    ada_keep(dve, 11, 7)

                @block.tensor
                def _(pe):
                    pe.wait_ge(*made(4))
                    pe.wait_ge(*c_silu(1))
                    for k in range(KT):
                        ins = pe.transpose(ps[:, 6, 9 * k:9 * k + 9], crow2[:, 128 * k:128 * k + 128], ident[0:9, 0:9])
                    ins.then_inc(v_turned.sem, 1)
                    pe.wait_ge(*small_in(16 * 9))
                    pe.transpose(ps[:, 7, 0:ALL_T], brow[:, :], ident[0:ALL_T, 0:ALL_T])
                    pe.transpose(ps[:, 7, 128:248], vrow[:, :], ident[0:120, 0:120]).then_inc(v_turned.sem, 1)
                    for g in range(3 * KT):
                        u, k = divmod(g, KT)
                        if g % KT == 0:
                            pe.wait_ge(*x_in[u](48))
                        if g >= 6:
                            e, m = (x_kept, (g - 6) // 2 + 1) if g % 2 == 0 else (x_kept_a, (g - 7) // 2 + 1)
                            pe.wait_ge(*e(m))
                        for c in range(3):
                            tt = 3 * u + c
                            rows = 64 if tt == 8 else P
                            ins = pe.transpose(ps[:, g % 6, 128 * c:128 * c + rows],
                                               xtok[0:rows, tt, 128 * k:128 * k + 128], ident[0:rows, 0:rows])
                        ins.then_inc(x_turned.sem, 1)
                        if k == KT - 1:
                            if u == 0:
                                pe.wait_ge(*cs_ready(1))
                                pe.wait_ge(*v_kept(4))
                            for a in range(4 * u, 4 * u + 4):
                                ada_product(pe, a, 6 + a % 2, a % 2, reused=a >= 2)
            sq.close()
            ada_in[0].base += 48

        class Norm:

            def __init__(self, g_at, shift, scale, final=False, gate=None, factor=None):
                self.g_at, self.shift, self.scale, self.final, self.gate, self.factor = g_at, shift, scale, final, gate, factor
                self.dst = y_out if final else hhi

            def means(self, pe):
                for n, (t0, w) in enumerate(UNITS):
                    pe.matmul(ps[:, n, 0:w], mean[:, :], rr[:, t0:t0 + w], start=True, stop=True).then_inc(mean_done.sem, 1)

            def roots(self, act):
                for n, (t0, w) in enumerate(UNITS):
                    act.wait_ge(*mean_done(n + 1))
                    act.activation(rr[:, t0:t0 + w], ps[:, n, 0:w], ACT.Sqrt, bias=eps_col[:, 0:1]).then_inc(rms_done.sem, 1)

            def high(self, act, j):
                n, k = divmod(j, KT)
                t0, w = UNITS[n]
                wp = w if n < 2 else TAIL_P
                act.wait_ge(*t_done(j + 1))
                act.activation(self.dst[:, k, t0:t0 + wp], ring[:, j % RINGS, 0:wp], ACT.Identity,
                               bias=ada[:, self.shift + k, 0:1]).then_inc(hi_done.sem, 1)

            def high_samples(self, act):
                act.wait_ge(*t_done(3 * KT + 1))
                act.activation(self.dst[:, :, SEQ:T], ts[:, :, :, :].rearrange("p k s t -> p k (s t)"),
                               ACT.Copy).then_inc(hi_done.sem, 1)

            def factors(self, dve):
                scale, g_at, gate = self.scale, self.g_at, self.gate
                dve.scalar_tensor_tensor(out=gp[:, :], in0=ada[:, scale:scale + KT, 0], scalar=1.0,
                                         in1=vT[:, g_at:g_at + KT], op0=ALU.add, op1=ALU.mult).then_inc(*dve_steps.one())
                dve.scalar_tensor_tensor(out=gs[:, :, :], in0=ada[:, scale:scale + KT, 1:9], scalar=1.0,
                                         in1=bc(vT[:, g_at:g_at + KT], 2, NSEQ), op0=ALU.add,
                                         op1=ALU.mult).then_inc(*dve_steps.one())

            def gates(self, dve):
                gate = self.gate
                dve.tensor_scalar(gate_p[:, :], ada[:, gate:gate + KT, 0], self.factor, None, ALU.mult).then_inc(*dve_steps.one())
                dve.tensor_scalar(gate_s[:, :, :], ada[:, gate:gate + KT, 1:9], self.factor, None, ALU.mult).then_inc(*dve_steps.one())
                dve.wait_ge(*dve_steps.now())

            def low(self, dve, j):
                if self.final:
                    return
                n, k = divmod(j, KT)
                t0, w = UNITS[n]
                wp = w if n < 2 else TAIL_P
                dve.wait_ge(*hi_done(j + 1))
                dve.scalar_tensor_tensor(out=hlo[:, k, t0:t0 + wp], in0=ring[:, j % RINGS, 0:wp],
                                         scalar=ada[:, self.shift + k, 0:1], in1=hhi[:, k, t0:t0 + wp].bitcast(F32),
                                         op0=ALU.add, op1=ALU.subtract).then_inc(lo_done.sem, 1)

            def unit(self, dve, n, between=None):
                t0, w = UNITS[n]
                wp = w if n < 2 else TAIL_P
                dve.wait_ge(*rms_done(n + 1))
                dve.reciprocal(rr[:, t0:t0 + w], rr[:, t0:t0 + w]).then_inc(*dve_steps.one())
                dve.wait_ge(*dve_steps.now())
                for k in range(KT):
                    j = n * KT + k
                    if j >= RINGS:
                        dve.wait_ge(*(hi_done if self.final else lo_done)(j - RINGS + 1))
                    dve.scalar_tensor_tensor(out=ring[:, j % RINGS, 0:wp], in0=xT[:, k, t0:t0 + wp],
                                             scalar=gp[:, k:k + 1], in1=rr[:, t0:t0 + wp],
                                             op0=ALU.mult, op1=ALU.mult).then_inc(t_done.sem, 1)
                    if k >= 2:
                        self.low(dve, j - 2)
                    if between and k == 3:
                        between()
                self.low(dve, n * KT + KT - 2)
                self.low(dve, n * KT + KT - 1)

            def samples(self, dve):
                shift = self.shift
                xs = xT[:, :, SEQ:T].rearrange("p k (s t) -> p k s t", t=STOK)
                dve.tensor_tensor(ts[:, :, :, :], xs, bc(gs[:, :, :], 3, STOK), ALU.mult).then_inc(*dve_steps.one())
                dve.wait_ge(*dve_steps.now())
                tsf = ts[:, :, :, :].rearrange("p k s t -> p k (s t)")
                dve.tensor_tensor(tsf, tsf, bc(rr[:, SEQ:T], 1, KT), ALU.mult).then_inc(*dve_steps.one())
                dve.wait_ge(*dve_steps.now())
                dve.tensor_tensor(ts[:, :, :, :], ts[:, :, :, :], bc(ada[:, shift:shift + KT, 1:9], 3, STOK),
                                  ALU.add).then_inc(t_done.sem, 1)
                if not self.final:
                    dve.wait_ge(*hi_done(3 * KT + 1))
                    dve.wait_ge(*t_done(3 * KT + 1))
                    dve.tensor_tensor(hlo[:, :, SEQ:T], tsf, hhi[:, :, SEQ:T].bitcast(F32), ALU.subtract).then_inc(lo_done.sem, 1)

            def close(self):
                mean_done.base += 3
                rms_done.base += 3
                t_done.base += 3 * KT + 1
                hi_done.base += 3 * KT + 1
                lo_done.base += 0 if self.final else 3 * KT + 1

        def norm_alone(norm):
            with nc.Block() as block:
                @block.tensor
                def _(pe):
                    norm.means(pe)

                @block.scalar
                def _(act):
                    norm.roots(act)
                    for j in range(3 * KT):
                        norm.high(act, j)
                    norm.high_samples(act)

                @block.vector
                def _(dve):
                    norm.factors(dve)
                    for n in range(3):
                        norm.unit(dve, n)
                    norm.samples(dve)
                    norm.gates(dve)
            norm.close()

        ffn_counts = {n: cnt("ffn_" + n) for n in (
            "a_in", "b_in", "o_in", "a_hi", "b_hi", "o_hi", "a_lo", "b_lo", "o_lo",
            "a_unit", "b_unit", "out_unit", "silu", "hidden", "hid_hi", "hid_lo", "x_added")}
        ffn_mem = {}

        OUT_ORDER = [(0, 0), (0, 1), (1, 0), (1, 1), (0, 2), (1, 2)] + [(m, n) for m in range(2, KT) for n in range(3)]

        def add_out(dve, own, m, n, bank, tmp, x_added):
            t0, w = UNITS[n]
            wp = w if n < 2 else TAIL_P
            ins = dve.scalar_tensor_tensor(out=xT[:, m, t0:t0 + wp], in0=ps[:, bank, 0:wp], scalar=gate_p[:, m:m + 1],
                                           in1=xT[:, m, t0:t0 + wp], op0=ALU.mult, op1=ALU.add)
            if n < 2:
                ins.then_inc(x_added.sem, 1)
                return
            ins.then_inc(*own.one())
            dve.tensor_tensor(tmp, ps[:, bank, TAIL_P:w].rearrange("p (s t) -> p s t", t=STOK),
                              bc(gate_s[:, m, :], 2, STOK), ALU.mult).then_inc(*own.one())
            dve.wait_ge(*own.now())
            xs = xT[:, m, SEQ:T].rearrange("p (s t) -> p s t", t=STOK)
            dve.tensor_tensor(xs, xs, tmp, ALU.add).then_inc(x_added.sem, 1)

        def ffn(w_up, w_down, norm, ada_first=None):
            if not ffn_mem:
                ar.at = work
                for nm in ("a", "b", "o"):
                    ffn_mem[nm + "_raw"] = None
                    ffn_mem[nm + "_hi"] = ar.put(f"w{nm}_hi", [P, 2048], F32R)
                    at = ar.at
                    ffn_mem[nm + "_lo"] = ar.put(f"w{nm}_lo", [P, 2048], F32R)
                    ffn_mem[nm + "_raw"] = ar.put(f"w{nm}_raw", [P, 2048], at=at)
                ffn_mem["g_hi"] = ar.put("g_hi", [P, 2, T], F32R)
                ffn_mem["g_lo"] = ar.put("g_lo", [P, 2, T], F32R)
                ffn_mem["st"] = ar.put("st", [P, 3, 384])
                ffn_mem["hf"] = ar.put("hf", [P, 3, 384])
                ffn_mem["tmp"] = ar.put("ffn_tmp", [P, 4, NSEQ, STOK])
                assert ar.at <= top
            M = ffn_mem
            C = ffn_counts
            sq = Squares(OUT_ORDER)
            ADA_BLOCKS = (ALL_T // 2 - ada_first) // 4 if ada_first else 0

            def group(b, q):
                return b * 4 + (ada_first - 4 + q)
            up_d = w_up.rearrange("(k p) n -> p k n", p=P)
            down_d = w_down.rearrange("(b k p) n -> p b k n", k=2, p=P)

            def part(nm, kind, i):
                t = M[f"{nm}_{kind}"]
                if nm == "o":
                    return t[:, 1024 * i:1024 * i + 1024]
                return t[:, :].rearrange("p (k n) -> p k n", n=256)[:, :, 128 * i:128 * i + 128]

            with nc.Block() as block:
                @block.sync
                def _(sp):
                    def load(nm, b):
                        dst = M[f"{nm}_raw"]
                        if nm == "o":
                            src = down_d[:, b, :, :] if isinstance(b, int) else down_d[:, bass.ds(b, 1), :, :].squeeze(1)
                            sp.dma_start(dst[:, :].rearrange("p (k n) -> p k n", k=2), src).then_inc(C["o_in"].sem, 16)
                        else:
                            off = 0 if nm == "a" else DFF
                            sp.dma_start(dst[:, :].rearrange("p (k n) -> p k n", k=KT),
                                         up_d[:, :, bass.ds(b * 256 + off, 256)]).then_inc(C[nm + "_in"].sem, 16)
                    load("a", 0)
                    load("b", 0)
                    load("o", 0)

                    def body(b, ada_too):
                        sp.wait_ge(*C["a_unit"](b * 6))
                        load("a", b)
                        sp.wait_ge(*C["b_unit"](b * 6))
                        load("b", b)
                        for q in range(4 if ada_too else 0):
                            sp.wait_ge(*ada_lo_done(group(b, q) * 2))
                            ada_load(sp, group(b, q))
                            if q == 0:
                                sp.wait_ge(*C["out_unit"](b * 24))
                                load("o", b)
                        if not ada_too:
                            sp.wait_ge(*C["out_unit"](b * 24))
                            load("o", b)

                    if ada_first:
                        with sp.Fori(1, (ADA_T // 2 - ada_first) // 4 + 1) as b:
                            body(b, True)
                        for b in range((ADA_T // 2 - ada_first) // 4 + 1, FB):
                            body(b, b <= ADA_BLOCKS)
                    else:
                        with sp.Fori(1, FB) as b:
                            body(b, False)

                def blocks(eng, body, own=None):
                    def loop(first, end, ada_too):
                        with eng.Fori(first, end) as b:
                            if own:
                                own.enter(b, 2 * KT + (4 if ada_too else 0), first=first)
                            body(b, ada_too, False)
                            if own:
                                own.leave(end - first)
                    body(0, False, False)
                    if ada_first:
                        loop(1, ADA_BLOCKS + 1, True)
                        for b in range(ADA_BLOCKS + 1, FB - 1):
                            body(b, False, False)
                    else:
                        loop(1, FB - 1, False)
                    body(FB - 1, False, True)

                @block.scalar
                def _(act):
                    def split(nm, i, b):
                        if i == 0:
                            act.wait_ge(*C[nm + "_in"](b * 16 + 16))
                        act.activation(part(nm, "hi", i), part(nm, "raw", i), ACT.Copy).then_inc(C[nm + "_hi"].sem, 1)

                    def silu(i, n, b):
                        act.wait_ge(*C["a_unit"](b * 6 + 3 * i + n + 1))
                        if i == 1:
                            act.wait_ge(*C["hidden"](b * 6 + n + 1))
                        w = UNITS[n][1]
                        act.activation(M["st"][:, n, 0:w], ps[:, n, 0:w], ACT.Silu).then_inc(C["silu"].sem, 1)

                    def hid(i, n, b):
                        t0, w = UNITS[n]
                        act.wait_ge(*C["hidden"](b * 6 + 3 * i + n + 1))
                        act.activation(M["g_hi"][:, i, t0:t0 + w], M["hf"][:, n, 0:w], ACT.Copy).then_inc(C["hid_hi"].sem, 1)

                    def high(b, q):
                        ada_high(act, (b - 1) * 4 + q, group(b, q))

                    def body(b, ada_too, last):
                        if ada_too:
                            high(b, 0)
                        split("b", 1, b)
                        for n in range(3):
                            silu(0, n, b)
                            hid(0, n, b)
                            if n == 0 and ada_too:
                                high(b, 1)
                            if n > 0:
                                split("o", n - 1, b)
                        if ada_too:
                            high(b, 2)
                        for n in range(3):
                            silu(1, n, b)
                            hid(1, n, b)
                            if n == 0 and ada_too:
                                high(b, 3)
                        if not last:
                            split("a", 0, b + 1)
                            split("b", 0, b + 1)
                            split("a", 1, b + 1)
                        else:
                            for u in range(24):
                                act.wait_ge(*C["x_added"](b * 24 + u + 1))
                                sq.square(act, u)

                    norm.roots(act)
                    for j in range(3 * KT):
                        if j == 4:
                            split("a", 0, 0)
                            split("b", 0, 0)
                        if j == 2 * KT:
                            split("a", 1, 0)
                        norm.high(act, j)
                    norm.high_samples(act)
                    blocks(act, body)

                @block.gpsimd
                def _(pool):
                    for u in range(24):
                        sq.add(pool, u)

                @block.vector
                def _(dve):
                    own = dve_steps

                    def split(nm, i, b):
                        dve.wait_ge(*C[nm + "_hi"](b * 2 + i + 1))
                        dve.tensor_tensor(part(nm, "lo", i), part(nm, "raw", i), part(nm, "hi", i).bitcast(F32),
                                          ALU.subtract).then_inc(C[nm + "_lo"].sem, 1)

                    def hidden(i, n, b):
                        w = UNITS[n][1]
                        dve.wait_ge(*C["b_unit"](b * 6 + 3 * i + n + 1))
                        dve.wait_ge(*C["silu"](b * 6 + 3 * i + n + 1))
                        if i == 1:
                            dve.wait_ge(*C["hid_lo"](b * 6 + n + 1))
                            dve.wait_ge(*C["hid_hi"](b * 6 + n + 1))
                        dve.tensor_tensor(M["hf"][:, n, 0:w], M["st"][:, n, 0:w], ps[:, 3 + n, 0:w],
                                          ALU.mult).then_inc(C["hidden"].sem, 1)

                    def low(i, n, b):
                        t0, w = UNITS[n]
                        dve.wait_ge(*C["hid_hi"](b * 6 + 3 * i + n + 1))
                        dve.tensor_tensor(M["g_lo"][:, i, t0:t0 + w], M["hf"][:, n, 0:w],
                                          M["g_hi"][:, i, t0:t0 + w].bitcast(F32), ALU.subtract).then_inc(C["hid_lo"].sem, 1)

                    def body(b, ada_too, last):
                        if ada_too:
                            ada_low(dve, group(b, 0))
                        split("b", 1, b)
                        for n in range(3):
                            hidden(0, n, b)
                            low(0, n, b)
                            if n == 0 and ada_too:
                                ada_keep(dve, group(b, 0), 6)
                                ada_low(dve, group(b, 1))
                            if n > 0:
                                split("o", n - 1, b)
                        if ada_too:
                            ada_keep(dve, group(b, 1), 7)
                            ada_low(dve, group(b, 2))
                        for n in range(3):
                            hidden(1, n, b)
                            low(1, n, b)
                            if n == 0 and ada_too:
                                ada_keep(dve, group(b, 2), 6)
                                ada_low(dve, group(b, 3))
                        if ada_too:
                            ada_keep(dve, group(b, 3), 7)
                        for u, (m, n) in enumerate(OUT_ORDER):
                            dve.wait_ge(*C["out_unit"](b * 24 + u + 1))
                            add_out(dve, own, m, n, u % 6, M["tmp"][:, m % 4, :, :], C["x_added"])
                            if not last and u in (9, 13, 17):
                                split(*{9: ("a", 0), 13: ("b", 0), 17: ("a", 1)}[u], b + 1)

                    norm.factors(dve)
                    norm.unit(dve, 0, between=lambda: split("a", 0, 0))
                    split("b", 0, 0)
                    norm.unit(dve, 1)
                    split("a", 1, 0)
                    norm.unit(dve, 2)
                    norm.samples(dve)
                    norm.gates(dve)
                    blocks(dve, body, own)

                @block.tensor
                def _(pe):
                    def three(bank, w, pairs):
                        last = len(pairs) - 1
                        for j, (wh, wl, xh, xl) in enumerate(pairs):
                            pe.matmul(ps[:, bank, 0:w], wh, xh, start=(j == 0), stop=False)
                            pe.matmul(ps[:, bank, 0:w], wh, xl, start=False, stop=False)
                            ins = pe.matmul(ps[:, bank, 0:w], wl, xh, start=False, stop=(j == last))
                        return ins

                    def up(nm, i, n, b):
                        t0, w = UNITS[n]
                        first = isinstance(b, int) and b == 0
                        bank = n if nm == "a" else 3 + n
                        if i == 1:
                            pe.wait_ge(*C["silu" if nm == "a" else "hidden"](b * 6 + n + 1))
                        elif not first:
                            pe.wait_ge(*C["x_added"](b * 24 - 6 + bank + 1))
                        wh, wl = part(nm, "hi", i), part(nm, "lo", i)
                        for k in range(KT):
                            if first and i == 0 and nm == "a":
                                pe.wait_ge(*lo_done(n * KT + k + 1 if n < 2 or k else 3 * KT + 1))
                            xh, xl = hhi[:, k, t0:t0 + w], hlo[:, k, t0:t0 + w]
                            pe.matmul(ps[:, bank, 0:w], wh[:, k, :], xh, start=(k == 0), stop=False)
                            pe.matmul(ps[:, bank, 0:w], wh[:, k, :], xl, start=False, stop=False)
                            ins = pe.matmul(ps[:, bank, 0:w], wl[:, k, :], xh, start=False, stop=(k == KT - 1))
                        ins.then_inc(C[nm + "_unit"].sem, 1)

                    def body(b, ada_too, last):
                        for i in range(2):
                            pe.wait_ge(*C["a_lo"](b * 2 + i + 1))
                            for n in range(3):
                                up("a", i, n, b)
                                if n == 0:
                                    pe.wait_ge(*C["b_lo"](b * 2 + i + 1))
                                up("b", i, n, b)
                                if ada_too and n != 1:
                                    q = 2 * i + n // 2
                                    ada_product(pe, group(b, q), 6 + q % 2)
                        pe.wait_ge(*C["o_lo"](b * 2 + 2))
                        for u, (m, n) in enumerate(OUT_ORDER):
                            t0, w = UNITS[n]
                            if u < 3:
                                pe.wait_ge(*C["silu"](b * 6 + 3 + u + 1))
                            elif u < 6:
                                pe.wait_ge(*C["hidden"](b * 6 + u + 1))
                            else:
                                pe.wait_ge(*C["x_added"](b * 24 + u - 6 + 1))
                            if m == 0:
                                pe.wait_ge(*C["hid_lo"](b * 6 + 3 + n + 1))
                            ms = slice(128 * m, 128 * m + 128)
                            ins = three(u % 6, w, [(part("o", "hi", i)[:, ms], part("o", "lo", i)[:, ms],
                                                    M["g_hi"][:, i, t0:t0 + w], M["g_lo"][:, i, t0:t0 + w])
                                                   for i in range(2)])
                            ins.then_inc(C["out_unit"].sem, 1)

                    norm.means(pe)
                    blocks(pe, body)
            norm.close()
            sq.close()
            if ada_first:
                ada_in[0].base += 16 * 4 * ADA_BLOCKS

            for n, c in C.items():
                c.base += {"a_in": 16, "b_in": 16, "o_in": 16, "a_hi": 2, "b_hi": 2, "o_hi": 2, "a_lo": 2, "b_lo": 2,
                           "o_lo": 2, "a_unit": 6, "b_unit": 6, "out_unit": 24,
                           "silu": 6, "hidden": 6, "hid_hi": 6, "hid_lo": 6, "x_added": 24}[n] * FB

        def mixer_memory():
            ar.at = work
            m = {}
            m["m_rows"] = ar.put("m_rows", [H, T])
            m["tok"] = ar.put("tok", [P, NTT, 4, H])
            m["a_prev"] = ar.put("a_prev", [H, 16])
            m["m_new"] = ar.put("m_new", [H, 16])
            m["conv_in"] = ar.put("conv_in", [P, 2, KT, NSEQ * 3])
            m["n_in"] = ar.put("n_in", [P, 2, NSEQ, H])
            m["tails"] = ar.put("tails", [P, 2 * KT, 27])
            m["n_out"] = ar.put("n_out", [P, 2, NSEQ, H])
            m["np_out"] = ar.put("np_out", [P, 2, H])
            m["neg_mask"] = ar.put("neg_mask", [P, P])
            m["neg_diag"] = ar.put("neg_diag", [64, 64])
            m["seq_mask"] = ar.put("seq_mask", [64, NSEQ])
            m["half"] = ar.put("half", [P, NTT])
            m["w_hi"], m["w_lo"], m["w_raw"] = [], [], []
            m["ring_at"] = ar.at
            for s in range(2):
                m["w_hi"].append(ar.put(f"mw{s}_hi", [P, 2048], F32R))
                at = ar.at
                m["w_lo"].append(ar.put(f"mw{s}_lo", [P, 2048], F32R))
                m["w_raw"].append(ar.put(f"mw{s}_raw", [P, 2048], at=at))
            return m, ar.at

        def pair_part(M, kind, slot, i, rows=False):
            t = M["w_" + kind][slot]
            if rows:
                return t[:, 1024 * i:1024 * i + 1024]
            return t[:, :].rearrange("p (k n) -> p k n", n=256)[:, :, 128 * i:128 * i + 128]

        def three(pe, out, operands):
            last = len(operands) - 1
            for j, (wh, wl, xh, xl) in enumerate(operands):
                pe.matmul(out, wh, xh, start=(j == 0), stop=False)
                pe.matmul(out, wh, xl, start=False, stop=False)
                ins = pe.matmul(out, wl, xh, start=False, stop=(j == last))
            return ins

        def split_counts():
            return cnt("mw_hi_done"), cnt("mw_lo_done")

        w_d = I["w_in"][0].rearrange("(k p) n -> p k n", p=P)

        def gates_and_v(M, free, v_raw):
            ar.at = free
            rows_i = ar.put("rows_i", [H, T])
            rows_l = ar.put("rows_l", [H, T])
            rows_k = ar.put("rows_k", [H, T])
            rows_q = ar.put("rows_q", [P, T])
            bias_i = ar.put("bias_i", [H, 1])
            bias_f = ar.put("bias_f", [H, 1])
            m0 = ar.put("m0", [H, NSEQ])
            b_last = ar.put("b_last", [H, 16])
            a_max = ar.put("a_max", [H, 16])
            m_prev = ar.put("m_prev", [H, 16])
            m_last = ar.put("m_last", [H, 16])
            m_rows, tok, a_prev, m_new = M["m_rows"], M["tok"], M["a_prev"], M["m_new"]
            zeroed, gate_in, small, v_in = cnt("g_zeroed"), cnt("gate_in"), cnt("gate_small"), [cnt(f"v_in{p}") for p in range(4)]
            g_unit, v_unit, v_kept = cnt("gate_unit"), cnt("v_unit"), cnt("gelu_v_kept")
            hi_done, lo_done = cnt("gv_hi_done"), cnt("gv_lo_done")
            abs_ready, log_ready, e_ready, e_done = cnt("abs_ready"), cnt("log_ready"), cnt("e_ready"), cnt("e_done")
            q_turned, tok_done, m_out = cnt("q_turned"), cnt("tok_done"), cnt("m_out")
            PRO, SAM = slice(0, SEQ), slice(SEQ, T)

            def chunks(row):
                return (row[:, PRO].rearrange("h (c t) -> h c t", t=CHUNK), row[:, SAM].rearrange("h (c t) -> h c t", t=STOK))

            with nc.Block() as block:
                @block.sync
                def _(sp):
                    sp.wait_ge(*zeroed(1))
                    gw = pair_part(M, "raw", 0, 0)
                    sp.dma_start(gw[:, :, 0:4], w_d[:, :, GATE_COLS:GATE_COLS + 4]).then_inc(gate_in.sem, 16)
                    sp.dma_start(gw[:, :, 32:36], w_d[:, :, GATE_COLS + 4:GATE_COLS + 8]).then_inc(gate_in.sem, 16)
                    for p in range(4):
                        if p == 1:
                            sp.wait_ge(*g_unit(3))
                        if p > 1:
                            sp.wait_ge(*v_unit(9 * (p - 1)))
                        sp.dma_start(M["w_raw"][(p + 1) % 2][:, :].rearrange("p (k n) -> p k n", k=KT),
                                     w_d[:, :, V_COLS + 256 * p:V_COLS + 256 * p + 256]).then_inc(v_in[p].sem, 16)
                    sp.wait_ge(*tok_done(NTT + 1))
                    sp.dma_start(O["m_prompt"].rearrange("l b h -> h (l b)"), m_new[:, 7:8]).then_inc(m_out.sem, 16)
                    with nc.allow_non_contiguous_dma(reason="32 numbers"):
                        sp.dma_start(O["m_sample"].rearrange("l b h -> h (l b)"), m_new[:, 8:16]).then_inc(m_out.sem, 16)
                    sp.wait_ge(*m_out(32))

                @block.gpsimd
                def _(pool):
                    pool.memset(pair_part(M, "raw", 0, 0), 0.0).then_inc(zeroed.sem, 1)
                    with nc.allow_non_contiguous_dma(reason="a few numbers"):
                        pool.dma_start(bias_i[:, :], I["b_gates"][0:1, 0:H].rearrange("l h -> h l")).then_inc(small.sem, 16)
                        pool.dma_start(bias_f[:, :], I["b_gates"][0:1, H:2 * H].rearrange("l h -> h l")).then_inc(small.sem, 16)
                        pool.dma_start(m0[:, :], I["state_mlstm_m"].rearrange("l b h -> h (l b)")).then_inc(small.sem, 16)
                    pool.memset(rows_k[:, :], 1.0).then_inc(*pool_steps.one())
                    pool.memset(m_prev[:, :], 0.0).then_inc(*pool_steps.one())
                    pool.memset(rows_q[:, :], 0.0).then_inc(*pool_steps.one())
                    pool.wait_ge(*pool_steps.now())
                    kp, ks = chunks(rows_k)
                    pool.memset(kp[:, :, 0:1], 0.0).then_inc(*pool_steps.one())
                    pool.memset(ks[:, :, 0:1], 0.0).then_inc(zeroed.sem, 1)

                @block.scalar
                def _(act):
                    act.wait_ge(*gate_in(32))
                    act.activation(pair_part(M, "hi", 0, 0), pair_part(M, "raw", 0, 0), ACT.Copy).then_inc(hi_done.sem, 1)

                    def split(p):
                        act.wait_ge(*v_in[p](16))
                        for i in range(2):
                            s = (p + 1) % 2
                            act.activation(pair_part(M, "hi", s, i), pair_part(M, "raw", s, i), ACT.Copy).then_inc(hi_done.sem, 1)

                    split(0)
                    for p in range(4):
                        for t in range(NTT):
                            rows = 64 if t == 8 else P
                            act.wait_ge(*v_unit(9 * p + t + 1))
                            r0 = 64 if t == 8 else 0
                            act.activation(v_raw[0:rows, t, 256 * p:256 * p + 256], ps[r0:r0 + rows, 3 + t % 3, 0:256],
                                           ACT.Gelu_apprx_tanh).then_inc(v_kept.sem, 1)
                            if t == 1 and p < 3:
                                split(p + 1)
                            if (p, t) == (0, 2):
                                act.wait_ge(*abs_ready(1))
                                act.activation(rows_l[:, :], rows_l[:, :], ACT.Exp, scale=-1.0).then_inc(*act_steps.one())
                                act.wait_ge(*act_steps.now())
                                act.activation(rows_l[:, :], rows_l[:, :], ACT.Ln, bias=1.0).then_inc(log_ready.sem, 1)
                            if (p, t) == (1, 6):
                                act.wait_ge(*e_ready(1))
                                act.activation(a_prev[:, :], m_last[:, :], ACT.Exp).then_inc(*act_steps.one())
                                act.activation(rows_q[32:36, :], rows_k[:, :], ACT.Exp).then_inc(e_done.sem, 1)
                                act.wait_ge(*e_ready(2))
                                act.activation(rows_q[64:68, :], rows_k[:, :], ACT.Exp).then_inc(e_done.sem, 1)
                                act.wait_ge(*e_ready(3))
                                act.activation(rows_q[96:100, :], rows_k[:, :], ACT.Exp, scale=-1.0).then_inc(e_done.sem, 1)

                @block.vector
                def _(dve):
                    own = dve_steps

                    def low(n, s, i):
                        dve.wait_ge(*hi_done(n))
                        dve.tensor_tensor(pair_part(M, "lo", s, i), pair_part(M, "raw", s, i),
                                          pair_part(M, "hi", s, i).bitcast(F32), ALU.subtract).then_inc(lo_done.sem, 1)

                    def split(p):
                        for i in range(2):
                            low(2 * p + i + 2, (p + 1) % 2, i)

                    def link(ins):
                        ins.then_inc(*own.one())
                        dve.wait_ge(*own.now())

                    low(1, 0, 0)
                    split(0)
                    dve.wait_ge(*small(48))
                    dve.wait_ge(*zeroed(2))
                    for n, (t0, w) in enumerate(UNITS):
                        dve.wait_ge(*g_unit(n + 1))
                        dve.tensor_scalar(rows_i[:, t0:t0 + w], ps[0:4, n, 0:w], bias_i[:, 0:1], None, ALU.add).then_inc(*own.one())
                        link(dve.tensor_scalar(m_rows[:, t0:t0 + w], ps[32:36, n, 0:w], bias_f[:, 0:1], None, ALU.add))
                    dve.scalar_tensor_tensor(out=rows_l[:, :], in0=m_rows[:, :], scalar=-1.0, in1=m_rows[:, :],
                                             op0=ALU.mult, op1=ALU.max).then_inc(abs_ready.sem, 1)
                    dve.wait_ge(*log_ready(1))
                    link(dve.scalar_tensor_tensor(out=m_rows[:, :], in0=m_rows[:, :], scalar=0.0, in1=rows_l[:, :],
                                                  op0=ALU.min, op1=ALU.subtract))
                    link(dve.tensor_tensor_scan(rows_l[:, :], rows_k[:, :], m_rows[:, :], 0.0, ALU.mult, ALU.add))
                    dve.tensor_tensor(rows_i[:, :], rows_i[:, :], rows_l[:, :], ALU.subtract).then_inc(*own.one())
                    link(dve.tensor_scalar(rows_k[:, :], rows_k[:, :], -1.0, BIG, ALU.add, ALU.mult))
                    link(dve.tensor_tensor_scan(m_rows[:, :], rows_k[:, :], rows_i[:, :], -BIG, ALU.add, ALU.max))
                    split(1)
                    for dst, src in ((b_last, rows_l), (a_max, m_rows)):
                        sp_, ss_ = chunks(src)
                        dve.tensor_copy(dst[:, 0:8], sp_[:, :, CHUNK - 1]).then_inc(*own.one())
                        link(dve.tensor_copy(dst[:, 8:16], ss_[:, :, STOK - 1]))
                    dve.tensor_copy(m_prev[:, 8:16], m0[:, :]).then_inc(*own.one())
                    dve.tensor_tensor(m_new[:, 8:16], a_max[:, 8:16], m0[:, :], ALU.max).then_inc(*own.one())
                    link(dve.tensor_tensor_scan(m_new[:, 0:8], a_max[:, 0:8], b_last[:, 0:8], 0.0, ALU.max, ALU.add))
                    link(dve.tensor_tensor(m_new[:, 8:16], m_new[:, 8:16], b_last[:, 8:16], ALU.add))
                    link(dve.tensor_copy(m_prev[:, 1:8], m_new[:, 0:7]))
                    link(dve.tensor_tensor(a_max[:, :], m_prev[:, :], a_max[:, :], ALU.max))
                    link(dve.tensor_tensor(m_last[:, :], m_prev[:, :], a_max[:, :], ALU.subtract))
                    for mr, c0, L in zip(chunks(m_rows), (0, 8), (CHUNK, STOK)):
                        link(dve.tensor_tensor(mr, mr, bc(m_prev[:, c0:c0 + 8], 2, L), ALU.max))
                    dve.tensor_copy(rows_q[0:4, :], rows_i[:, :]).then_inc(*own.one())
                    for n, (kr, ir, c0, L) in enumerate(zip(chunks(rows_k), chunks(rows_i), (0, 8), (CHUNK, STOK))):
                        ins = dve.tensor_tensor(kr, ir, bc(a_max[:, c0:c0 + 8], 2, L), ALU.subtract)
                        ins.then_inc(*(own.one() if n == 0 else (e_ready.sem, 1)))
                    dve.wait_ge(*e_done(1))
                    split(2)
                    for n, (kr, mr, c0, L) in enumerate(zip(chunks(rows_k), chunks(m_rows), (0, 8), (CHUNK, STOK))):
                        ins = dve.tensor_tensor(kr, bc(m_prev[:, c0:c0 + 8], 2, L), mr, ALU.subtract)
                        ins.then_inc(*(own.one() if n == 0 else (e_ready.sem, 1)))
                    dve.wait_ge(*e_done(2))
                    dve.tensor_tensor(rows_k[:, :], rows_l[:, :], m_rows[:, :], ALU.add).then_inc(e_ready.sem, 1)
                    split(3)
                    for t in range(NTT):
                        rows = 64 if t == 8 else P
                        dve.wait_ge(*q_turned(t + 1))
                        dve.tensor_copy(tok[0:rows, t, :, :],
                                        ps[0:rows, 6 + t % 2, 0:P].rearrange("p (q h) -> p q h", h=32)[:, :, 0:H]
                                        ).then_inc(tok_done.sem, 1)
                    dve.wait_ge(*tok_done(NTT))
                    dve.tensor_scalar(tok[:, 0:8, 1, :], tok[:, 0:8, 1, :], 1.0 / 16, None, ALU.mult).then_inc(*own.one())
                    dve.tensor_scalar(tok[0:64, 8, 1, :], tok[0:64, 8, 1, :], 1.0 / 16, None, ALU.mult).then_inc(tok_done.sem, 1)

                @block.tensor
                def _(pe):
                    pe.wait_ge(*lo_done(1))
                    wh, wl = pair_part(M, "hi", 0, 0), pair_part(M, "lo", 0, 0)
                    for n, (t0, w) in enumerate(UNITS):
                        three(pe, ps[:, n, 0:w], [(wh[:, k, :], wl[:, k, :], hhi[:, k, t0:t0 + w], hlo[:, k, t0:t0 + w])
                                                  for k in range(KT)]).then_inc(g_unit.sem, 1)
                    for p in range(4):
                        pe.wait_ge(*lo_done(2 * p + 3))
                        s = (p + 1) % 2
                        wh = M["w_hi"][s][:, :].rearrange("p (k n) -> p k n", k=KT)
                        wl = M["w_lo"][s][:, :].rearrange("p (k n) -> p k n", k=KT)
                        for t in range(NTT):
                            rows = 64 if t == 8 else P
                            if 9 * p + t >= 3:
                                pe.wait_ge(*v_kept(9 * p + t - 2))
                            a, b = (128 * t, 128 * t + 128) if t < 8 else (T - 128, T)
                            three(pe, ps[:, 3 + t % 3, 0:256],
                                  [(hhi[:, k, a:b], hlo[:, k, a:b], wh[:, k, :], wl[:, k, :]) for k in range(KT)]
                                  ).then_inc(v_unit.sem, 1)
                    pe.wait_ge(*e_done(3))
                    for t in range(NTT):
                        rows = 64 if t == 8 else P
                        if t >= 2:
                            pe.wait_ge(*tok_done(t - 1))
                        pe.transpose(ps[0:rows, 6 + t % 2, 0:P], rows_q[:, 128 * t:128 * t + rows],
                                     ident[:, :]).then_inc(q_turned.sem, 1)

        def spatial(M, free, v, mixed_d):
            ar.at = M["ring_at"]
            ln_g = ar.put("ln_g", [P, D])
            ln_b = ar.put("ln_b", [P, D])
            stage = ar.put("stage", [P, 2, KT, P])
            crow = ar.put("conv_rows", [NSEQ * 3, 2 * D])
            nrow = ar.put("n_rows", [NSEQ * H, DH])
            ar.at = free
            w_rows = ar.put("w_rows", [P, H, P])
            w_diag = ar.put("w_diag", [64, H, 64])
            w_t = ar.put("w_t", [P, H, P])
            w_dt = ar.put("w_dt", [64, H, 64])
            b_s = ar.put("b_s", [P, H, P])
            stats = ar.put("stats", [P, NTT, 2, 6])
            mv = ar.put("mv", [P, NTT, 2])
            rstd = ar.put("rstd", [P, NTT])
            names = ("ln_in", "w_in_", "diag_zero", "diag_in", "states_in", "consts", "w_turned", "w_copied", "w_masked",
                     "stats_done", "rstd_done", "scaled", "gained", "v_ready", "mix_unit", "mix_kept", "mix_out", "v_out",
                     "s_turned", "s_kept")
            (ln_in, w_in_, diag_zero, diag_in, states_in, consts, w_turned, w_copied, w_masked, stats_done, rstd_done,
             scaled, gained, v_ready, mix_unit, mix_kept, mix_out, v_out, s_turned, s_kept) = (cnt("sp_" + n) for n in names)
            mix_out = [mix_out, cnt("sp_mix_out1")]
            with nc.Block() as block:
                @block.sync
                def _(sp):
                    sp.dma_start(ln_g[:, :], I["gmlp_ln_g"].broadcast_to([P, D])).then_inc(ln_in.sem, 16)
                    sp.dma_start(ln_b[:, :], I["gmlp_ln_b"].broadcast_to([P, D])).then_inc(ln_in.sem, 16)
                    sp.dma_start(w_rows[:, :, :], I["gmlp_ws"][0].rearrange("g t s -> t g s")).then_inc(w_in_.sem, 16)
                    sp.dma_start(b_s[:, :, :], I["gmlp_bs"].broadcast_to([P, H, P])).then_inc(w_in_.sem, 16)
                    sp.dma_start(crow[:, :], I["state_conv"].rearrange("l b j c -> (l b j) c")).then_inc(states_in.sem, 16)
                    sp.dma_start(nrow[:, :], I["state_mlstm_n"].rearrange("l b h d -> (l b h) d")).then_inc(states_in.sem, 16)
                    sp.wait_ge(*diag_zero(1))
                    for b in range(NSEQ):
                        sp.dma_start(w_diag[8 * b:8 * b + 8, :, 8 * b:8 * b + 8],
                                     I["gmlp_ws"][0, :, 0:8, 0:8].rearrange("g t s -> t g s")).then_inc(diag_in.sem, 16)
                    md = mixed_d.rearrange("(f p) t -> p f t", p=P)
                    for t in range(NTT):
                        n = 64 if t == 8 else P
                        sp.wait_ge(*mix_kept(2 * t + 2))
                        sp.dma_start(md[:, :, 128 * t:128 * t + n], stage[:, t % 2, :, 0:n]).then_inc(mix_out[t % 2].sem, 16)
                    sp.wait_ge(*v_ready(NTT))
                    sp.dma_start(O["v_sample"].rearrange("l b t d -> (l b t) d"), v[0:64, 8, :]).then_inc(v_out.sem, 16)
                    sp.wait_ge(*v_out(16))
                    sp.wait_ge(*mix_out[0](80))
                    sp.wait_ge(*mix_out[1](64))

                @block.gpsimd
                def _(pool):
                    own = pool_steps
                    pool.memset(w_diag[:, :, :], 0.0).then_inc(diag_zero.sem, 1)
                    pool.memset(M["half"][:, :], -0.5).then_inc(consts.sem, 1)
                    pool.memset(M["neg_mask"][:, :], 0.0).then_inc(*own.one())
                    pool.memset(M["neg_diag"][:, :], 0.0).then_inc(*own.one())
                    pool.memset(M["seq_mask"][:, :], 1.0).then_inc(*own.one())
                    pool.wait_ge(*own.now())
                    pool.affine_select(out=M["neg_mask"][:, :], in_=M["neg_mask"][:, :], compare_op=ALU.is_ge, fill=-BIG,
                                       base=0, pattern=[[1, P]], channel_multiplier=-1).then_inc(*own.one())
                    pool.affine_select(out=M["neg_diag"][:, :], in_=M["neg_diag"][:, :], compare_op=ALU.is_ge, fill=-BIG,
                                       base=0, pattern=[[1, 64]], channel_multiplier=-1).then_inc(*own.one())
                    pool.affine_select(out=M["seq_mask"][:, :], in_=M["seq_mask"][:, :], compare_op=ALU.is_ge, fill=0.0,
                                       base=0, pattern=[[-8, NSEQ]], channel_multiplier=1).then_inc(*own.one())
                    pool.wait_ge(*own.now())
                    nd = M["neg_diag"][:, :].rearrange("s (b t) -> s b t", t=STOK)
                    pool.affine_select(out=nd, in_=nd, compare_op=ALU.is_ge, fill=-BIG, base=0,
                                       pattern=[[-8, NSEQ], [0, STOK]], channel_multiplier=1).then_inc(*own.one())
                    pool.affine_select(out=M["seq_mask"][:, :], in_=M["seq_mask"][:, :], compare_op=ALU.is_ge, fill=0.0,
                                       base=7, pattern=[[8, NSEQ]], channel_multiplier=-1).then_inc(consts.sem, 1)
                    pool.wait_ge(*w_copied(2))
                    for n, (w, L) in enumerate(((w_t, P), (w_dt, 64))):
                        pool.affine_select(out=w[:, :, :], in_=w[:, :, :], compare_op=ALU.is_ge, fill=0.0, base=0,
                                           pattern=[[0, H], [1, L]], channel_multiplier=-1).then_inc(w_masked.sem, 1)
                    pool.wait_ge(*stats_done(NTT))
                    pool.tensor_scalar(rstd[:, :], mv[:, :, 1], EPS, None, ALU.add).then_inc(*own.one())
                    pool.wait_ge(*own.now())
                    pool.tensor_tensor(rstd[:, :], rstd[:, :], M["half"][:, :], ALU.pow).then_inc(rstd_done.sem, 1)
                    pool.wait_ge(*ln_in(32))
                    for t in range(NTT):
                        rows = 64 if t == 8 else P
                        pool.wait_ge(*scaled(t + 1))
                        pool.tensor_tensor(v[0:rows, t, :], v[0:rows, t, :], ln_g[0:rows, :], ALU.mult).then_inc(gained.sem, 1)

                @block.scalar
                def _(act):
                    act.wait_ge(*s_turned(1))
                    act.activation(M["conv_in"][:, :, :, :].rearrange("p a t n -> p (a t n)"), ps[:, 6, 0:384], ACT.Copy).then_inc(s_kept.sem, 1)
                    act.wait_ge(*s_turned(2))
                    act.activation(M["n_in"][:, :, :, :].rearrange("p i b h -> p (i b h)"), ps[:, 7, 0:64], ACT.Copy).then_inc(s_kept.sem, 1)
                    act.wait_ge(*w_turned(1))
                    act.activation(w_t[:, :, :].rearrange("p g t -> p (g t)"), ps[:, 0, 0:512], ACT.Copy).then_inc(w_copied.sem, 1)
                    act.wait_ge(*w_turned(2))
                    act.activation(w_dt[:, :, :].rearrange("p g t -> p (g t)"), ps[0:64, 1, 0:256], ACT.Copy).then_inc(w_copied.sem, 1)

                @block.vector
                def _(dve):
                    own = dve_steps
                    dve.memset(mv[:, 8, :], 1.0).then_inc(*own.one())
                    dve.wait_ge(*own.now())
                    for t in range(NTT):
                        rows = 64 if t == 8 else P
                        for i in range(2):
                            dve.bn_stats(stats[0:rows, t, i, :], v[0:rows, t, 512 * i:512 * i + 512]).then_inc(*own.one())
                        dve.wait_ge(*own.now())
                        dve.bn_aggr(mv[0:rows, t, :], stats[0:rows, t, :, :].rearrange("p a b -> p (a b)")).then_inc(stats_done.sem, 1)
                    dve.wait_ge(*rstd_done(1))

                    def scale(t):
                        rows = 64 if t == 8 else P
                        dve.tensor_scalar(v[0:rows, t, :], v[0:rows, t, :], mv[0:rows, t, 0:1], rstd[0:rows, t:t + 1],
                                          ALU.subtract, ALU.mult).then_inc(scaled.sem, 1)

                    def shift(t):
                        rows = 64 if t == 8 else P
                        dve.wait_ge(*gained(t + 1))
                        dve.tensor_tensor(v[0:rows, t, :], v[0:rows, t, :], ln_b[0:rows, :], ALU.add).then_inc(v_ready.sem, 1)

                    def keep(t):
                        for hf in range(2):
                            dve.wait_ge(*mix_unit(2 * t + hf + 1))
                            if t >= 2 and hf == 0:
                                dve.wait_ge(*mix_out[t % 2](16 * (t // 2)))
                            bank = 2 + (2 * t + hf) % 6
                            if t < 8:
                                dve.tensor_tensor(stage[:, t % 2, 4 * hf:4 * hf + 4, :].rearrange("p (g f) t -> p g f t", f=2),
                                                  ps[:, bank, 0:512].rearrange("p (g f t) -> p g f t", g=2, f=2),
                                                  bc(b_s[:, 2 * hf:2 * hf + 2, :], 2, 2), ALU.add).then_inc(mix_kept.sem, 1)
                            else:
                                for g in range(2):
                                    f0 = 4 * hf + 2 * g
                                    ins = dve.tensor_tensor(
                                        stage[:, 0, f0:f0 + 2, 0:64].rearrange("p f (b t) -> p f b t", t=STOK),
                                        ps[:, bank, 128 * g:128 * g + 128].rearrange("p (f b t) -> p f b t", f=2, t=STOK),
                                        bc(bc(b_s[:, 2 * hf + g, 0:STOK], 1, NSEQ), 1, 2), ALU.add)
                                ins.then_inc(mix_kept.sem, 1)

                    scale(0)
                    scale(1)
                    for t in range(NTT):
                        if t + 2 < NTT:
                            scale(t + 2)
                        shift(t)
                        if t >= 1:
                            keep(t - 1)
                    keep(8)

                @block.tensor
                def _(pe):
                    pe.wait_ge(*states_in(32))
                    for j in range(16):
                        ins = pe.transpose(ps[:, 6, 24 * j:24 * j + 24], crow[:, 128 * j:128 * j + 128], ident[0:24, 0:24])
                    ins.then_inc(s_turned.sem, 1)
                    for i in range(2):
                        ins = pe.transpose(ps[:, 7, 32 * i:32 * i + 32], nrow[:, 128 * i:128 * i + 128], ident[0:32, 0:32])
                    ins.then_inc(s_turned.sem, 1)
                    pe.wait_ge(*w_in_(32))
                    for g in range(H):
                        ins = pe.transpose(ps[:, 0, 128 * g:128 * g + 128], w_rows[:, g, :], ident[:, :])
                    ins.then_inc(w_turned.sem, 1)
                    pe.wait_ge(*diag_in(16 * NSEQ))
                    for g in range(H):
                        ins = pe.transpose(ps[0:64, 1, 64 * g:64 * g + 64], w_diag[:, g, :], ident[0:64, 0:64])
                    ins.then_inc(w_turned.sem, 1)
                    pe.wait_ge(*w_masked(2))
                    pe.wait_ge(*s_kept(2))
                    for t in range(NTT):
                        rows = 64 if t == 8 else P
                        pe.wait_ge(*v_ready(t + 1))
                        for hf in range(2):
                            u = 2 * t + hf
                            if u >= 6:
                                pe.wait_ge(*mix_kept(u - 5))
                            w = w_t if t < 8 else w_dt
                            for f in range(4):
                                ft = 4 * hf + f
                                ins = pe.matmul(ps[:, 2 + u % 6, rows * f:rows * f + rows], v[0:rows, t, 128 * ft:128 * ft + 128],
                                                w[:, ft // 2, :], start=True, stop=True)
                            ins.then_inc(mix_unit.sem, 1)

        def heads(M, free, mixed_d):
            ar.at = free
            q = ar.put("q", [P, 2, T], at=None)
            q_at = ar.at - 2 * T * 4
            k_at = ar.at
            kk = ar.put("kk", [P, 2, T])
            mix_hi = ar.put("mix_hi", [P, 2, T], F32R, at=q_at)
            mix_lo = ar.put("mix_lo", [P, 2, T], F32R, at=k_at)
            vx = ar.put("vx", [P, NTT, DH + 1])
            ob = ar.put("ob", [P, 2, T])
            ub = ar.put("ub", [P, 2, T])
            zc_at = ar.at
            ZP, ZS = SEQ + 3, NSEQ * (STOK + 3)
            zc = ar.put("zc", [P, ZP + ZS])
            zc_end = ar.at
            ar.at = zc_at
            ex = ar.put("ex", [P, P])
            st = ar.put("s_t", [P, P])
            kw = ar.put("kw", [P, DH])
            inter = ar.put("inter", [P, DH + 1])
            ar.at = max(ar.at, zc_end)
            num = ar.put("num", [P, DH + 1])
            tmp = ar.put("gate_tmp", [P, 2, 384])
            C = ar.put("C", [P, 2, DH + 1])
            cs = ar.put("cs", [P, 2, 2, DH + 1])
            kws = ar.put("kws", [64, DH])
            inter_s = ar.put("inter_s", [64, DH + 1])
            vb = ar.put("vb", [64, DH + 1])
            otmp = ar.put("otmp", [P, 4, NSEQ, STOK])
            cw = ar.put("cw", [P, CW, 2, 2])
            cb = ar.put("cb", [P, 2, 2])
            ng = ar.put("ng", [P, 2])
            pads = ar.put("pads", [P, 2, 2, 24])
            tk = ar.put("tk", [P, NTT, 4])
            sel = ar.put("sel", [H, P])
            ap_ = ar.put("ap_", [P, 16])
            hn0 = ar.put("hn0", [P, 2, NSEQ])
            w_mask = ar.put("w_mask", [64, NSEQ])
            den = ar.put("den", [P, 2])
            hst = ar.put("hst", [P, 6])
            hmv = ar.put("hmv", [P, 2])
            var = ar.put("var", [P, 2])
            x_added = ffn_counts["x_added"]
            names = ("hi", "lo", "qk_unit", "zc_kept", "conv", "qk_ready", "vm_unit", "vm_kept", "step_unit",
                     "step_act", "step_mul", "mix_sum", "mix_hi", "mix_lo", "out_unit", "staged", "ap_mm", "ap_kept", "kT", "kw_done",
                     "s0", "e_ready", "e_done", "st_done", "inter_mm", "inter_done", "s1", "b5_read", "c_upd", "var_ready",
                     "rs_ready", "h_ready", "s2", "h_kept", "prep", "seq_mm", "seq_upd", "ub_in", "cp_out", "ones_made", "passed")
            K = {n: cnt("h_" + n) for n in names}
            w_in_ = [cnt("h_w_in0"), cnt("h_w_in1")]
            c_in = [cnt("h_c_in0"), cnt("h_c_in1")]
            c_out = [cnt("h_c_out0"), cnt("h_c_out1")]
            JOBS = [0, 1, 2, 3, "S", 4, 5, 6, 7]
            NJ = len(JOBS)
            EVENTS, unit = [], 0
            for gap in range(3 * NJ):
                EVENTS.append(("stage", gap // 3, gap % 3))
                while unit < (gap + 1) * 24 // (3 * NJ):
                    EVENTS.append(("unit", unit, None))
                    unit += 1

            def place(p):
                c = JOBS[p]
                return (False, None, SEQ, 64, 8) if c == "S" else (True, c, c * CHUNK, CHUNK, c)

            def seq_at(p, stage):
                return 2 * p + stage // 2 if p < 4 and stage != 1 else None

            def zc_out(n, w):
                t0 = UNITS[n][0]
                return zc[:, 3 + t0:3 + t0 + w]

            zs = zc[:, ZP:ZP + ZS].rearrange("p (b t) -> p b t", t=STOK + 3)

            with nc.Block() as block:
                @block.sync
                def _(sp):
                    DOWN = I["w_out"][0].rearrange("(h k p) n -> p h k n", k=2, p=P)

                    def load(h, pair):
                        dst = M["w_raw"][pair % 2]
                        sp.sem_inc(K["passed"].sem, 1)
                        if pair == 7:
                            src = DOWN[:, bass.ds(h, 1), :, :].squeeze(1)
                            sp.dma_start(dst[:, :].rearrange("p (k n) -> p k n", k=2), src).then_inc(w_in_[1].sem, 16)
                            return
                        col = (Q_COLS, K_COLS, VM_COLS, GB_COLS, O_COLS, GA_COLS, GELU_COLS)[pair]
                        sp.dma_start(dst[:, :].rearrange("p (k n) -> p k n", k=KT),
                                     w_d[:, :, bass.ds(h * 256 + col, 256)]).then_inc(w_in_[pair % 2].sem, 16)

                    def load_state(h, b):
                        src = I["state_mlstm_C"][0, b].rearrange("h (i p) e -> p h i e", p=P)[:, bass.ds(h, 1), :, :].squeeze(1)
                        sp.dma_start(cs[:, b % 2, :, 0:DH], src).then_inc(c_in[b % 2].sem, 16)

                    def body(h, last):
                        sp.wait_ge(*x_added(h * 24))
                        sp.dma_start(ub[:, :, :], mixed_d.rearrange("(h i p) t -> p h i t", i=2, p=P)[:, bass.ds(h, 1), :, :]
                                     .squeeze(1)).then_inc(K["ub_in"].sem, 16)
                        load_state(h, 0)
                        load_state(h, 1)
                        for pair in range(3):
                            sp.wait_ge(*(K["qk_unit"](h * 12 + 6 * pair + 6) if pair < 2 else K["vm_unit"](h * NTT + NTT)))
                            load(h, pair + 2)
                        for kind, a, stage in EVENTS:
                            if kind == "stage" and seq_at(a, stage) is not None:
                                b = seq_at(a, stage)
                                sp.wait_ge(*K["seq_upd"](h * 8 + b + 1))
                                dst = O["C_sample"][0, b].rearrange("h (i p) e -> p h i e", p=P)[:, bass.ds(h, 1), :, :].squeeze(1)
                                sp.dma_start(dst, cs[:, b % 2, :, 0:DH]).then_inc(c_out[b % 2].sem, 16)
                                if b + 2 < NSEQ:
                                    sp.wait_ge(*c_out[b % 2](h * 64 + 16 * (b // 2 + 1)))
                                    load_state(h, b + 2)
                            if kind == "unit" and a % 6 == 5:
                                pair = 3 + a // 6
                                sp.wait_ge(*K["step_unit"](h * 24 + a + 1))
                                if pair < 6:
                                    load(h, pair + 2)
                                elif not last:
                                    load(h + 1, 0)
                        for s in range(2):
                            sp.wait_ge(*c_out[s](h * 64 + 64))
                        sp.wait_ge(*K["c_upd"](h * 8 + 8))
                        dst = O["C_prompt"][0, 0].rearrange("h (i p) e -> p h i e", p=P)[:, bass.ds(h, 1), :, :].squeeze(1)
                        sp.dma_start(dst, C[:, :, 0:DH]).then_inc(K["cp_out"].sem, 16)
                        sp.wait_ge(*K["cp_out"](h * 16 + 16))
                        if not last:
                            sp.wait_ge(*K["out_unit"](h * 24 + 24))
                            load(h + 1, 1)

                    load(0, 0)
                    load(0, 1)
                    with sp.Fori(0, H - 1) as h:
                        body(h, False)
                    body(H - 1, True)

                @block.gpsimd
                def _(pool):
                    own = pool_steps
                    pool.memset(vx[:, :, DH:DH + 1], 1.0).then_inc(K["ones_made"].sem, 1)
                    with pool.Fori(0, H) as h:
                        own.enter(h, NJ)
                        for p in range(NJ):
                            rows = place(p)[3]
                            pool.wait_ge(*K["var_ready"](h * NJ + p + 1))
                            pool.sem_inc(K["passed"].sem, 1)
                            pool.tensor_scalar(var[0:rows, 1:2], var[0:rows, 0:1], EPS, None, ALU.add).then_inc(*own.one())
                            pool.wait_ge(*own.now())
                            pool.tensor_tensor(var[0:rows, 1:2], var[0:rows, 1:2], M["half"][0:rows, 0:1], ALU.pow
                                               ).then_inc(K["rs_ready"].sem, 1)
                        own.leave(H)

                @block.scalar
                def _(act):
                    def split(h, j):
                        pair, i = j // 2, j % 2
                        if i == 0:
                            act.wait_ge(*w_in_[pair % 2](h * 64 + 16 * (pair // 2) + 16))
                        rows = pair == 7
                        act.activation(pair_part(M, "hi", pair % 2, i, rows), pair_part(M, "raw", pair % 2, i, rows),
                                       ACT.Copy).then_inc(K["hi"].sem, 1)

                    def silu(h, j):
                        act.wait_ge(*K["conv"](h * 4 + j + 1))
                        t = (q, kk)[j // 2][:, j % 2, :]
                        act.activation(t, t, ACT.Silu).then_inc(K["qk_ready"].sem, 1)

                    def unit(h, u):
                        tile, n = divmod(u, 3)
                        t0, w = UNITS[n]
                        i = tile % 2
                        act.wait_ge(*K["step_unit"](h * 24 + u + 1))
                        if tile < 2:
                            dst = ob[:, i, t0:t0 + w]
                        else:
                            dst = tmp[:, u % 2, 0:w]
                            if u >= 8:
                                act.wait_ge(*K["step_mul"](h * 18 + u - 7))
                        f = ACT.Gelu_apprx_tanh if tile >= 6 else ACT.Sigmoid
                        act.activation(dst, ps[:, u % 3, 0:w], f).then_inc(K["step_act"].sem, 1)

                    def stage0(h, p):
                        chunk, c, t0, L, tt = place(p)
                        if chunk:
                            act.wait_ge(*K["kT"](h * NJ + c + 2))
                            if p:
                                act.wait_ge(*K["s1"](h * NJ + p))
                            act.activation(kw[:, :], ps[:, 4, 0:DH], ACT.Copy, scale=tk[:, tt, 1:2]).then_inc(K["kw_done"].sem, 1)
                        act.wait_ge(*K["e_ready"](h * NJ + p + 1))
                        act.activation(ex[0:L, 0:L], ex[0:L, 0:L], ACT.Exp, bias=tk[0:L, tt, 0:1]).then_inc(K["e_done"].sem, 1)

                    def stage1(h, p):
                        chunk, c, t0, L, tt = place(p)
                        if chunk:
                            act.wait_ge(*K["inter_mm"](h * 8 + c + 1))
                            act.activation(inter[:, :], ps[:, 4, 0:DH + 1], ACT.Copy, scale=tk[:, tt, 2:3]
                                           ).then_inc(K["inter_done"].sem, 1)

                    def stage2(h, p):
                        chunk, c, t0, L, tt = place(p)
                        act.wait_ge(*K["s2"](h * NJ + p + 1))
                        for i in range(2):
                            ins = act.activation(q[:, i, t0:t0 + L], ps[:, 4, 128 * i:128 * i + L], ACT.Copy, scale=ng[:, i:i + 1])
                        ins.then_inc(K["h_kept"].sem, 1)

                    with act.Fori(0, H) as h:
                        split(h, 0)
                        split(h, 1)
                        for j in range(4):
                            for n, (t0, w) in enumerate(UNITS):
                                act.wait_ge(*K["qk_unit"](h * 12 + 3 * j + n + 1))
                                if n == 0 and j:
                                    act.wait_ge(*K["conv"](h * 4 + j))
                                if n < 2:
                                    act.activation(zc_out(n, w), ps[:, n, 0:w], ACT.Copy).then_inc(K["zc_kept"].sem, 1)
                                else:
                                    act.activation(zc_out(n, TAIL_P), ps[:, n, 0:TAIL_P], ACT.Copy)
                                    act.activation(zs[:, :, 3:3 + STOK], ps[:, n, TAIL_P:w].rearrange("p (b t) -> p b t", t=STOK),
                                                   ACT.Copy).then_inc(K["zc_kept"].sem, 1)
                                if n == 0:
                                    split(h, j + 2)
                                if n == 1 and j:
                                    silu(h, j - 1)
                        for t in range(NTT):
                            rows, r0 = (64, 64) if t == 8 else (P, 0)
                            act.wait_ge(*K["vm_unit"](h * NTT + t + 1))
                            act.activation(vx[0:rows, t, 0:DH], ps[r0:r0 + rows, t % 3, 0:DH], ACT.Copy).then_inc(K["vm_kept"].sem, 1)
                            if t == 1:
                                silu(h, 3)
                            if t in (3, 4):
                                split(h, t + 3)
                        act.wait_ge(*K["kT"](h * NJ + 1))
                        act.activation(kws[:, :], ps[0:64, 4, 0:DH], ACT.Copy, scale=tk[0:64, 8, 1:2]).then_inc(K["kw_done"].sem, 1)
                        for kind, a, s in EVENTS:
                            if kind == "stage":
                                (stage0, stage1, stage2)[s](h, a)
                            else:
                                unit(h, a)
                                if a % 3 == 1:
                                    split(h, a // 3 + 8)
                        for n in range(3):
                            t0, w = UNITS[n]
                            for i in range(2):
                                act.wait_ge(*K["mix_sum"](h * 6 + 2 * n + i + 1))
                                act.activation(mix_hi[:, i, t0:t0 + w], ub[:, i, t0:t0 + w], ACT.Copy).then_inc(K["mix_hi"].sem, 1)

                @block.vector
                def _(dve):
                    own = dve_steps

                    def link(ins):
                        ins.then_inc(*own.one())
                        dve.wait_ge(*own.now())

                    def split(h, j):
                        pair, i = j // 2, j % 2
                        rows = pair == 7
                        dve.wait_ge(*K["hi"](h * 16 + j + 1))
                        dve.tensor_tensor(pair_part(M, "lo", pair % 2, i, rows), pair_part(M, "raw", pair % 2, i, rows),
                                          pair_part(M, "hi", pair % 2, i, rows).bitcast(F32), ALU.subtract).then_inc(K["lo"].sem, 1)

                    def stage_head(h):
                        cwv = vT[:, V_CW:V_CW + 64].rearrange("p (j a t) -> p (j a) t", j=CW, a=2)
                        dve.tensor_copy(cw[:, :, :, :].rearrange("p j a i -> p (j a) i"), cwv[:, :, bass.ds(h * 2, 2)]).then_inc(*own.one())
                        dve.tensor_copy(cb[:, :, :], vT[:, V_CB:V_CB + 16].rearrange("p (a t) -> p a t", a=2)[:, :, bass.ds(h * 2, 2)]).then_inc(*own.one())
                        dve.tensor_copy(ng[:, :], vT[:, V_NORM:V_NORM + 8][:, bass.ds(h * 2, 2)]).then_inc(*own.one())
                        dve.tensor_copy(pads[:, :, :, :], M["conv_in"][:, :, bass.ds(h * 2, 2), :]).then_inc(*own.one())
                        dve.tensor_copy(tk[:, 0:8, :], M["tok"][:, 0:8, :, bass.ds(h, 1)].squeeze(3)).then_inc(*own.one())
                        dve.tensor_copy(tk[0:64, 8, :], M["tok"][0:64, 8, :, bass.ds(h, 1)].squeeze(2)).then_inc(*own.one())
                        dve.tensor_copy(sel[:, :], ident[0:H, bass.ds(h, 1)].broadcast_to([H, P])).then_inc(*own.one())
                        dve.tensor_copy(hn0[:, :, :], M["n_in"][:, :, :, bass.ds(h, 1)].squeeze(3)).then_inc(*own.one())
                        dve.memset(C[:, :, :], 0.0).then_inc(*own.one())
                        dve.wait_ge(*own.now())
                        dve.tensor_scalar(w_mask[:, :], M["seq_mask"][:, :], tk[0:64, 8, 2:3], None, ALU.mult).then_inc(K["staged"].sem, 1)

                    def conv(h, j):
                        a, i = divmod(j, 2)
                        dst = (q, kk)[a]
                        dve.tensor_copy(zs[:, :, 0:3], pads[:, a, i, :].rearrange("p (b t) -> p b t", t=3)).then_inc(*own.one())
                        link(dve.memset(zc[:, 0:3], 0.0))
                        dve.wait_ge(*K["zc_kept"](h * 12 + 3 * j + 3))
                        ds = dst[:, i, SEQ:T].rearrange("p (b t) -> p b t", t=STOK)
                        tails = M["tails"][:, bass.ds(h * 2 + (8 * a + i), 1), :].squeeze(1)
                        dve.tensor_copy(tails[:, 0:3], zc[:, SEQ:SEQ + 3]).then_inc(*own.one())
                        dve.tensor_copy(tails[:, 3:27].rearrange("p (b t) -> p b t", t=3), zs[:, :, STOK:STOK + 3]).then_inc(*own.one())
                        for w in range(CW):
                            for out, src in ((dst[:, i, 0:SEQ], zc[:, w:w + SEQ]), (ds, zs[:, :, w:w + STOK])):
                                if w == 0:
                                    ins = dve.tensor_scalar(out, src, cw[:, 0, a, i:i + 1], cb[:, a, i:i + 1], ALU.mult, ALU.add)
                                else:
                                    ins = dve.scalar_tensor_tensor(out=out, in0=src, scalar=cw[:, w, a, i:i + 1], in1=out,
                                                                   op0=ALU.mult, op1=ALU.add)
                                if w == CW - 1 and out is ds:
                                    ins.then_inc(K["conv"].sem, 1)
                                else:
                                    ins.then_inc(*own.one())
                            if w < CW - 1:
                                dve.wait_ge(*own.now())

                    def prep(h, b):
                        dve.tensor_copy(cs[:, b % 2, :, DH:DH + 1], hn0[:, :, b:b + 1]).then_inc(*own.one())
                        dve.tensor_scalar(vb[:, :], vx[0:64, 8, :], M["seq_mask"][:, b:b + 1], None, ALU.mult).then_inc(K["prep"].sem, 1)

                    def sequence(h, b):
                        dve.wait_ge(*K["seq_mm"](h * 8 + b + 1))
                        if b == 0:
                            dve.tensor_scalar(inter_s[:, :], ps[0:64, 7, 0:DH + 1], w_mask[:, 0:1], None, ALU.mult).then_inc(*own.one())
                        else:
                            dve.scalar_tensor_tensor(out=inter_s[:, :], in0=ps[0:64, 7, 0:DH + 1], scalar=w_mask[:, b:b + 1],
                                                     in1=inter_s[:, :], op0=ALU.mult, op1=ALU.add).then_inc(*own.one())
                        s = b % 2
                        dve.scalar_tensor_tensor(out=cs[:, s, :, DH:DH + 1], in0=cs[:, s, :, DH:DH + 1], scalar=ap_[:, 8 + b:9 + b],
                                                 in1=ps[:, 3, 300:302].unsqueeze(2), op0=ALU.mult, op1=ALU.add).then_inc(*own.one())
                        dve.scalar_tensor_tensor(out=cs[:, s, :, 0:DH], in0=cs[:, s, :, 0:DH], scalar=ap_[:, 8 + b:9 + b],
                                                 in1=ps[:, 6, 0:512].rearrange("p (i e) -> p i e", i=2), op0=ALU.mult,
                                                 op1=ALU.add).then_inc(K["seq_upd"].sem, 1)
                        dve.wait_ge(*own.now())
                        dve.tensor_copy(M["n_out"][:, :, b, bass.ds(h, 1)], cs[:, s, :, DH:DH + 1]).then_inc(*own.one())
                        if b + 1 < NSEQ:
                            prep(h, b + 1)

                    def stage0(h, p):
                        chunk, c, t0, L, tt = place(p)
                        dve.wait_ge(*K["s0"](h * NJ + p + 1))
                        mask = M["neg_mask"] if chunk else M["neg_diag"]
                        dve.tensor_tensor(ex[0:L, 0:L], mask[:, :], ps[0:L, 3, 128:128 + L], ALU.subtract).then_inc(K["e_ready"].sem, 1)
                        b = seq_at(p, 0)
                        if b is not None:
                            sequence(h, b)
                        dve.wait_ge(*K["e_done"](h * NJ + p + 1))
                        dve.scalar_tensor_tensor(out=st[0:L, 0:L], in0=ps[0:L, 3, 0:L], scalar=1.0 / 16, in1=ex[0:L, 0:L],
                                                 op0=ALU.mult, op1=ALU.mult).then_inc(K["st_done"].sem, 1)

                    def stage1(h, p):
                        chunk, c, t0, L, tt = place(p)
                        dve.wait_ge(*K["s1"](h * NJ + p + 1))
                        if chunk:
                            dve.wait_ge(*K["inter_done"](h * 8 + c + 1))
                        if p:
                            dve.wait_ge(*K["s2"](h * NJ + p))
                        src = inter if chunk else inter_s
                        ins = dve.tensor_tensor(num[0:L, :], src[0:L, :], ps[0:L, 5, 0:DH + 1], ALU.add)
                        if chunk:
                            ins.then_inc(*own.one())
                            dve.scalar_tensor_tensor(out=C[:, :, DH:DH + 1], in0=C[:, :, DH:DH + 1], scalar=ap_[:, c:c + 1],
                                                     in1=ps[:, 5, 300:302].unsqueeze(2), op0=ALU.mult, op1=ALU.add
                                                     ).then_inc(K["b5_read"].sem, 1)
                            dve.scalar_tensor_tensor(out=C[:, :, 0:DH], in0=C[:, :, 0:DH], scalar=ap_[:, c:c + 1],
                                                     in1=ps[:, 6, 0:512].rearrange("p (i e) -> p i e", i=2), op0=ALU.mult,
                                                     op1=ALU.add).then_inc(K["c_upd"].sem, 1)
                            dve.wait_ge(*own.now())
                        else:
                            ins.then_inc(K["b5_read"].sem, 1)
                            dve.wait_ge(*K["b5_read"](h * NJ + p + 1))
                        dve.tensor_scalar(den[0:L, 0:1], num[0:L, DH:DH + 1], -1.0, tk[0:L, tt, 3:4], ALU.mult, ALU.max
                                          ).then_inc(*own.one())
                        link(dve.bn_stats(hst[0:L, :], num[0:L, 0:DH]))
                        link(dve.tensor_scalar(den[0:L, 0:1], den[0:L, 0:1], num[0:L, DH:DH + 1], None, ALU.max))
                        dve.reciprocal(den[0:L, 1:2], den[0:L, 0:1]).then_inc(*own.one())
                        link(dve.bn_aggr(hmv[0:L, :], hst[0:L, :]))
                        dve.tensor_scalar(var[0:L, 0:1], hmv[0:L, 1:2], den[0:L, 1:2], den[0:L, 1:2], ALU.mult, ALU.mult
                                          ).then_inc(K["var_ready"].sem, 1)
                        dve.wait_ge(*K["rs_ready"](h * NJ + p + 1))
                        link(dve.tensor_scalar(den[0:L, 0:1], var[0:L, 1:2], den[0:L, 1:2], None, ALU.mult))
                        dve.tensor_scalar(num[0:L, 0:DH], num[0:L, 0:DH], hmv[0:L, 0:1], den[0:L, 0:1], ALU.subtract, ALU.mult
                                          ).then_inc(K["h_ready"].sem, 1)

                    def stage2(h, p):
                        b = seq_at(p, 2)
                        if b is not None:
                            sequence(h, b)

                    def unit(h, u):
                        tile, n = divmod(u, 3)
                        t0, w = UNITS[n]
                        i = tile % 2
                        if tile < 2:
                            return
                        dst = (ob, ub)[tile >= 4][:, i, t0:t0 + w]
                        dve.wait_ge(*K["step_act"](h * 24 + u + 1))
                        if u == 12:
                            dve.wait_ge(*K["ub_in"](h * 16 + 16))
                        dve.tensor_tensor(dst, dst, tmp[:, u % 2, 0:w], ALU.mult).then_inc(K["step_mul"].sem, 1)

                    dve.wait_ge(*K["ones_made"](1))
                    with dve.Fori(0, H) as h:
                        own.enter(h, HEAD_STEPS)
                        split(h, 0)
                        split(h, 1)
                        stage_head(h)
                        for j in range(4):
                            split(h, j + 2)
                            conv(h, j)
                        dve.wait_ge(*K["vm_kept"](h * NTT + 4))
                        split(h, 6)
                        split(h, 7)
                        dve.wait_ge(*K["ap_mm"](h + 1))
                        dve.tensor_copy(ap_[:, :], ps[:, 3, 0:16]).then_inc(K["ap_kept"].sem, 1)
                        dve.wait_ge(*K["ap_kept"](h + 1))
                        dve.wait_ge(*K["vm_kept"](h * NTT + NTT))
                        prep(h, 0)
                        for kind, a, s in EVENTS:
                            if kind == "stage":
                                (stage0, stage1, stage2)[s](h, a)
                            else:
                                unit(h, a)
                                if a % 3 == 1:
                                    split(h, a // 3 + 8)
                        dve.wait_ge(*K["h_kept"](h * NJ + NJ))
                        dve.tensor_copy(M["np_out"][:, :, bass.ds(h, 1)], C[:, :, DH:DH + 1]).then_inc(*own.one())

                        def low(j):
                            n, i = divmod(j, 2)
                            t0, w = UNITS[n]
                            dve.wait_ge(*K["mix_hi"](h * 6 + j + 1))
                            dve.tensor_tensor(mix_lo[:, i, t0:t0 + w], ub[:, i, t0:t0 + w], mix_hi[:, i, t0:t0 + w].bitcast(F32),
                                              ALU.subtract).then_inc(K["mix_lo"].sem, 1)

                        for j in range(6):
                            n, i = divmod(j, 2)
                            t0, w = UNITS[n]
                            dve.wait_ge(*K["step_mul"](h * 18 + 18))
                            link(dve.tensor_tensor(ob[:, i, t0:t0 + w], ob[:, i, t0:t0 + w], q[:, i, t0:t0 + w], ALU.mult))
                            dve.tensor_tensor(ub[:, i, t0:t0 + w], ub[:, i, t0:t0 + w], ob[:, i, t0:t0 + w], ALU.add
                                              ).then_inc(K["mix_sum"].sem, 1)
                            if j:
                                low(j - 1)
                        low(5)
                        for u, (m, n) in enumerate(OUT_ORDER):
                            dve.wait_ge(*K["out_unit"](h * 24 + u + 1))
                            add_out(dve, own, m, n, u % 6, otmp[:, m % 4, :, :], x_added)
                        dve.wait_ge(*K["cp_out"](h * 16 + 16))
                        own.leave(H)

                @block.tensor
                def _(pe):
                    def operands(pair, i, t0, w):
                        wh, wl = (pair_part(M, kd, pair % 2, i) for kd in ("hi", "lo"))
                        return [(wh[:, k, :], wl[:, k, :], hhi[:, k, t0:t0 + w], hlo[:, k, t0:t0 + w]) for k in range(KT)]

                    def sequence(h, p, stage):
                        b = seq_at(p, stage)
                        if b is None:
                            return
                        s = b % 2
                        if stage == 2:
                            pe.wait_ge(*K["st_done"](h * NJ + p + 1))
                            pe.wait_ge(*K["seq_upd"](h * 8 + b))
                            state_n(h, b)
                        pe.wait_ge(*c_in[s](h * 64 + 16 * (b // 2 + 1)))
                        if b:
                            pe.wait_ge(*K["seq_upd"](h * 8 + b))
                        if stage == 0 and p:
                            pe.wait_ge(*K["c_upd"](h * 8 + p))
                        if stage == 2:
                            pe.wait_ge(*K["c_upd"](h * 8 + p + 1))
                        for i in range(2):
                            pe.matmul(ps[0:64, 7, 0:DH + 1], q[:, i, SEQ:T], cs[:, s, i, :], start=(i == 0), stop=(i == 1))
                        for i in range(2):
                            ins = pe.matmul(ps[:, 6, 256 * i:256 * i + 256], kws[:, 128 * i:128 * i + 128], vb[:, 0:DH],
                                            start=True, stop=True)
                        ins.then_inc(K["seq_mm"].sem, 1)

                    def state_n(h, b):
                        pe.wait_ge(*K["prep"](h * 8 + b + 1))
                        pe.wait_ge(*K["kw_done"](h * NJ + 1))
                        for i in range(2):
                            ins = pe.matmul(ps[:, 3, 300 + i:301 + i], kws[:, 128 * i:128 * i + 128], vb[:, DH:DH + 1],
                                            start=True, stop=True)
                        return ins

                    def stage0(h, p):
                        chunk, c, t0, L, tt = place(p)
                        if chunk:
                            if p:
                                pe.wait_ge(*K["h_kept"](h * NJ + p))
                            else:
                                pe.wait_ge(*K["kw_done"](h * NJ + 1))
                            for i in range(2):
                                ins = pe.transpose(ps[:, 4, 128 * i:128 * i + 128], kk[:, i, t0:t0 + L], ident[:, :])
                            ins.then_inc(K["kT"].sem, 1)
                        if p:
                            pe.wait_ge(*K["st_done"](h * NJ + p))
                            if p <= 4:
                                pe.wait_ge(*K["seq_upd"](h * 8 + 2 * p))
                        else:
                            pe.wait_ge(*K["ap_kept"](h + 1))
                        if not chunk:
                            pe.sem_inc(K["passed"].sem, 1)
                        for i in range(2):
                            pe.matmul(ps[0:L, 3, 0:L], kk[:, i, t0:t0 + L], q[:, i, t0:t0 + L], start=(i == 0), stop=(i == 1))
                        ins = pe.matmul(ps[0:L, 3, 128:128 + L], sel[:, 0:L], M["m_rows"][:, t0:t0 + L], start=True, stop=True)
                        if seq_at(p, 0) is not None:
                            ins = state_n(h, seq_at(p, 0))
                        ins.then_inc(K["s0"].sem, 1)
                        sequence(h, p, 0)

                    def stage1(h, p):
                        chunk, c, t0, L, tt = place(p)
                        if chunk:
                            pe.wait_ge(*K["kw_done"](h * NJ + c + 2))
                            if c:
                                pe.wait_ge(*K["c_upd"](h * 8 + c))
                            for i in range(2):
                                ins = pe.matmul(ps[:, 4, 0:DH + 1], q[:, i, t0:t0 + L], C[:, i, :], start=(i == 0), stop=(i == 1))
                            ins.then_inc(K["inter_mm"].sem, 1)
                        pe.wait_ge(*K["st_done"](h * NJ + p + 1))
                        if p:
                            pe.wait_ge(*K["b5_read"](h * NJ + p))
                        if not chunk:
                            pe.sem_inc(K["passed"].sem, 1)
                        ins = pe.matmul(ps[0:L, 5, 0:DH + 1], st[0:L, 0:L], vx[0:L, tt, :], start=True, stop=True)
                        if chunk:
                            for i in range(2):
                                pe.matmul(ps[:, 5, 300 + i:301 + i], kw[:, 128 * i:128 * i + 128], vx[:, tt, DH:DH + 1],
                                          start=True, stop=True)
                            if p < 4:
                                pe.wait_ge(*K["seq_upd"](h * 8 + 2 * p + 1))
                            for i in range(2):
                                ins = pe.matmul(ps[:, 6, 256 * i:256 * i + 256], kw[:, 128 * i:128 * i + 128], vx[:, tt, 0:DH],
                                                start=True, stop=True)
                        ins.then_inc(K["s1"].sem, 1)

                    def stage2(h, p):
                        chunk, c, t0, L, tt = place(p)
                        pe.wait_ge(*K["h_ready"](h * NJ + p + 1))
                        if chunk:
                            pe.wait_ge(*K["inter_done"](h * 8 + c + 1))
                        else:
                            pe.wait_ge(*K["h_kept"](h * NJ + p))
                        if not chunk:
                            pe.sem_inc(K["passed"].sem, 1)
                        for i in range(2):
                            ins = pe.transpose(ps[:, 4, 128 * i:128 * i + L], num[0:L, 128 * i:128 * i + 128], ident[0:L, 0:L])
                        ins.then_inc(K["s2"].sem, 1)
                        sequence(h, p, 2)

                    def unit(h, u):
                        tile, n = divmod(u, 3)
                        t0, w = UNITS[n]
                        if n == 0:
                            pe.wait_ge(*K["lo"](h * 16 + 6 + tile + 1))
                        if u < 3:
                            pe.wait_ge(*K["vm_kept"](h * NTT + 6 + u + 1))
                        else:
                            pe.wait_ge(*K["step_act"](h * 24 + u - 2))
                        ins = three(pe, ps[:, n, 0:w], operands(3 + tile // 2, tile % 2, t0, w))
                        ins.then_inc(K["step_unit"].sem, 1)

                    with pe.Fori(0, H) as h:
                        pe.wait_ge(*x_added(h * 24))
                        for j in range(4):
                            pe.wait_ge(*K["lo"](h * 16 + j + 1))
                            for n, (t0, w) in enumerate(UNITS):
                                if j:
                                    pe.wait_ge(*K["zc_kept"](h * 12 + 3 * (j - 1) + n + 1))
                                three(pe, ps[:, n, 0:w], operands(j // 2, j % 2, t0, w)).then_inc(K["qk_unit"].sem, 1)
                        pe.wait_ge(*K["lo"](h * 16 + 6))
                        wh, wl = (M["w_" + kd][0][:, :].rearrange("p (k n) -> p k n", k=KT) for kd in ("hi", "lo"))
                        for t in range(NTT):
                            if t < 3:
                                pe.wait_ge(*K["zc_kept"](h * 12 + 9 + t + 1))
                            else:
                                pe.wait_ge(*K["vm_kept"](h * NTT + t - 2))
                            a = 128 * t if t < 8 else T - P
                            three(pe, ps[:, t % 3, 0:DH], [(hhi[:, k, a:a + P], hlo[:, k, a:a + P], wh[:, k, :], wl[:, k, :])
                                                           for k in range(KT)]).then_inc(K["vm_unit"].sem, 1)
                        pe.wait_ge(*K["staged"](h + 1))
                        pe.matmul(ps[:, 3, 0:16], sel[:, :], M["a_prev"][:, :], start=True, stop=True).then_inc(K["ap_mm"].sem, 1)
                        pe.wait_ge(*K["qk_ready"](h * 4 + 4))
                        pe.sem_inc(K["passed"].sem, 1)
                        for i in range(2):
                            ins = pe.transpose(ps[0:64, 4, 128 * i:128 * i + 128], kk[:, i, SEQ:T], ident[:, :])
                        ins.then_inc(K["kT"].sem, 1)
                        pe.wait_ge(*K["vm_kept"](h * NTT + NTT))
                        for kind, a, s in EVENTS:
                            if kind == "stage":
                                (stage0, stage1, stage2)[s](h, a)
                            else:
                                unit(h, a)
                        pe.wait_ge(*K["lo"](h * 16 + 16))
                        for u, (m, n) in enumerate(OUT_ORDER):
                            t0, w = UNITS[n]
                            if u < 3:
                                pe.wait_ge(*K["step_act"](h * 24 + 21 + u + 1))
                            elif u >= 6:
                                pe.wait_ge(*x_added(h * 24 + (u - 5)))
                            if m == 0:
                                pe.wait_ge(*K["mix_lo"](h * 6 + 2 * n + 2))
                            ms = slice(128 * m, 128 * m + 128)
                            three(pe, ps[:, u % 6, 0:w], [(pair_part(M, "hi", 1, i, True)[:, ms], pair_part(M, "lo", 1, i, True)[:, ms],
                                                           mix_hi[:, i, t0:t0 + w], mix_lo[:, i, t0:t0 + w]) for i in range(2)]
                                  ).then_inc(K["out_unit"].sem, 1)
            x_added.base += 24 * H

        def states_out(M, free):
            ar.at = free
            crow = ar.put("conv_rows_out", [27, 2 * D])
            nrow = ar.put("n_rows_out", [NSEQ * H, DH])
            nprow = ar.put("np_rows_out", [H, DH])
            turned, kept, out = cnt("so_turned"), cnt("so_kept"), cnt("so_out")
            sq = Squares([(k, u) for k in range(KT) for u in range(3)])
            with nc.Block() as block:
                @block.scalar
                def _(act):
                    for s in range(3 * KT):
                        sq.square(act, s)

                @block.tensor
                def _(pe):
                    for j in range(16):
                        ins = pe.transpose(ps[0:27, j // 4, 128 * (j % 4):128 * (j % 4) + 128], M["tails"][:, j, :], ident[:, :])
                    ins.then_inc(turned.sem, 1)
                    for i in range(2):
                        pe.transpose(ps[0:32, 4, 128 * i:128 * i + 128], M["n_out"][:, i, :, :].rearrange("p b h -> p (b h)"), ident[:, :])
                        ins = pe.transpose(ps[0:H, 5, 128 * i:128 * i + 128], M["np_out"][:, i, :], ident[:, :])
                    ins.then_inc(turned.sem, 1)

                @block.vector
                def _(dve):
                    dve.wait_ge(*turned(1))
                    for j in range(4):
                        dve.tensor_copy(crow[:, 512 * j:512 * j + 512], ps[0:27, j, :]).then_inc(kept.sem, 1)
                    dve.wait_ge(*turned(2))
                    dve.tensor_copy(nrow[:, :], ps[0:32, 4, 0:DH]).then_inc(kept.sem, 1)
                    dve.tensor_copy(nprow[:, :], ps[0:H, 5, 0:DH]).then_inc(kept.sem, 1)
                    for s in range(3 * KT):
                        sq.add(dve, s)

                @block.sync
                def _(sp):
                    sp.wait_ge(*kept(6))
                    sp.dma_start(O["conv_prompt"][0, 0], crow[0:3, :]).then_inc(out.sem, 16)
                    sp.dma_start(O["conv_sample"].rearrange("l b j c -> (l b j) c"), crow[3:27, :]).then_inc(out.sem, 16)
                    sp.dma_start(O["n_sample"].rearrange("l b h d -> (l b h) d"), nrow[:, :]).then_inc(out.sem, 16)
                    sp.dma_start(O["n_prompt"].rearrange("l b h d -> (l b h) d"), nprow[:, :]).then_inc(out.sem, 16)
                    sp.wait_ge(*out(64))
            sq.close()

        def final_norm(norm):
            ar.at = work
            y = y_out
            row = ar.put("y_row", [P, 4, D])
            turned, kept = cnt("y_turned"), [cnt("y_kept_v"), cnt("y_kept_a")]
            out = [cnt(f"y_out{s}") for s in range(4)]
            with nc.Block() as block:
                @block.tensor
                def _(pe):
                    norm.means(pe)
                    for t in range(NTT):
                        n = 64 if t == 8 else P
                        if t % 3 == 0:
                            pe.wait_ge(*hi_done(KT * (t // 3 + 1)))
                        if t == 8:
                            pe.wait_ge(*hi_done(3 * KT + 1))
                        for hf in range(2):
                            u = 2 * t + hf
                            if t >= 4:
                                pe.wait_ge(*kept[hf](t - 3))
                            for f in range(4):
                                ins = pe.transpose(ps[0:n, u % 8, 128 * f:128 * f + 128], y[:, 4 * hf + f, 128 * t:128 * t + n], ident[:, :])
                            ins.then_inc(turned.sem, 1)

                def keep(eng, hf, t):
                    n = 64 if t == 8 else P
                    eng.wait_ge(*turned(2 * t + hf + 1))
                    if t >= 4:
                        eng.wait_ge(*out[t % 4](16 * (t // 4)))
                    dst, src = row[0:n, t % 4, 512 * hf:512 * hf + 512], ps[0:n, (2 * t + hf) % 8, :]
                    if hf == 0:
                        eng.tensor_copy(dst, src).then_inc(kept[0].sem, 1)
                    else:
                        eng.activation(dst, src, ACT.Copy).then_inc(kept[1].sem, 1)

                @block.vector
                def _(dve):
                    norm.factors(dve)
                    norm.unit(dve, 0)
                    norm.unit(dve, 1)
                    for t in range(3):
                        keep(dve, 0, t)
                    norm.unit(dve, 2)
                    norm.samples(dve)
                    for t in range(3, NTT):
                        keep(dve, 0, t)

                @block.scalar
                def _(act):
                    norm.roots(act)
                    for j in range(3 * KT):
                        norm.high(act, j)
                        if j == 2 * KT - 1:
                            for t in range(3):
                                keep(act, 1, t)
                    norm.high_samples(act)
                    for t in range(3, NTT):
                        keep(act, 1, t)

                @block.sync
                def _(sp):
                    for t in range(NTT):
                        n = 64 if t == 8 else P
                        sp.wait_ge(*kept[0](t + 1))
                        sp.wait_ge(*kept[1](t + 1))
                        dst = O["y_prompt"][0, 128 * t:128 * t + P, :] if t < 8 else O["y_sample"].rearrange("b t d -> (b t) d")
                        sp.dma_start(dst, row[0:n, t % 4, :]).then_inc(out[t % 4].sem, 16)
                    for s in range(4):
                        sp.wait_ge(*out[s](16 * (3 if s == 0 else 2)))
            norm.close()

        bring_in()
        ffn(I["w_ffn1_in"][0], I["w_ffn1_out"][0], Norm(V_FFN1, 0, 8, gate=16, factor=0.5), ada_first=12)
        norm_alone(Norm(V_MIX, 24, 32, gate=40, factor=1.0))
        M, after = mixer_memory()
        ar.at = after
        v = ar.put("v", [P, NTT, D])
        mixed_d = nc.dram_tensor("mixed", [D, T], F32, kind="Internal").ap()
        gates_and_v(M, ar.at, v)
        spatial(M, after + NTT * D * 4, v, mixed_d)
        heads(M, after, mixed_d)
        states_out(M, after)
        ffn(I["w_ffn2_in"][0], I["w_ffn2_out"][0], Norm(V_FFN2, 48, 56, gate=64, factor=0.5))
        final_norm(Norm(V_FINAL, ADA_T, ADA_T + KT, final=True))


def dump(nc, ctx, dbg, t, n):
    s = ctx.enter_context(nc.semaphore("dumped"))
    with nc.Block() as block:
        @block.sync
        def _(sp):
            sp.dma_start(dbg, t[:, :, :]).then_inc(s, 16)
            sp.wait_ge(s, 16)


_INS = ['x_prompt', 'x_sample', 'c_prompt', 'c_sample', 'state_mlstm_C', 'state_mlstm_n', 'state_mlstm_m', 'state_conv',
        'w_ada', 'b_ada', 'g_ffn1', 'w_ffn1_in', 'w_ffn1_out', 'g_mix', 'w_in', 'b_gates', 'conv_w', 'conv_b',
        'gmlp_ln_g', 'gmlp_ln_b', 'gmlp_ws', 'gmlp_bs', 'mlstm_norm_g', 'w_out', 'g_ffn2', 'w_ffn2_in', 'w_ffn2_out',
        'w_ada_final', 'b_ada_final', 'g_final']
_OUTS = [("y_prompt", (1, SEQ, D)), ("y_sample", (NSEQ, STOK, D)), ("C_prompt", (1, 1, H, DH, DH)), ("n_prompt", (1, 1, H, DH)),
         ("m_prompt", (1, 1, H)), ("conv_prompt", (1, 1, CW - 1, 2 * D)), ("C_sample", (1, NSEQ, H, DH, DH)),
         ("n_sample", (1, NSEQ, H, DH)), ("m_sample", (1, NSEQ, H)), ("conv_sample", (1, NSEQ, CW - 1, 2 * D)),
         ("v_sample", (1, NSEQ, STOK, D))]
STOP = 0
DBG = (P, KT, T)


def kernel(**inputs):
    import numpy as _np
    import concourse.bacc as _bacc
    from concourse.bass_utils import run_bass_kernel_spmd as _run

    nc = _bacc.Bacc("TRN2", target_bir_lowering=False, num_devices=1, dynamic_dma_scratch_size=4096)
    arrays = {f"in_{n}": _np.ascontiguousarray(inputs[n]) for n in _INS}
    ins = {n: nc.dram_tensor(f"in_{n}", arrays[f"in_{n}"].shape, F32, kind="ExternalInput").ap() for n in _INS}
    dbg = None
    if STOP:
        dbg = nc.dram_tensor("dbg", DBG, F32, kind="ExternalOutput").ap()
        outs = {}
    else:
        outs = {n: nc.dram_tensor(f"out_{n}", s, F32, kind="ExternalOutput").ap() for n, s in _OUTS}
    layer(nc, dbg, STOP, ins, outs)
    r = _run(nc, [arrays], core_ids=[0])
    if STOP:
        return r.results[0]["dbg"]
    return tuple(r.results[0][f"out_{n}"] for n, _ in _OUTS)
```

```python
from contextlib import ExitStack

import concourse.bass as bass
from concourse import mybir

F32 = mybir.dt.float32
F32R = mybir.dt.float32r
ALU = mybir.AluOpType
ACT = mybir.ActivationFunctionType

P = 128
D = 1024
KT = D // P
SEQ = 1024
NSEQ = 8
STOK = 8
T = SEQ + NSEQ * STOK
UNITS = [(0, 384), (384, 384), (768, T - 768)]
TAIL_P = SEQ - 768
DFF = 2816
FB = DFF // 256
H = 4
DH = 256
CW = 4
CHUNK = 128
NCH = SEQ // CHUNK
NTT = NCH + 1
ADA_T = 9 * KT
ALL_T = ADA_T + 2 * KT
EPS = 1e-6
HEAD_STEPS = 170
BIG = 1.0e30
GELU_COLS, V_COLS, Q_COLS, K_COLS, VM_COLS, O_COLS, GATE_COLS = 0, 1024, 2048, 3072, 4096, 5120, 6144
GA_COLS, GB_COLS = 6152, 7176


class Count:

    def __init__(self, ctx, nc, name):
        self.sem = ctx.enter_context(nc.semaphore(name))
        self.base = 0

    def __call__(self, n):
        return self.sem, n + self.base


class Steps:

    def __init__(self, ctx, nc, name):
        self.sem = ctx.enter_context(nc.semaphore(name))
        self.n = 0
        self.turn = None

    def one(self):
        self.n += 1
        return self.sem, 1

    def now(self):
        if self.turn is None:
            return self.sem, self.n
        return self.sem, self.turn * self.stride + self.n

    def enter(self, turn, stride, first=0):
        self.turn, self.stride, self.start, self.first = turn, stride, self.n, first
        self.n -= first * stride

    def leave(self, turns):
        n = self.n + self.first * self.stride
        assert n - self.start == self.stride, (n - self.start, self.stride)
        self.n = self.start + self.stride * turns
        self.turn = None


class Arena:

    def __init__(self, nc):
        self.nc, self.at, self.end = nc, -(-nc.sbuf_base // 32) * 32, nc.sbuf_usable_end

    def put(self, name, shape, dtype=F32, at=None):
        size = 4
        for s in shape[1:]:
            size *= s
        size = -(-size // 32) * 32
        offset = self.at if at is None else at
        if at is None:
            self.at += size
        assert offset + size <= self.end, (name, offset + size - self.end)
        t = self.nc.alloc_sbuf_tensor_at(name, shape, dtype, offset=offset)
        return t


def bc(ap, axis, n):
    a = ap.unsqueeze(axis)
    shape = list(a.shape)
    shape[axis] = n
    return a.broadcast_to(shape)


def layer(nc, I, O):
    with ExitStack() as ctx:
        ar = Arena(nc)

        def cnt(name):
            return Count(ctx, nc, name)

        ps = ctx.enter_context(nc.psum_tensor("ps", [P, 8, 512], F32))

        xT = ar.put("xT", [P, KT, T])
        hi_at = ar.at
        hhi = ar.put("hhi", [P, KT, T], F32R)
        hlo = ar.put("hlo", [P, KT, T], F32R)
        ada = ar.put("ada", [P, ALL_T, 9])
        ident = ar.put("ident", [P, P])
        mean = ar.put("mean", [P, P])
        eps_col = ar.put("eps_col", [P, 1])
        vT = ar.put("vT", [P, 128])
        gp = ar.put("gp", [P, KT])
        gs = ar.put("gs", [P, KT, NSEQ])
        gate_p = ar.put("gate_p", [P, KT])
        gate_s = ar.put("gate_s", [P, KT, NSEQ])
        V_FFN1, V_MIX, V_FFN2, V_FINAL, V_NORM, V_CB, V_CW, V_LN = 0, 8, 16, 24, 32, 40, 56, 120
        cs_r = ar.put("cs_r", [P, KT, 18], F32R)
        bT = ar.put("bT", [P, ALL_T])
        work = ar.at
        y_out = ar.put("y", [P, KT, T], at=hi_at)
        RINGS = 4
        ar.at = top = ar.end // 32 * 32 - 4 * (RINGS * 384 + T + KT * NSEQ * STOK) - 3 * 8192
        ada_raw = [ar.put("ada_raw0", [P, KT, 256])] + [
            ar.put(f"ada_raw{s}", [P, KT, 256], at=hi_at + 8192 * (s - 1)) for s in range(1, 4)]
        ada_hi = [ar.put("ada_hi0", [P, KT, 256], F32R), ar.put("ada_hi1", [P, KT, 256], F32R, at=hi_at + 3 * 8192),
                  ar.put("ada_hi2", [P, KT, 256], F32R, at=hi_at + 5 * 8192)]
        ada_lo = [ar.put("ada_lo0", [P, KT, 256], F32R), ar.put("ada_lo1", [P, KT, 256], F32R, at=hi_at + 4 * 8192),
                  ar.put("ada_lo2", [P, KT, 256], F32R, at=hi_at + 6 * 8192)]
        norm_at = ar.at
        ring = ar.put("norm_ring", [P, RINGS, 384])
        rr = ar.put("rr", [P, T])
        ada_rows = ar.put("ada_rows", [18, 256], at=ar.at)
        ts = ar.put("norm_samples", [P, KT, NSEQ, STOK])
        ada_in = [cnt(f"ada_in{s}") for s in range(4)]
        ada_hi_done, ada_lo_done, ada_mm, ada_rows_kept, ada_turned, ada_kept, ada_passed = (
            cnt("ada_" + n) for n in ("hi_done", "lo_done", "mm", "rows_kept", "turned", "kept", "passed"))
        squared, squares_added, mean_done, rms_done, t_done, hi_done, lo_done = (
            cnt("norm_" + n) for n in ("squared", "squares_added", "mean_done", "rms_done", "t_done", "hi_done", "lo_done"))
        dve_steps, act_steps, pool_steps = (Steps(ctx, nc, n) for n in ("dve_steps", "act_steps", "pool_steps"))

        class Squares:

            def __init__(self, order):
                self.order, self.add_of, self.before, last = order, [], [], {}
                for k, n in order:
                    if k == 0:
                        self.add_of.append(None)
                        self.before.append(None)
                    else:
                        self.before.append(last.get(n))
                        last[n] = sum(a is not None for a in self.add_of)
                        self.add_of.append(last[n])

            def square(self, act, s):
                k, n = self.order[s]
                t0, w = UNITS[n]
                if k == 0:
                    dst = rr[:, t0:t0 + w]
                else:
                    r = self.add_of[s]
                    if r >= RINGS:
                        act.wait_ge(*squares_added(r - RINGS + 1))
                    dst = ring[:, r % RINGS, 0:w]
                act.activation(dst, xT[:, k, t0:t0 + w], ACT.Square).then_inc(squared.sem, 1)

            def add(self, eng, s):
                k, n = self.order[s]
                if k == 0:
                    return
                t0, w = UNITS[n]
                eng.wait_ge(*squared(s + 1))
                if self.before[s] is not None:
                    eng.wait_ge(*squares_added(self.before[s] + 1))
                eng.tensor_tensor(rr[:, t0:t0 + w], rr[:, t0:t0 + w], ring[:, self.add_of[s] % RINGS, 0:w],
                                  ALU.add).then_inc(squares_added.sem, 1)

            def close(self):
                squared.base += 3 * KT
                squares_added.base += 3 * (KT - 1)

        wa_d = I["w_ada"][0].rearrange("(k p) n -> p k n", p=P)
        wf_d = I["w_ada_final"].rearrange("(k p) n -> p k n", p=P)

        def ada_load(sp, g, slot=0):
            if isinstance(g, int) and g >= ADA_T // 2:
                src = wf_d[:, :, 256 * g - P * ADA_T:256 * g - P * ADA_T + 256]
            else:
                src = wa_d[:, :, bass.ds(g * 256, 256)]
            sp.dma_start(ada_raw[slot][:, :, :], src).then_inc(ada_in[slot].sem, 16)

        def ada_high(act, turn, halves_free, slot=0, half=0):
            act.wait_ge(*ada_in[slot](turn * 16 + 16))
            if halves_free is not None:
                act.wait_ge(*ada_mm(halves_free))
            for i in range(2):
                act.activation(ada_hi[half][:, :, 128 * i:128 * i + 128], ada_raw[slot][:, :, 128 * i:128 * i + 128],
                               ACT.Copy).then_inc(ada_hi_done.sem, 1)

        def ada_low(dve, g, slot=0, half=0):
            for i in range(2):
                c = slice(128 * i, 128 * i + 128)
                dve.wait_ge(*ada_hi_done(g * 2 + (i + 1)))
                dve.tensor_tensor(ada_lo[half][:, :, c], ada_raw[slot][:, :, c], ada_hi[half][:, :, c].bitcast(F32),
                                  ALU.subtract).then_inc(ada_lo_done.sem, 1)

        def ada_product(pe, g, half=0, reused=True):
            pe.wait_ge(*ada_lo_done(g * 2 + 2))
            if reused:
                pe.wait_ge(*ada_rows_kept(g))
            for k in range(KT):
                pe.matmul(ps[0:18, 6, 0:256], cs_r[:, k, :], ada_hi[half][:, k, :], start=(k == 0), stop=False)
                ins = pe.matmul(ps[0:18, 6, 0:256], cs_r[:, k, :], ada_lo[half][:, k, :], start=False, stop=(k == KT - 1))
            ins.then_inc(ada_mm.sem, 1)

        def ada_copy_rows(act, g, reused=True):
            act.wait_ge(*ada_mm(g + 1))
            if reused:
                act.wait_ge(*ada_turned(g))
            act.activation(ada_rows[:, :], ps[0:18, 6, 0:256], ACT.Copy).then_inc(ada_rows_kept.sem, 1)

        def ada_turn(pe, g, reused=True):
            if reused:
                pe.wait_ge(*ada_kept(g))
            pe.wait_ge(*ada_rows_kept(g + 1))
            pe.sem_inc(ada_passed.sem, 1)
            for i in range(2):
                ins = pe.transpose(ps[:, 7, 18 * i:18 * i + 18], ada_rows[:, 128 * i:128 * i + 128], ident[0:18, 0:18])
            ins.then_inc(ada_turned.sem, 1)

        def ada_keep(dve, g):
            dve.wait_ge(*ada_turned(g + 1))
            dst = ada[:, bass.ds(g * 2, 2), :]
            out = ps[:, 7, 0:36].rearrange("p (j s) -> p j s", s=18)
            dve.tensor_tensor(dst, out[:, :, 0:9], bc(bT[:, bass.ds(g * 2, 2)], 2, 9), ALU.add).then_inc(*dve_steps.one())
            dve.wait_ge(*dve_steps.now())
            dve.tensor_tensor(dst, dst, out[:, :, 9:18], ALU.add).then_inc(ada_kept.sem, 1)

        def bring_in():
            ar.at = work
            xtok = ar.put("xtok", [P, NTT, D])
            crow = ar.put("crow", [9, D])
            crow2 = ar.put("crow2", [9, D])
            csT = ar.put("csT", [P, KT, 9])
            brow = ar.put("brow", [ALL_T, P])
            vrow = ar.put("vrow", [128, P])
            assert ar.at <= top
            x_in = [cnt(f"x_in{u}") for u in range(3)]
            c_in, small_in, made, x_turned, x_kept, c_silu, v_turned, v_kept, cs_ready = (
                cnt(n) for n in ("c_in", "small_in", "made", "x_turned", "x_kept", "c_silu", "v_turned", "v_kept", "cs_ready"))
            x_kept_a = cnt("x_kept_a")
            sq = Squares([(k, u) for u in range(3) for k in range(KT)])
            with nc.Block() as block:
                @block.sync
                def _(sp):
                    for u in range(3):
                        for tt in range(3 * u, 3 * u + (3 if u < 2 else 2)):
                            sp.dma_start(xtok[:, tt, :], I["x_prompt"][0, 128 * tt:128 * tt + 128, :]).then_inc(x_in[u].sem, 16)
                    sp.dma_start(xtok[0:64, 8, :], I["x_sample"].rearrange("b t d -> (b t) d")).then_inc(x_in[2].sem, 16)
                    for g in range(12):
                        if g >= 4:
                            sp.wait_ge(*ada_lo_done(2 * (g - 4) + 2))
                        ada_load(sp, g, g % 4)

                @block.scalar
                def _(act):
                    act.dma_start(crow[0:1, :], I["c_prompt"]).then_inc(c_in.sem, 16)
                    act.dma_start(crow[1:9, :], I["c_sample"]).then_inc(c_in.sem, 16)
                    act.dma_start(brow[0:ADA_T, :], I["b_ada"].rearrange("l (t p) -> (l t) p", p=P)).then_inc(small_in.sem, 16)
                    act.dma_start(brow[ADA_T:ALL_T, :], I["b_ada_final"].rearrange("(t p) -> t p", p=P)).then_inc(small_in.sem, 16)
                    for at, n, src in ((V_FFN1, 8, I["g_ffn1"].rearrange("l (t p) -> (l t) p", p=P)),
                                       (V_MIX, 8, I["g_mix"].rearrange("l (t p) -> (l t) p", p=P)),
                                       (V_FFN2, 8, I["g_ffn2"].rearrange("l (t p) -> (l t) p", p=P)),
                                       (V_FINAL, 8, I["g_final"].rearrange("(t p) -> t p", p=P)),
                                       (V_NORM, 8, I["mlstm_norm_g"].rearrange("l (t p) -> (l t) p", p=P)),
                                       (V_CB, 16, I["conv_b"].rearrange("l (t p) -> (l t) p", p=P)),
                                       (V_CW, 64, I["conv_w"].rearrange("l j (t p) -> (l j t) p", p=P)),
                                       (V_LN, 8, I["gmlp_ln_g"].rearrange("l (t p) -> (l t) p", p=P))):
                        act.dma_start(vrow[at:at + n, :], src).then_inc(small_in.sem, 16)
                    act.wait_ge(*c_in(32))
                    act.activation(crow2[:, :], crow[:, :], ACT.Silu).then_inc(c_silu.sem, 1)

                    def high(g):
                        ada_high(act, g // 4, g - 2 if g >= 3 else None, g % 4, g % 3)

                    for u, (t0, n) in enumerate(UNITS):
                        for k in range(1, KT, 2):
                            g = KT * u + k
                            act.wait_ge(*x_turned(g + 1))
                            act.activation(xT[:, k, t0:t0 + n], ps[:, g % 6, 0:n], ACT.Copy).then_inc(x_kept_a.sem, 1)
                        high(u)
                        if u == 0:
                            act.wait_ge(*v_turned(1))
                            act.activation(csT[:, :, :], ps[:, 6, 0:72], ACT.Copy).then_inc(v_kept.sem, 1)
                            act.wait_ge(*v_kept(1))
                            act.activation(cs_r[:, :, 0:9], csT[:, :, :], ACT.Copy).then_inc(v_kept.sem, 1)
                    act.wait_ge(*v_turned(2))
                    act.activation(bT[:, :], ps[:, 7, 0:ALL_T], ACT.Copy).then_inc(v_kept.sem, 1)
                    act.activation(vT[:, :], ps[:, 7, 128:256], ACT.Copy).then_inc(v_kept.sem, 1)
                    act.wait_ge(*x_kept(12))
                    act.wait_ge(*x_kept_a(12))
                    for g in range(12):
                        ada_copy_rows(act, g, reused=g >= 1)
                        if g < 9:
                            high(g + 3)
                        sq.square(act, 2 * g)
                        sq.square(act, 2 * g + 1)

                @block.gpsimd
                def _(pool):
                    pool.memset(ident[:, :], 0.0).then_inc(made.sem, 1)
                    pool.memset(mean[:, :], 1.0 / D).then_inc(made.sem, 1)
                    pool.memset(eps_col[:, :], EPS).then_inc(made.sem, 1)
                    pool.wait_ge(*made(3))
                    pool.affine_select(out=ident[:, :], in_=ident[:, :], compare_op=ALU.not_equal, fill=1.0,
                                       base=0, pattern=[[-1, P]], channel_multiplier=1).then_inc(made.sem, 1)
                    for s in range(3 * KT):
                        sq.add(pool, s)

                @block.vector
                def _(dve):
                    for u, (t0, n) in enumerate(UNITS):
                        for k in range(0, KT, 2):
                            g = KT * u + k
                            dve.wait_ge(*x_turned(g + 1))
                            dve.tensor_copy(xT[:, k, t0:t0 + n], ps[:, g % 6, 0:n]).then_inc(x_kept.sem, 1)
                        ada_low(dve, u, u, u)
                    dve.wait_ge(*v_kept(2))
                    dve.tensor_tensor(cs_r[:, :, 9:18], csT[:, :, :], cs_r[:, :, 0:9].bitcast(F32), ALU.subtract).then_inc(cs_ready.sem, 1)
                    dve.wait_ge(*v_kept(4))
                    for g in range(12):
                        if g < 9:
                            ada_low(dve, g + 3, (g + 3) % 4, g % 3)
                        if g >= 1:
                            ada_keep(dve, g - 1)
                    ada_keep(dve, 11)

                @block.tensor
                def _(pe):
                    pe.wait_ge(*made(4))
                    for g in range(3 * KT):
                        u, k = divmod(g, KT)
                        if g % KT == 0:
                            pe.wait_ge(*x_in[u](48))
                        if g >= 6:
                            e, m = (x_kept, (g - 6) // 2 + 1) if g % 2 == 0 else (x_kept_a, (g - 7) // 2 + 1)
                            pe.wait_ge(*e(m))
                        for c in range(3):
                            tt = 3 * u + c
                            rows = 64 if tt == 8 else P
                            ins = pe.transpose(ps[:, g % 6, 128 * c:128 * c + rows],
                                               xtok[0:rows, tt, 128 * k:128 * k + 128], ident[0:rows, 0:rows])
                        ins.then_inc(x_turned.sem, 1)
                        if g == KT - 1:
                            pe.wait_ge(*c_silu(1))
                            for i in range(KT):
                                ins = pe.transpose(ps[:, 6, 9 * i:9 * i + 9], crow2[:, 128 * i:128 * i + 128], ident[0:9, 0:9])
                            ins.then_inc(v_turned.sem, 1)
                    pe.wait_ge(*small_in(16 * 10))
                    pe.transpose(ps[:, 7, 0:ALL_T], brow[:, :], ident[0:ALL_T, 0:ALL_T])
                    pe.transpose(ps[:, 7, 128:256], vrow[:, :], ident[:, :]).then_inc(v_turned.sem, 1)
                    pe.wait_ge(*cs_ready(1))
                    for g in range(12):
                        ada_product(pe, g, g % 3, reused=g >= 1)
                        if g == 1:
                            pe.wait_ge(*v_kept(4))
                        if g:
                            ada_turn(pe, g - 1, reused=g >= 2)
                    ada_turn(pe, 11)
            sq.close()
            ada_in[0].base += 48

        class Norm:

            def __init__(self, g_at, shift, scale, final=False, gate=None, factor=None):
                self.g_at, self.shift, self.scale, self.final, self.gate, self.factor = g_at, shift, scale, final, gate, factor
                self.dst = y_out if final else hhi

            def means(self, pe):
                for n, (t0, w) in enumerate(UNITS):
                    pe.matmul(ps[:, n, 0:w], mean[:, :], rr[:, t0:t0 + w], start=True, stop=True).then_inc(mean_done.sem, 1)

            def roots(self, act):
                for n, (t0, w) in enumerate(UNITS):
                    act.wait_ge(*mean_done(n + 1))
                    act.activation(rr[:, t0:t0 + w], ps[:, n, 0:w], ACT.Sqrt, bias=eps_col[:, 0:1]).then_inc(rms_done.sem, 1)

            def high(self, act, j):
                n, k = divmod(j, KT)
                t0, w = UNITS[n]
                wp = w if n < 2 else TAIL_P
                act.wait_ge(*t_done(j + 1))
                act.activation(self.dst[:, k, t0:t0 + wp], ring[:, j % RINGS, 0:wp], ACT.Identity,
                               bias=ada[:, self.shift + k, 0:1]).then_inc(hi_done.sem, 1)

            def high_samples(self, act):
                act.wait_ge(*t_done(3 * KT + 1))
                act.activation(self.dst[:, :, SEQ:T], ts[:, :, :, :].rearrange("p k s t -> p k (s t)"),
                               ACT.Copy).then_inc(hi_done.sem, 1)

            def factors(self, dve):
                scale, g_at, gate = self.scale, self.g_at, self.gate
                dve.scalar_tensor_tensor(out=gp[:, :], in0=ada[:, scale:scale + KT, 0], scalar=1.0,
                                         in1=vT[:, g_at:g_at + KT], op0=ALU.add, op1=ALU.mult).then_inc(*dve_steps.one())
                dve.scalar_tensor_tensor(out=gs[:, :, :], in0=ada[:, scale:scale + KT, 1:9], scalar=1.0,
                                         in1=bc(vT[:, g_at:g_at + KT], 2, NSEQ), op0=ALU.add,
                                         op1=ALU.mult).then_inc(*dve_steps.one())

            def gates(self, dve):
                gate = self.gate
                dve.tensor_scalar(gate_p[:, :], ada[:, gate:gate + KT, 0], self.factor, None, ALU.mult).then_inc(*dve_steps.one())
                dve.tensor_scalar(gate_s[:, :, :], ada[:, gate:gate + KT, 1:9], self.factor, None, ALU.mult).then_inc(*dve_steps.one())
                dve.wait_ge(*dve_steps.now())

            def low(self, dve, j):
                if self.final:
                    return
                n, k = divmod(j, KT)
                t0, w = UNITS[n]
                wp = w if n < 2 else TAIL_P
                dve.wait_ge(*hi_done(j + 1))
                dve.scalar_tensor_tensor(out=hlo[:, k, t0:t0 + wp], in0=ring[:, j % RINGS, 0:wp],
                                         scalar=ada[:, self.shift + k, 0:1], in1=hhi[:, k, t0:t0 + wp].bitcast(F32),
                                         op0=ALU.add, op1=ALU.subtract).then_inc(lo_done.sem, 1)

            def unit(self, dve, n, between=None):
                t0, w = UNITS[n]
                wp = w if n < 2 else TAIL_P
                dve.wait_ge(*rms_done(n + 1))
                dve.reciprocal(rr[:, t0:t0 + w], rr[:, t0:t0 + w]).then_inc(*dve_steps.one())
                dve.wait_ge(*dve_steps.now())
                for k in range(KT):
                    j = n * KT + k
                    if j >= RINGS:
                        dve.wait_ge(*(hi_done if self.final else lo_done)(j - RINGS + 1))
                    dve.scalar_tensor_tensor(out=ring[:, j % RINGS, 0:wp], in0=xT[:, k, t0:t0 + wp],
                                             scalar=gp[:, k:k + 1], in1=rr[:, t0:t0 + wp],
                                             op0=ALU.mult, op1=ALU.mult).then_inc(t_done.sem, 1)
                    if k >= 2:
                        self.low(dve, j - 2)
                    if between and k == 3:
                        between()
                self.low(dve, n * KT + KT - 2)
                self.low(dve, n * KT + KT - 1)

            def samples(self, dve):
                shift = self.shift
                xs = xT[:, :, SEQ:T].rearrange("p k (s t) -> p k s t", t=STOK)
                dve.tensor_tensor(ts[:, :, :, :], xs, bc(gs[:, :, :], 3, STOK), ALU.mult).then_inc(*dve_steps.one())
                dve.wait_ge(*dve_steps.now())
                tsf = ts[:, :, :, :].rearrange("p k s t -> p k (s t)")
                dve.tensor_tensor(tsf, tsf, bc(rr[:, SEQ:T], 1, KT), ALU.mult).then_inc(*dve_steps.one())
                dve.wait_ge(*dve_steps.now())
                dve.tensor_tensor(ts[:, :, :, :], ts[:, :, :, :], bc(ada[:, shift:shift + KT, 1:9], 3, STOK),
                                  ALU.add).then_inc(t_done.sem, 1)
                if not self.final:
                    dve.wait_ge(*hi_done(3 * KT + 1))
                    dve.wait_ge(*t_done(3 * KT + 1))
                    dve.tensor_tensor(hlo[:, :, SEQ:T], tsf, hhi[:, :, SEQ:T].bitcast(F32), ALU.subtract).then_inc(lo_done.sem, 1)

            def close(self):
                mean_done.base += 3
                rms_done.base += 3
                t_done.base += 3 * KT + 1
                hi_done.base += 3 * KT + 1
                lo_done.base += 0 if self.final else 3 * KT + 1

        ffn_counts = {n: cnt("ffn_" + n) for n in (
            "a_in", "b_in", "o_in", "a_hi", "b_hi", "o_hi", "a_lo", "b_lo", "o_lo",
            "a_unit", "b_unit", "out_unit", "silu", "hidden", "hid_hi", "hid_lo", "x_added")}
        ffn_mem = {}

        OUT_ORDER = [(0, 0), (0, 1), (1, 0), (1, 1), (0, 2), (1, 2)] + [(m, n) for m in range(2, KT) for n in range(3)]

        def add_out(dve, own, m, n, bank, tmp, x_added):
            t0, w = UNITS[n]
            wp = w if n < 2 else TAIL_P
            ins = dve.scalar_tensor_tensor(out=xT[:, m, t0:t0 + wp], in0=ps[:, bank, 0:wp], scalar=gate_p[:, m:m + 1],
                                           in1=xT[:, m, t0:t0 + wp], op0=ALU.mult, op1=ALU.add)
            if n < 2:
                ins.then_inc(x_added.sem, 1)
                return
            ins.then_inc(*own.one())
            dve.tensor_tensor(tmp, ps[:, bank, TAIL_P:w].rearrange("p (s t) -> p s t", t=STOK),
                              bc(gate_s[:, m, :], 2, STOK), ALU.mult).then_inc(*own.one())
            dve.wait_ge(*own.now())
            xs = xT[:, m, SEQ:T].rearrange("p (s t) -> p s t", t=STOK)
            dve.tensor_tensor(xs, xs, tmp, ALU.add).then_inc(x_added.sem, 1)

        def ffn(w_up, w_down, norm, ada_first=None):
            if not ffn_mem:
                ar.at = work
                for nm in ("a", "b", "o"):
                    ffn_mem[nm + "_raw"] = None
                    ffn_mem[nm + "_hi"] = ar.put(f"w{nm}_hi", [P, 2048], F32R)
                    at = ar.at
                    ffn_mem[nm + "_lo"] = ar.put(f"w{nm}_lo", [P, 2048], F32R)
                    ffn_mem[nm + "_raw"] = ar.put(f"w{nm}_raw", [P, 2048], at=at)
                ffn_mem["g_hi"] = ar.put("g_hi", [P, 2, T], F32R)
                ffn_mem["g_lo"] = ar.put("g_lo", [P, 2, T], F32R)
                ffn_mem["st"] = ar.put("st", [P, 3, 384])
                ffn_mem["hf"] = ar.put("hf", [P, 3, 384])
                ffn_mem["tmp"] = ar.put("ffn_tmp", [P, 4, NSEQ, STOK])
                assert ar.at <= top
            M = ffn_mem
            C = ffn_counts
            sq = Squares(OUT_ORDER)
            ADA_BLOCKS = (ALL_T // 2 - ada_first) // 4 if ada_first else 0

            def group(b, q):
                return b * 4 + (ada_first - 4 + q)
            up_d = w_up.rearrange("(k p) n -> p k n", p=P)
            down_d = w_down.rearrange("(b k p) n -> p b k n", k=2, p=P)

            def part(nm, kind, i):
                t = M[f"{nm}_{kind}"]
                if nm == "o":
                    return t[:, 1024 * i:1024 * i + 1024]
                return t[:, :].rearrange("p (k n) -> p k n", n=256)[:, :, 128 * i:128 * i + 128]

            with nc.Block() as block:
                @block.sync
                def _(sp):
                    def load(nm, b):
                        dst = M[f"{nm}_raw"]
                        if nm == "o":
                            src = down_d[:, b, :, :] if isinstance(b, int) else down_d[:, bass.ds(b, 1), :, :].squeeze(1)
                            sp.dma_start(dst[:, :].rearrange("p (k n) -> p k n", k=2), src).then_inc(C["o_in"].sem, 16)
                        else:
                            off = 0 if nm == "a" else DFF
                            sp.dma_start(dst[:, :].rearrange("p (k n) -> p k n", k=KT),
                                         up_d[:, :, bass.ds(b * 256 + off, 256)]).then_inc(C[nm + "_in"].sem, 16)
                    load("a", 0)
                    load("b", 0)
                    load("o", 0)

                    def body(b, ada_too):
                        sp.wait_ge(*C["a_unit"](b * 6))
                        load("a", b)
                        sp.wait_ge(*C["b_unit"](b * 6))
                        load("b", b)
                        for q in range(4 if ada_too else 0):
                            sp.wait_ge(*ada_lo_done(group(b, q) * 2))
                            ada_load(sp, group(b, q))
                            if q == 0:
                                sp.wait_ge(*C["out_unit"](b * 24))
                                load("o", b)
                        if not ada_too:
                            sp.wait_ge(*C["out_unit"](b * 24))
                            load("o", b)

                    if ada_first:
                        with sp.Fori(1, (ADA_T // 2 - ada_first) // 4 + 1) as b:
                            body(b, True)
                        for b in range((ADA_T // 2 - ada_first) // 4 + 1, FB):
                            body(b, b <= ADA_BLOCKS)
                    else:
                        with sp.Fori(1, FB) as b:
                            body(b, False)

                UP_ORDER = [(i, n) for i in range(2) for n in range(3)]
                FIRST_ORDER = [(0, 0), (1, 0), (0, 1), (1, 1), (0, 2), (1, 2)]
                FIRST_BANKS = {(0, 0): (0, 3, None), (1, 0): (6, 7, None), (0, 1): (1, 4, None), (1, 1): (2, 5, None),
                               (0, 2): (0, 3, 0), (1, 2): (6, 7, 3)}

                def first(b):
                    return isinstance(b, int) and b == 0

                def up_unit(b, i, n):
                    return b * 6 + ((FIRST_ORDER if first(b) else UP_ORDER).index((i, n)) + 1)

                def up_bank(nm, b, i, n):
                    if first(b):
                        return FIRST_BANKS[i, n][0 if nm == "a" else 1]
                    return n if nm == "a" else 3 + n

                def blocks(eng, body, own=None):
                    def loop(first, end, ada_too):
                        with eng.Fori(first, end) as b:
                            if own:
                                own.enter(b, 2 * KT + (4 if ada_too else 0), first=first)
                            body(b, ada_too, False)
                            if own:
                                own.leave(end - first)
                    body(0, False, False)
                    if ada_first:
                        loop(1, ADA_BLOCKS + 1, True)
                        for b in range(ADA_BLOCKS + 1, FB - 1):
                            body(b, False, False)
                    else:
                        loop(1, FB - 1, False)
                    body(FB - 1, False, True)

                @block.scalar
                def _(act):
                    def split(nm, i, b):
                        if i == 0:
                            act.wait_ge(*C[nm + "_in"](b * 16 + 16))
                        act.activation(part(nm, "hi", i), part(nm, "raw", i), ACT.Copy).then_inc(C[nm + "_hi"].sem, 1)

                    def silu(i, n, b):
                        act.wait_ge(*C["a_unit"](up_unit(b, i, n)))
                        if i == 1:
                            act.wait_ge(*C["hidden"](b * 6 + n + 1))
                        w = UNITS[n][1]
                        act.activation(M["st"][:, n, 0:w], ps[:, up_bank("a", b, i, n), 0:w], ACT.Silu).then_inc(C["silu"].sem, 1)

                    def hid(i, n, b):
                        t0, w = UNITS[n]
                        act.wait_ge(*C["hidden"](b * 6 + 3 * i + n + 1))
                        act.activation(M["g_hi"][:, i, t0:t0 + w], M["hf"][:, n, 0:w], ACT.Copy).then_inc(C["hid_hi"].sem, 1)

                    def high(b, q):
                        ada_high(act, (b - 1) * 4 + q, group(b, q))

                    def body(b, ada_too, last):
                        if ada_too:
                            high(b, 0)
                        if not first(b):
                            split("b", 1, b)
                        for n in range(3):
                            silu(0, n, b)
                            hid(0, n, b)
                            if n == 0 and ada_too:
                                ada_copy_rows(act, group(b, 0))
                                high(b, 1)
                            if n > 0 and not first(b):
                                split("o", n - 1, b)
                        if ada_too:
                            ada_copy_rows(act, group(b, 1))
                            high(b, 2)
                        for n in range(3):
                            silu(1, n, b)
                            hid(1, n, b)
                            if n == 0 and first(b):
                                split("o", 0, b)
                                split("o", 1, b)
                            if n == 0 and ada_too:
                                ada_copy_rows(act, group(b, 2))
                                high(b, 3)
                        if ada_too:
                            ada_copy_rows(act, group(b, 3))
                        if not last:
                            split("a", 0, b + 1)
                            split("b", 0, b + 1)
                            split("a", 1, b + 1)
                        else:
                            for u in range(24):
                                act.wait_ge(*C["x_added"](b * 24 + u + 1))
                                sq.square(act, u)

                    norm.roots(act)
                    for j in range(3 * KT):
                        if j == 4:
                            split("a", 0, 0)
                            split("b", 0, 0)
                        if j == KT:
                            split("a", 1, 0)
                            split("b", 1, 0)
                        norm.high(act, j)
                    norm.high_samples(act)
                    blocks(act, body)

                @block.gpsimd
                def _(pool):
                    for u in range(24):
                        sq.add(pool, u)

                @block.vector
                def _(dve):
                    own = dve_steps

                    def split(nm, i, b):
                        dve.wait_ge(*C[nm + "_hi"](b * 2 + i + 1))
                        dve.tensor_tensor(part(nm, "lo", i), part(nm, "raw", i), part(nm, "hi", i).bitcast(F32),
                                          ALU.subtract).then_inc(C[nm + "_lo"].sem, 1)

                    def hidden(i, n, b):
                        w = UNITS[n][1]
                        dve.wait_ge(*C["b_unit"](up_unit(b, i, n)))
                        dve.wait_ge(*C["silu"](b * 6 + 3 * i + n + 1))
                        if i == 1:
                            dve.wait_ge(*C["hid_lo"](b * 6 + n + 1))
                            dve.wait_ge(*C["hid_hi"](b * 6 + n + 1))
                        dve.tensor_tensor(M["hf"][:, n, 0:w], M["st"][:, n, 0:w], ps[:, up_bank("b", b, i, n), 0:w],
                                          ALU.mult).then_inc(C["hidden"].sem, 1)

                    def low(i, n, b):
                        t0, w = UNITS[n]
                        dve.wait_ge(*C["hid_hi"](b * 6 + 3 * i + n + 1))
                        dve.tensor_tensor(M["g_lo"][:, i, t0:t0 + w], M["hf"][:, n, 0:w],
                                          M["g_hi"][:, i, t0:t0 + w].bitcast(F32), ALU.subtract).then_inc(C["hid_lo"].sem, 1)

                    def body(b, ada_too, last):
                        if ada_too:
                            ada_low(dve, group(b, 0))
                        if not first(b):
                            split("b", 1, b)
                        for n in range(3):
                            hidden(0, n, b)
                            low(0, n, b)
                            if n == 0 and ada_too:
                                ada_low(dve, group(b, 1))
                            if n == 1 and ada_too:
                                ada_keep(dve, group(b, 0))
                            if n > 0 and not first(b):
                                split("o", n - 1, b)
                        if ada_too:
                            ada_low(dve, group(b, 2))
                        for n in range(3):
                            hidden(1, n, b)
                            low(1, n, b)
                            if n == 0 and first(b):
                                split("o", 0, b)
                                split("o", 1, b)
                            if n == 0 and ada_too:
                                ada_keep(dve, group(b, 1))
                                ada_low(dve, group(b, 3))
                            if n == 2 and ada_too:
                                ada_keep(dve, group(b, 2))
                        for u, (m, n) in enumerate(OUT_ORDER):
                            dve.wait_ge(*C["out_unit"](b * 24 + u + 1))
                            add_out(dve, own, m, n, u % 6, M["tmp"][:, m % 4, :, :], C["x_added"])
                            if ada_too and u == 4:
                                ada_keep(dve, group(b, 3))
                            if not last and u in (9, 13, 17):
                                split(*{9: ("a", 0), 13: ("b", 0), 17: ("a", 1)}[u], b + 1)

                    norm.factors(dve)
                    norm.unit(dve, 0, between=lambda: split("a", 0, 0))
                    split("b", 0, 0)
                    split("a", 1, 0)
                    split("b", 1, 0)
                    norm.unit(dve, 1)
                    norm.unit(dve, 2)
                    norm.samples(dve)
                    norm.gates(dve)
                    blocks(dve, body, own)

                @block.tensor
                def _(pe):
                    def three(bank, w, pairs):
                        last = len(pairs) - 1
                        for j, (wh, wl, xh, xl) in enumerate(pairs):
                            pe.matmul(ps[:, bank, 0:w], wh, xh, start=(j == 0), stop=False)
                            pe.matmul(ps[:, bank, 0:w], wh, xl, start=False, stop=False)
                            ins = pe.matmul(ps[:, bank, 0:w], wl, xh, start=False, stop=(j == last))
                        return ins

                    def up(nm, i, n, b):
                        t0, w = UNITS[n]
                        bank = up_bank(nm, b, i, n)
                        read = C["silu" if nm == "a" else "hidden"]
                        if first(b):
                            if FIRST_BANKS[i, n][2] is not None:
                                pe.wait_ge(*read(FIRST_BANKS[i, n][2] + 1))
                        elif i == 1:
                            pe.wait_ge(*read(b * 6 + n + 1))
                        else:
                            pe.wait_ge(*C["x_added"](b * 24 - 6 + bank + 1))
                        wh, wl = part(nm, "hi", i), part(nm, "lo", i)
                        for k in range(KT):
                            if first(b) and i == 0 and nm == "a":
                                pe.wait_ge(*lo_done(n * KT + k + 1 if n < 2 or k else 3 * KT + 1))
                            xh, xl = hhi[:, k, t0:t0 + w], hlo[:, k, t0:t0 + w]
                            pe.matmul(ps[:, bank, 0:w], wh[:, k, :], xh, start=(k == 0), stop=False)
                            pe.matmul(ps[:, bank, 0:w], wh[:, k, :], xl, start=False, stop=False)
                            ins = pe.matmul(ps[:, bank, 0:w], wl[:, k, :], xh, start=False, stop=(k == KT - 1))
                        ins.then_inc(C[nm + "_unit"].sem, 1)

                    def body(b, ada_too, last):
                        for i, n in FIRST_ORDER if first(b) else UP_ORDER:
                            if n == 0:
                                pe.wait_ge(*C["a_lo"](b * 2 + i + 1))
                            up("a", i, n, b)
                            if n == 0:
                                pe.wait_ge(*C["b_lo"](b * 2 + i + 1))
                            up("b", i, n, b)
                            if ada_too and (i, n) == (1, 0):
                                ada_turn(pe, group(b, 1))
                            if ada_too and n != 1:
                                ada_product(pe, group(b, 2 * i + n // 2))
                            elif ada_too:
                                ada_turn(pe, group(b, 2 * i))
                        pe.wait_ge(*C["o_lo"](b * 2 + 2))
                        for u, (m, n) in enumerate(OUT_ORDER):
                            t0, w = UNITS[n]
                            if u < 3:
                                pe.wait_ge(*C["silu"](b * 6 + 3 + u + 1))
                            elif u < 6:
                                pe.wait_ge(*C["hidden"](b * 6 + u + 1))
                            else:
                                pe.wait_ge(*C["x_added"](b * 24 + u - 6 + 1))
                            if m == 0:
                                pe.wait_ge(*C["hid_lo"](b * 6 + 3 + n + 1))
                            ms = slice(128 * m, 128 * m + 128)
                            ins = three(u % 6, w, [(part("o", "hi", i)[:, ms], part("o", "lo", i)[:, ms],
                                                    M["g_hi"][:, i, t0:t0 + w], M["g_lo"][:, i, t0:t0 + w])
                                                   for i in range(2)])
                            ins.then_inc(C["out_unit"].sem, 1)
                            if ada_too and u == 2:
                                ada_turn(pe, group(b, 3))

                    norm.means(pe)
                    blocks(pe, body)
            norm.close()
            sq.close()
            if ada_first:
                ada_in[0].base += 16 * 4 * ADA_BLOCKS

            for n, c in C.items():
                c.base += {"a_in": 16, "b_in": 16, "o_in": 16, "a_hi": 2, "b_hi": 2, "o_hi": 2, "a_lo": 2, "b_lo": 2,
                           "o_lo": 2, "a_unit": 6, "b_unit": 6, "out_unit": 24,
                           "silu": 6, "hidden": 6, "hid_hi": 6, "hid_lo": 6, "x_added": 24}[n] * FB

        def mixer_memory():
            ar.at = work
            m = {}
            m["m_rows"] = ar.put("m_rows", [H, T])
            m["tok"] = ar.put("tok", [P, NTT, 4, H])
            m["a_prev"] = ar.put("a_prev", [H, 16])
            m["m_new"] = ar.put("m_new", [H, 16])
            m["conv_in"] = ar.put("conv_in", [P, 2, KT, NSEQ * 3])
            m["n_in"] = ar.put("n_in", [P, 2, NSEQ, H])
            m["tails"] = ar.put("tails", [P, 2 * KT, 27])
            m["n_out"] = ar.put("n_out", [P, 2, NSEQ, H])
            m["np_out"] = ar.put("np_out", [P, 2, H])
            m["neg_mask"] = ar.put("neg_mask", [P, P])
            m["neg_diag"] = ar.put("neg_diag", [64, 64])
            m["seq_mask"] = ar.put("seq_mask", [64, NSEQ])
            m["half"] = ar.put("half", [P, NTT])
            m["w_hi"], m["w_lo"], m["w_raw"] = [], [], []
            m["ring_at"] = ar.at
            for s in range(2):
                m["w_hi"].append(ar.put(f"mw{s}_hi", [P, 2048], F32R))
                at = ar.at
                m["w_lo"].append(ar.put(f"mw{s}_lo", [P, 2048], F32R))
                m["w_raw"].append(ar.put(f"mw{s}_raw", [P, 2048], at=at))
            return m, ar.at

        def pair_part(M, kind, slot, i, rows=False):
            t = M["w_" + kind][slot]
            if rows:
                return t[:, 1024 * i:1024 * i + 1024]
            return t[:, :].rearrange("p (k n) -> p k n", n=256)[:, :, 128 * i:128 * i + 128]

        def three(pe, out, operands):
            last = len(operands) - 1
            for j, (wh, wl, xh, xl) in enumerate(operands):
                pe.matmul(out, wh, xh, start=(j == 0), stop=False)
                pe.matmul(out, wh, xl, start=False, stop=False)
                ins = pe.matmul(out, wl, xh, start=False, stop=(j == last))
            return ins

        w_d = I["w_in"][0].rearrange("(k p) n -> p k n", p=P)

        def gates_and_v(M, v_at, free, v_raw, norm):
            ar.at = free
            rows_i = ar.put("rows_i", [H, T])
            rows_l = ar.put("rows_l", [H, T])
            rows_k = ar.put("rows_k", [H, T])
            rows_q = ar.put("rows_q", [P, T])
            bias_i = ar.put("bias_i", [H, 1])
            bias_f = ar.put("bias_f", [H, 1])
            m0 = ar.put("m0", [H, NSEQ])
            b_last = ar.put("b_last", [H, 16])
            a_max = ar.put("a_max", [H, 16])
            m_prev = ar.put("m_prev", [H, 16])
            m_last = ar.put("m_last", [H, 16])
            assert ar.at <= norm_at
            v_r = ar.put("gate_tile_r", [P, NTT, D], F32R, at=v_at)
            gate_raw, gate_hi, gate_lo = v_raw[:, 0:KT, 896:D], v_r[:, 0:KT, 768:896], v_r[:, 0:KT, 896:D]
            S = spatial_memory()
            w_rows, w_diag, b_s, ln_b = (ar.put(n, s) for n, s in (
                ("w_rows", [P, H, P]), ("w_diag", [64, H, 64]), ("b_s", [P, H, P]), ("ln_b", [P, D])))
            mix_in, diag_zero, diag_in, w_turned, w_copied, w_masked, bias_mm, stats_done, rstd_done = (cnt("sp_" + n) for n in (
                "mix_in", "diag_zero", "diag_in", "w_turned", "w_copied", "w_masked", "bias_mm", "stats_done", "rstd_done"))
            m_rows, tok, a_prev, m_new = M["m_rows"], M["tok"], M["a_prev"], M["m_new"]
            zeroed, gate_in, small, v_in = cnt("g_zeroed"), cnt("gate_in"), cnt("gate_small"), [cnt(f"v_in{p}") for p in range(4)]
            g_unit, v_unit, v_kept = cnt("gate_unit"), cnt("v_unit"), cnt("gelu_v_kept")
            w_hi_done, w_lo_done = cnt("gv_hi_done"), cnt("gv_lo_done")
            abs_ready, log_ready, e_ready, e_done = cnt("abs_ready"), cnt("log_ready"), cnt("e_ready"), cnt("e_done")
            q_turned, tok_done, m_out = cnt("q_turned"), cnt("tok_done"), cnt("m_out")
            PRO, SAM = slice(0, SEQ), slice(SEQ, T)

            def chunks(row):
                return (row[:, PRO].rearrange("h (c t) -> h c t", t=CHUNK), row[:, SAM].rearrange("h (c t) -> h c t", t=STOK))

            with nc.Block() as block:
                @block.sync
                def _(sp):
                    sp.wait_ge(*zeroed(1))
                    gw = gate_raw
                    sp.dma_start(gw[:, :, 0:4], w_d[:, :, GATE_COLS:GATE_COLS + 4]).then_inc(gate_in.sem, 16)
                    sp.dma_start(gw[:, :, 32:36], w_d[:, :, GATE_COLS + 4:GATE_COLS + 8]).then_inc(gate_in.sem, 16)
                    for p in range(4):
                        if p > 1:
                            sp.wait_ge(*v_unit(9 * (p - 1)))
                        sp.dma_start(M["w_raw"][p % 2][:, :].rearrange("p (k n) -> p k n", k=KT),
                                     w_d[:, :, V_COLS + 256 * p:V_COLS + 256 * p + 256]).then_inc(v_in[p].sem, 16)
                        if p == 1:
                            sp.wait_ge(*lo_done(3 * KT + 1))
                            sp.dma_start(w_rows[:, :, :], I["gmlp_ws"][0].rearrange("g t s -> t g s")).then_inc(mix_in.sem, 16)
                            sp.dma_start(b_s[:, :, :], I["gmlp_bs"].broadcast_to([P, H, P])).then_inc(mix_in.sem, 16)
                            sp.dma_start(ln_b[:, :], I["gmlp_ln_b"].broadcast_to([P, D])).then_inc(mix_in.sem, 16)
                            sp.wait_ge(*diag_zero(1))
                            for b in range(NSEQ):
                                sp.dma_start(w_diag[8 * b:8 * b + 8, :, 8 * b:8 * b + 8],
                                             I["gmlp_ws"][0, :, 0:8, 0:8].rearrange("g t s -> t g s")).then_inc(diag_in.sem, 16)
                    sp.wait_ge(*e_ready(1))
                    sp.dma_start(O["m_prompt"].rearrange("l b h -> h (l b)"), m_new[:, 7:8]).then_inc(m_out.sem, 16)
                    with nc.allow_non_contiguous_dma(reason="32 numbers"):
                        sp.dma_start(O["m_sample"].rearrange("l b h -> h (l b)"), m_new[:, 8:16]).then_inc(m_out.sem, 16)
                    sp.wait_ge(*m_out(32))

                @block.gpsimd
                def _(pool):
                    pool.memset(gate_raw, 0.0).then_inc(zeroed.sem, 1)
                    with nc.allow_non_contiguous_dma(reason="a few numbers"):
                        pool.dma_start(bias_i[:, :], I["b_gates"][0:1, 0:H].rearrange("l h -> h l")).then_inc(small.sem, 16)
                        pool.dma_start(bias_f[:, :], I["b_gates"][0:1, H:2 * H].rearrange("l h -> h l")).then_inc(small.sem, 16)
                        pool.dma_start(m0[:, :], I["state_mlstm_m"].rearrange("l b h -> h (l b)")).then_inc(small.sem, 16)
                    pool.memset(rows_k[:, :], 1.0).then_inc(*pool_steps.one())
                    pool.memset(m_prev[:, :], 0.0).then_inc(*pool_steps.one())
                    pool.memset(rows_q[:, :], 0.0).then_inc(*pool_steps.one())
                    pool.wait_ge(*pool_steps.now())
                    kp, ks = chunks(rows_k)
                    pool.memset(kp[:, :, 0:1], 0.0).then_inc(*pool_steps.one())
                    pool.memset(ks[:, :, 0:1], 0.0).then_inc(zeroed.sem, 1)
                    own = pool_steps
                    pool.wait_ge(*lo_done(3 * KT + 1))
                    pool.memset(w_diag[:, :, :], 0.0).then_inc(diag_zero.sem, 1)
                    pool.memset(M["half"][:, :], -0.5).then_inc(*own.one())
                    pool.memset(M["neg_mask"][:, :], 0.0).then_inc(*own.one())
                    pool.memset(M["neg_diag"][:, :], 0.0).then_inc(*own.one())
                    pool.memset(M["seq_mask"][:, :], 1.0).then_inc(*own.one())
                    pool.wait_ge(*own.now())
                    pool.affine_select(out=M["neg_mask"][:, :], in_=M["neg_mask"][:, :], compare_op=ALU.is_ge, fill=-BIG,
                                       base=0, pattern=[[1, P]], channel_multiplier=-1).then_inc(*own.one())
                    pool.affine_select(out=M["neg_diag"][:, :], in_=M["neg_diag"][:, :], compare_op=ALU.is_ge, fill=-BIG,
                                       base=0, pattern=[[1, 64]], channel_multiplier=-1).then_inc(*own.one())
                    pool.affine_select(out=M["seq_mask"][:, :], in_=M["seq_mask"][:, :], compare_op=ALU.is_ge, fill=0.0,
                                       base=0, pattern=[[-8, NSEQ]], channel_multiplier=1).then_inc(*own.one())
                    pool.wait_ge(*own.now())
                    nd = M["neg_diag"][:, :].rearrange("s (b t) -> s b t", t=STOK)
                    pool.affine_select(out=nd, in_=nd, compare_op=ALU.is_ge, fill=-BIG, base=0,
                                       pattern=[[-8, NSEQ], [0, STOK]], channel_multiplier=1).then_inc(*own.one())
                    pool.affine_select(out=M["seq_mask"][:, :], in_=M["seq_mask"][:, :], compare_op=ALU.is_ge, fill=0.0,
                                       base=7, pattern=[[8, NSEQ]], channel_multiplier=-1).then_inc(*own.one())
                    pool.wait_ge(*w_copied(2))
                    for n, (w, L) in enumerate(((S["w_t"], P), (S["w_dt"], 64))):
                        pool.affine_select(out=w[:, :, :], in_=w[:, :, :], compare_op=ALU.is_ge, fill=0.0, base=0,
                                           pattern=[[0, H], [1, L]], channel_multiplier=-1).then_inc(w_masked.sem, 1)
                    pool.wait_ge(*stats_done(NTT))
                    pool.tensor_scalar(S["rstd"][:, :], S["mv"][:, :, 1], EPS, None, ALU.add).then_inc(*own.one())
                    pool.wait_ge(*own.now())
                    pool.tensor_tensor(S["rstd"][:, :], S["rstd"][:, :], M["half"][:, :], ALU.pow).then_inc(rstd_done.sem, 1)

                @block.scalar
                def _(act):
                    def split(p):
                        act.wait_ge(*v_in[p](16))
                        for i in range(2):
                            s = p % 2
                            act.activation(pair_part(M, "hi", s, i), pair_part(M, "raw", s, i), ACT.Copy).then_inc(w_hi_done.sem, 1)

                    norm.roots(act)
                    for j in range(2 * KT):
                        if j == 4:
                            act.wait_ge(*gate_in(32))
                            act.activation(gate_hi, gate_raw, ACT.Copy).then_inc(w_hi_done.sem, 1)
                        if j == KT:
                            split(0)
                        norm.high(act, j)
                    for p in range(4):
                        for t in range(NTT):
                            rows = 64 if t == 8 else P
                            if (p, t) == (0, 3):
                                for j in range(2 * KT, 3 * KT):
                                    norm.high(act, j)
                                norm.high_samples(act)
                            act.wait_ge(*v_unit(9 * p + t + 1))
                            r0 = 64 if t == 8 else 0
                            act.activation(v_raw[0:rows, t, 256 * p:256 * p + 256], ps[r0:r0 + rows, 3 + t % 3, 0:256],
                                           ACT.Gelu_apprx_tanh).then_inc(v_kept.sem, 1)
                            if t == (3 if p == 0 else 1) and p < 3:
                                split(p + 1)
                            if (p, t) == (2, 3):
                                act.wait_ge(*w_turned(1))
                                act.activation(S["w_t"][:, :, :].rearrange("p g t -> p (g t)"), ps[:, 0, 0:512], ACT.Copy).then_inc(w_copied.sem, 1)
                                act.wait_ge(*w_turned(2))
                                act.activation(S["w_dt"][:, :, :].rearrange("p g t -> p (g t)"), ps[0:64, 1, 0:256], ACT.Copy).then_inc(w_copied.sem, 1)
                            if (p, t) == (0, 7):
                                act.wait_ge(*abs_ready(1))
                                act.activation(rows_l[:, :], rows_l[:, :], ACT.Exp, scale=-1.0).then_inc(*act_steps.one())
                                act.wait_ge(*act_steps.now())
                                act.activation(rows_l[:, :], rows_l[:, :], ACT.Ln, bias=1.0).then_inc(log_ready.sem, 1)
                            if (p, t) == (1, 6):
                                act.wait_ge(*e_ready(1))
                                act.activation(a_prev[:, :], m_last[:, :], ACT.Exp).then_inc(*act_steps.one())
                                act.activation(rows_q[32:36, :], rows_k[:, :], ACT.Exp).then_inc(e_done.sem, 1)
                                act.wait_ge(*e_ready(2))
                                act.activation(rows_q[64:68, :], rows_k[:, :], ACT.Exp).then_inc(e_done.sem, 1)
                                act.wait_ge(*e_ready(3))
                                act.activation(rows_q[96:100, :], rows_k[:, :], ACT.Exp, scale=-1.0).then_inc(e_done.sem, 1)

                @block.vector
                def _(dve):
                    own = dve_steps

                    def low(n, lo, raw, hi):
                        dve.wait_ge(*w_hi_done(n))
                        dve.tensor_tensor(lo, raw, hi.bitcast(F32), ALU.subtract).then_inc(w_lo_done.sem, 1)

                    def split(p):
                        for i in range(2):
                            low(2 * p + i + 2, *(pair_part(M, kd, p % 2, i) for kd in ("lo", "raw", "hi")))

                    def link(ins):
                        ins.then_inc(*own.one())
                        dve.wait_ge(*own.now())

                    norm.factors(dve)
                    norm.unit(dve, 0, between=lambda: low(1, gate_lo, gate_raw, gate_hi))
                    split(0)
                    norm.unit(dve, 1)
                    norm.unit(dve, 2)
                    norm.samples(dve)
                    norm.gates(dve)
                    split(1)
                    dve.wait_ge(*small(48))
                    dve.wait_ge(*zeroed(2))
                    for n, (t0, w) in enumerate(UNITS):
                        dve.wait_ge(*g_unit(n + 1))
                        dve.tensor_scalar(rows_i[:, t0:t0 + w], ps[0:4, n, 0:w], bias_i[:, 0:1], None, ALU.add).then_inc(*own.one())
                        link(dve.tensor_scalar(m_rows[:, t0:t0 + w], ps[32:36, n, 0:w], bias_f[:, 0:1], None, ALU.add))
                    dve.scalar_tensor_tensor(out=rows_l[:, :], in0=m_rows[:, :], scalar=-1.0, in1=m_rows[:, :],
                                             op0=ALU.mult, op1=ALU.max).then_inc(abs_ready.sem, 1)
                    dve.wait_ge(*log_ready(1))
                    link(dve.scalar_tensor_tensor(out=m_rows[:, :], in0=m_rows[:, :], scalar=0.0, in1=rows_l[:, :],
                                                  op0=ALU.min, op1=ALU.subtract))
                    link(dve.tensor_tensor_scan(rows_l[:, :], rows_k[:, :], m_rows[:, :], 0.0, ALU.mult, ALU.add))
                    dve.tensor_tensor(rows_i[:, :], rows_i[:, :], rows_l[:, :], ALU.subtract).then_inc(*own.one())
                    link(dve.tensor_scalar(rows_k[:, :], rows_k[:, :], -1.0, BIG, ALU.add, ALU.mult))
                    link(dve.tensor_tensor_scan(m_rows[:, :], rows_k[:, :], rows_i[:, :], -BIG, ALU.add, ALU.max))
                    for dst, src in ((b_last, rows_l), (a_max, m_rows)):
                        sp_, ss_ = chunks(src)
                        dve.tensor_copy(dst[:, 0:8], sp_[:, :, CHUNK - 1]).then_inc(*own.one())
                        link(dve.tensor_copy(dst[:, 8:16], ss_[:, :, STOK - 1]))
                    dve.tensor_copy(m_prev[:, 8:16], m0[:, :]).then_inc(*own.one())
                    dve.tensor_tensor(m_new[:, 8:16], a_max[:, 8:16], m0[:, :], ALU.max).then_inc(*own.one())
                    link(dve.tensor_tensor_scan(m_new[:, 0:8], a_max[:, 0:8], b_last[:, 0:8], 0.0, ALU.max, ALU.add))
                    link(dve.tensor_tensor(m_new[:, 8:16], m_new[:, 8:16], b_last[:, 8:16], ALU.add))
                    link(dve.tensor_copy(m_prev[:, 1:8], m_new[:, 0:7]))
                    link(dve.tensor_tensor(a_max[:, :], m_prev[:, :], a_max[:, :], ALU.max))
                    link(dve.tensor_tensor(m_last[:, :], m_prev[:, :], a_max[:, :], ALU.subtract))
                    for mr, c0, L in zip(chunks(m_rows), (0, 8), (CHUNK, STOK)):
                        link(dve.tensor_tensor(mr, mr, bc(m_prev[:, c0:c0 + 8], 2, L), ALU.max))
                    dve.tensor_copy(rows_q[0:4, :], rows_i[:, :]).then_inc(*own.one())
                    for n, (kr, ir, c0, L) in enumerate(zip(chunks(rows_k), chunks(rows_i), (0, 8), (CHUNK, STOK))):
                        ins = dve.tensor_tensor(kr, ir, bc(a_max[:, c0:c0 + 8], 2, L), ALU.subtract)
                        ins.then_inc(*(own.one() if n == 0 else (e_ready.sem, 1)))
                    dve.wait_ge(*e_done(1))
                    split(2)
                    for n, (kr, mr, c0, L) in enumerate(zip(chunks(rows_k), chunks(m_rows), (0, 8), (CHUNK, STOK))):
                        ins = dve.tensor_tensor(kr, bc(m_prev[:, c0:c0 + 8], 2, L), mr, ALU.subtract)
                        ins.then_inc(*(own.one() if n == 0 else (e_ready.sem, 1)))
                    dve.wait_ge(*e_done(2))
                    dve.tensor_tensor(rows_k[:, :], rows_l[:, :], m_rows[:, :], ALU.add).then_inc(e_ready.sem, 1)
                    split(3)
                    stats, mv = S["stats"], S["mv"]
                    dve.memset(mv[:, 8, :], 1.0).then_inc(*own.one())

                    def half_stats(t, i):
                        rows = 64 if t == 8 else P
                        dve.wait_ge(*v_kept(9 * (2 * i + 1) + t + 1))
                        dve.bn_stats(stats[0:rows, t, i, :], v_raw[0:rows, t, 512 * i:512 * i + 512]).then_inc(*own.one())

                    for t in range(NTT):
                        half_stats(t, 0)
                    for hf in range(2):
                        dve.wait_ge(*bias_mm(hf + 1))
                        dve.tensor_tensor(S["bias"][:, 4 * hf:4 * hf + 4, :].rearrange("p (g f) t -> p g f t", f=2),
                                          ps[:, hf, 0:512].rearrange("p (g f t) -> p g f t", g=2, f=2),
                                          bc(b_s[:, 2 * hf:2 * hf + 2, :], 2, 2), ALU.add).then_inc(*own.one())
                    for t in range(NTT):
                        rows = 64 if t == 8 else P
                        half_stats(t, 1)
                        dve.wait_ge(*own.now())
                        dve.bn_aggr(mv[0:rows, t, :], stats[0:rows, t, :, :].rearrange("p a b -> p (a b)")).then_inc(stats_done.sem, 1)
                    for t in range(NTT):
                        rows = 64 if t == 8 else P
                        dve.wait_ge(*q_turned(t + 1))
                        dve.tensor_copy(tok[0:rows, t, :, :],
                                        ps[0:rows, 6 + t % 2, 0:P].rearrange("p (q h) -> p q h", h=32)[:, :, 0:H]
                                        ).then_inc(tok_done.sem, 1)
                    dve.wait_ge(*tok_done(NTT))
                    dve.tensor_scalar(tok[:, 0:8, 1, :], tok[:, 0:8, 1, :], 1.0 / 16, None, ALU.mult).then_inc(*own.one())
                    dve.tensor_scalar(tok[0:64, 8, 1, :], tok[0:64, 8, 1, :], 1.0 / 16, None, ALU.mult).then_inc(tok_done.sem, 1)
                    dve.wait_ge(*rstd_done(1))
                    dve.scalar_tensor_tensor(out=S["off"][:, :], in0=mv[:, :, 0], scalar=-1.0, in1=S["rstd"][:, :],
                                             op0=ALU.mult, op1=ALU.mult).then_inc(*own.one())
                    dve.wait_ge(*own.now())

                @block.tensor
                def _(pe):
                    norm.means(pe)
                    wh, wl = gate_hi, gate_lo
                    pe.wait_ge(*w_lo_done(1))

                    def gate(n):
                        t0, w = UNITS[n]
                        if n == 2:
                            pe.wait_ge(*lo_done(3 * KT + 1))
                        for k in range(KT):
                            pe.wait_ge(*lo_done(KT * n + k + 1))
                            pe.matmul(ps[:, n, 0:w], wh[:, k, :], hhi[:, k, t0:t0 + w], start=(k == 0), stop=False)
                            pe.matmul(ps[:, n, 0:w], wh[:, k, :], hlo[:, k, t0:t0 + w], start=False, stop=False)
                            ins = pe.matmul(ps[:, n, 0:w], wl[:, k, :], hhi[:, k, t0:t0 + w], start=False, stop=(k == KT - 1))
                        ins.then_inc(g_unit.sem, 1)

                    for p in range(4):
                        s = p % 2
                        vh = M["w_hi"][s][:, :].rearrange("p (k n) -> p k n", k=KT)
                        vl = M["w_lo"][s][:, :].rearrange("p (k n) -> p k n", k=KT)
                        for t in range(NTT):
                            if p == 0 and t % 3 == 0:
                                gate(t // 3)
                            if t == 0:
                                pe.wait_ge(*w_lo_done(2 * p + 3))
                            if (p, t) == (2, 2):
                                pe.wait_ge(*mix_in(48))
                                for g in range(H):
                                    ins = pe.transpose(ps[:, 0, 128 * g:128 * g + 128], w_rows[:, g, :], ident[:, :])
                                ins.then_inc(w_turned.sem, 1)
                                pe.wait_ge(*diag_in(16 * NSEQ))
                                for g in range(H):
                                    ins = pe.transpose(ps[0:64, 1, 64 * g:64 * g + 64], w_diag[:, g, :], ident[0:64, 0:64])
                                ins.then_inc(w_turned.sem, 1)
                            if (p, t) == (3, 1):
                                pe.wait_ge(*w_masked(2))
                                for hf in range(2):
                                    for f in range(4):
                                        ft = 4 * hf + f
                                        ins = pe.matmul(ps[:, hf, 128 * f:128 * f + 128], ln_b[:, 128 * ft:128 * ft + 128],
                                                        S["w_t"][:, ft // 2, :], start=True, stop=True)
                                    ins.then_inc(bias_mm.sem, 1)
                            if 9 * p + t >= 3:
                                pe.wait_ge(*v_kept(9 * p + t - 2))
                            a, b = (128 * t, 128 * t + 128) if t < 8 else (T - 128, T)
                            three(pe, ps[:, 3 + t % 3, 0:256],
                                  [(hhi[:, k, a:b], hlo[:, k, a:b], vh[:, k, :], vl[:, k, :]) for k in range(KT)]
                                  ).then_inc(v_unit.sem, 1)
                    pe.wait_ge(*e_done(3))
                    for t in range(NTT):
                        rows = 64 if t == 8 else P
                        if t >= 2:
                            pe.wait_ge(*tok_done(t - 1))
                        pe.transpose(ps[0:rows, 6 + t % 2, 0:P], rows_q[:, 128 * t:128 * t + rows],
                                     ident[:, :]).then_inc(q_turned.sem, 1)
            norm.close()
            return S

        def spatial_memory():
            S = {n: ar.put("sp_" + n, s) for n, s in (
                ("bias", [P, KT, P]), ("w_t", [P, H, P]), ("w_dt", [64, H, 64]), ("stats", [P, NTT, 2, 6]),
                ("mv", [P, NTT, 2]), ("rstd", [P, NTT]), ("off", [P, NTT]))}
            S["end"] = ar.at
            return S

        def spatial(M, S, free, v, mixed_d):
            ar.at = M["ring_at"]
            crow = ar.put("conv_rows", [NSEQ * 3, 2 * D])
            ar.at = M["ring_at"] + 4 * 4096
            ln_g = ar.put("ln_g", [64, D])
            v_s = ar.put("v_s", [64, D])
            ar.at = free
            SLOTS = 4
            stage = ar.put("stage", [P, SLOTS, KT, P])
            nrow = ar.put("n_rows", [NSEQ * H, DH])
            assert ar.at <= free + 17408
            ar.at = S["end"]
            ln_b = ar.put("ln_b_s", [64, D])
            names = ("ln_in", "states_in", "scaled", "scaled_a", "v_ready", "mix_unit", "mix_kept", "v_out", "s_turned", "s_kept")
            ln_in, states_in, scaled_v, scaled_a, v_ready, mix_unit, mix_kept, v_out, s_turned, s_kept = (cnt("sp2_" + n) for n in names)
            mix_out = [cnt(f"sp_mix_out{s}") for s in range(SLOTS)]

            def scaled(t):
                return (scaled_a if t % 2 else scaled_v)(t // 2 + 1)

            with nc.Block() as block:
                @block.sync
                def _(sp):
                    sp.dma_start(crow[:, :], I["state_conv"].rearrange("l b j c -> (l b j) c")).then_inc(states_in.sem, 16)
                    sp.dma_start(nrow[:, :], I["state_mlstm_n"].rearrange("l b h d -> (l b h) d")).then_inc(states_in.sem, 16)
                    sp.dma_start(ln_g[:, :], I["gmlp_ln_g"].broadcast_to([64, D])).then_inc(ln_in.sem, 16)
                    sp.dma_start(ln_b[:, :], I["gmlp_ln_b"].broadcast_to([64, D])).then_inc(ln_in.sem, 16)
                    for s, col in enumerate((Q_COLS, K_COLS)):
                        sp.dma_start(M["w_raw"][s][:, :].rearrange("p (k n) -> p k n", k=KT),
                                     w_d[:, :, col:col + 256]).then_inc(head_w_in[s].sem, 16)
                    md = mixed_d.rearrange("(f p) t -> p f t", p=P)
                    for t in range(NTT):
                        n = 64 if t == 8 else P
                        sp.wait_ge(*mix_kept(2 * t + 2))
                        sp.dma_start(md[:, :, 128 * t:128 * t + n], stage[:, t % SLOTS, :, 0:n]).then_inc(mix_out[t % SLOTS].sem, 16)
                    sp.wait_ge(*v_ready(1))
                    sp.dma_start(O["v_sample"].rearrange("l b t d -> (l b t) d"), v_s[:, :]).then_inc(v_out.sem, 16)

                @block.gpsimd
                def _(pool):
                    pool.wait_ge(*ln_in(32))
                    pool.wait_ge(*scaled(8))
                    pool.tensor_tensor(v_s[:, :], v[0:64, 8, :], ln_g[:, :], ALU.mult).then_inc(*pool_steps.one())
                    pool.wait_ge(*pool_steps.now())
                    pool.tensor_tensor(v_s[:, :], v_s[:, :], ln_b[:, :], ALU.add).then_inc(v_ready.sem, 1)

                @block.scalar
                def _(act):
                    for t in range(1, NTT, 2):
                        act.activation(v[:, t, :], v[:, t, :], ACT.Identity, scale=S["rstd"][:, t:t + 1],
                                       bias=S["off"][:, t:t + 1]).then_inc(scaled_a.sem, 1)
                    act.wait_ge(*s_turned(1))
                    act.activation(M["conv_in"][:, :, :, :].rearrange("p a t n -> p (a t n)"), ps[:, 0, 0:384], ACT.Copy).then_inc(s_kept.sem, 1)
                    act.wait_ge(*s_turned(2))
                    act.activation(M["n_in"][:, :, :, :].rearrange("p i b h -> p (i b h)"), ps[:, 1, 0:64], ACT.Copy).then_inc(s_kept.sem, 1)

                @block.vector
                def _(dve):
                    def scale(t):
                        rows = 64 if t == 8 else P
                        dve.tensor_scalar(v[0:rows, t, :], v[0:rows, t, :], S["mv"][0:rows, t, 0:1], S["rstd"][0:rows, t:t + 1],
                                          ALU.subtract, ALU.mult).then_inc(scaled_v.sem, 1)

                    def keep(t):
                        for hf in range(2):
                            dve.wait_ge(*mix_unit(2 * t + hf + 1))
                            if t >= SLOTS and hf == 0:
                                dve.wait_ge(*mix_out[t % SLOTS](16 * (t // SLOTS)))
                            bank = 2 + (2 * t + hf) % 6
                            for f in range(4):
                                ft = 4 * hf + f
                                g = vT[:, V_LN + ft:V_LN + ft + 1]
                                if t < 8:
                                    ins = dve.scalar_tensor_tensor(
                                        out=stage[:, t % SLOTS, ft, :], in0=ps[:, bank, 128 * f:128 * f + 128], scalar=g,
                                        in1=S["bias"][:, ft, :], op0=ALU.mult, op1=ALU.add)
                                else:
                                    ins = dve.scalar_tensor_tensor(
                                        out=stage[:, 0, ft, 0:64].rearrange("p (b t) -> p b t", t=STOK),
                                        in0=ps[:, bank, 64 * f:64 * f + 64].rearrange("p (b t) -> p b t", t=STOK), scalar=g,
                                        in1=bc(S["bias"][:, ft, 0:STOK], 1, NSEQ), op0=ALU.mult, op1=ALU.add)
                            ins.then_inc(mix_kept.sem, 1)

                    scale(0)
                    scale(2)
                    for t in range(NTT):
                        if t % 2 == 0 and t + 4 < NTT:
                            scale(t + 4)
                        keep(t)

                @block.tensor
                def _(pe):
                    for t in range(NTT):
                        rows = 64 if t == 8 else P
                        pe.wait_ge(*scaled(t))
                        for hf in range(2):
                            u = 2 * t + hf
                            if u >= 6:
                                pe.wait_ge(*mix_kept(u - 5))
                            w = S["w_t"] if t < 8 else S["w_dt"]
                            for f in range(4):
                                ft = 4 * hf + f
                                ins = pe.matmul(ps[:, 2 + u % 6, rows * f:rows * f + rows], v[0:rows, t, 128 * ft:128 * ft + 128],
                                                w[:, ft // 2, :], start=True, stop=True)
                            ins.then_inc(mix_unit.sem, 1)
                    pe.wait_ge(*states_in(32))
                    for j in range(16):
                        ins = pe.transpose(ps[:, 0, 24 * j:24 * j + 24], crow[:, 128 * j:128 * j + 128], ident[0:24, 0:24])
                    ins.then_inc(s_turned.sem, 1)
                    for i in range(2):
                        ins = pe.transpose(ps[:, 1, 32 * i:32 * i + 32], nrow[:, 128 * i:128 * i + 128], ident[0:32, 0:32])
                    ins.then_inc(s_turned.sem, 1)

            return [v_out(16)] + [mix_out[t](16 * (3 if t == 0 else 2)) for t in range(SLOTS)]

        def heads(M, free, mixed_d, stored):
            ar.at = free
            q = ar.put("q", [P, 2, T], at=None)
            q_at = ar.at - 2 * T * 4
            k_at = ar.at
            kk = ar.put("kk", [P, 2, T])
            mix_hi = ar.put("mix_hi", [P, 2, T], F32R, at=q_at)
            mix_lo = ar.put("mix_lo", [P, 2, T], F32R, at=k_at)
            vx_at = ar.at
            vx = ar.put("vx", [P, NTT, DH + 1])
            ob = ar.put("ob", [P, 2, T])
            ub = ar.put("ub", [P, 2, T])
            zc_at = ar.at
            ZP, ZS = SEQ + 3, NSEQ * (STOK + 3)
            zc = ar.put("zc", [P, ZP + ZS])
            zc_end = ar.at
            ar.at = zc_at
            ex = ar.put("ex", [P, P])
            st = ar.put("s_t", [P, P])
            kw = ar.put("kw", [P, DH])
            inter = ar.put("inter", [P, DH + 1])
            ar.at = max(ar.at, zc_end)
            C = ar.put("C", [P, 2, DH + 1])
            otmp = ar.put("otmp", [P, 4, NSEQ, STOK])
            cw = ar.put("cw", [P, CW, 2, 2])
            cb = ar.put("cb", [P, 2, 2])
            ng = ar.put("ng", [P, 2])
            pads = ar.put("pads", [P, 2, 2, 24])
            tk = ar.put("tk", [P, NTT, 4])
            sel = ar.put("sel", [H, P])
            ap_ = ar.put("ap_", [P, 16])
            hn0 = ar.put("hn0", [P, 2, NSEQ])
            w_mask = ar.put("w_mask", [64, NSEQ])
            den = ar.put("den", [P, 2])
            hst = ar.put("hst", [P, 6])
            hmv = ar.put("hmv", [P, 2])
            var = ar.put("var", [P, 2])
            assert ar.at <= norm_at
            num = ar.put("num", [P, DH + 1])
            tmp = ar.put("gate_tmp", [P, 2, 384])
            kws = ar.put("kws", [64, DH])
            inter_s = ar.put("inter_s", [64, DH + 1])
            vb = ar.put("vb", [64, DH + 1])
            cs = ar.put("cs", [P, 2, 2, DH + 1])
            crow = ar.put("conv_rows_out", [27, 2 * D], at=vx_at)
            nrow = ar.put("n_rows_out", [NSEQ * H, DH], at=zc_at)
            nprow = ar.put("np_rows_out", [H, DH], at=zc_at + 4 * DH)
            state_turned, state_kept, states_stored = cnt("h_state_turned"), cnt("h_state_kept"), cnt("h_states_stored")
            sq = Squares(OUT_ORDER)
            x_added = ffn_counts["x_added"]
            names = ("hi", "lo", "qk_unit", "zc_kept", "conv", "qk_ready", "vm_unit", "vm_kept", "step_unit",
                     "step_act", "step_mul", "mix_sum", "mix_hi", "mix_lo", "out_unit", "staged", "ap_mm", "ap_kept", "kT", "kw_done",
                     "s0", "e_ready", "e_done", "st_done", "inter_mm", "inter_done", "s1", "b5_read", "c_upd", "var_ready",
                     "rs_ready", "h_ready", "s2", "h_kept", "prep", "seq_mm", "seq_upd", "ub_in", "cp_out", "ones_made", "passed")
            K = {n: cnt("h_" + n) for n in names}
            w_in_ = head_w_in
            c_in = [cnt("h_c_in0"), cnt("h_c_in1")]
            c_out = [cnt("h_c_out0"), cnt("h_c_out1")]
            JOBS = [0, 1, 2, 3, "S", 4, 5, 6, 7]
            NJ = len(JOBS)
            EVENTS, unit = [], 0
            for gap in range(3 * NJ):
                EVENTS.append(("stage", gap // 3, gap % 3))
                while unit < ((gap + 1) * 8 + 8) // 9:
                    EVENTS.append(("unit", unit, None))
                    unit += 1

            def place(p):
                c = JOBS[p]
                return (False, None, SEQ, 64, 8) if c == "S" else (True, c, c * CHUNK, CHUNK, c)

            def seq_at(p, stage):
                return 2 * p + stage // 2 if p < 4 and stage != 1 else None

            def zc_out(n, w):
                t0 = UNITS[n][0]
                return zc[:, 3 + t0:3 + t0 + w]

            zs = zc[:, ZP:ZP + ZS].rearrange("p (b t) -> p b t", t=STOK + 3)

            with nc.Block() as block:
                @block.sync
                def _(sp):
                    DOWN = I["w_out"][0].rearrange("(h k p) n -> p h k n", k=2, p=P)

                    def load(h, pair):
                        dst = M["w_raw"][pair % 2]
                        sp.sem_inc(K["passed"].sem, 1)
                        if pair == 7:
                            src = DOWN[:, bass.ds(h, 1), :, :].squeeze(1)
                            sp.dma_start(dst[:, :].rearrange("p (k n) -> p k n", k=2), src).then_inc(w_in_[1].sem, 16)
                            return
                        col = (Q_COLS, K_COLS, VM_COLS, GB_COLS, O_COLS, GA_COLS, GELU_COLS)[pair]
                        sp.dma_start(dst[:, :].rearrange("p (k n) -> p k n", k=KT),
                                     w_d[:, :, bass.ds(h * 256 + col, 256)]).then_inc(w_in_[pair % 2].sem, 16)

                    def load_state(h, b):
                        src = I["state_mlstm_C"][0, b].rearrange("h (i p) e -> p h i e", p=P)[:, bass.ds(h, 1), :, :].squeeze(1)
                        sp.dma_start(cs[:, b % 2, :, 0:DH], src).then_inc(c_in[b % 2].sem, 16)

                    def body(h, last):
                        sp.wait_ge(*x_added(h * 24))
                        sp.dma_start(ub[:, :, :], mixed_d.rearrange("(h i p) t -> p h i t", i=2, p=P)[:, bass.ds(h, 1), :, :]
                                     .squeeze(1)).then_inc(K["ub_in"].sem, 16)
                        load_state(h, 0)
                        load_state(h, 1)
                        for pair in range(3):
                            sp.wait_ge(*(K["qk_unit"](h * 12 + 6 * pair + 6) if pair < 2 else K["vm_unit"](h * NTT + NTT)))
                            load(h, pair + 2)
                        for kind, a, stage in EVENTS:
                            if kind == "stage" and seq_at(a, stage) is not None:
                                b = seq_at(a, stage)
                                sp.wait_ge(*K["seq_upd"](h * 8 + b + 1))
                                dst = O["C_sample"][0, b].rearrange("h (i p) e -> p h i e", p=P)[:, bass.ds(h, 1), :, :].squeeze(1)
                                sp.dma_start(dst, cs[:, b % 2, :, 0:DH]).then_inc(c_out[b % 2].sem, 16)
                                if b + 2 < NSEQ:
                                    sp.wait_ge(*c_out[b % 2](h * 64 + 16 * (b // 2 + 1)))
                                    load_state(h, b + 2)
                            if kind == "unit" and a % 6 == 5:
                                pair = 3 + a // 6
                                sp.wait_ge(*K["step_unit"](h * 24 + a + 1))
                                if pair < 6:
                                    load(h, pair + 2)
                                elif not last:
                                    load(h + 1, 0)
                        for s in range(2):
                            sp.wait_ge(*c_out[s](h * 64 + 64))
                        sp.wait_ge(*K["c_upd"](h * 8 + 8))
                        dst = O["C_prompt"][0, 0].rearrange("h (i p) e -> p h i e", p=P)[:, bass.ds(h, 1), :, :].squeeze(1)
                        sp.dma_start(dst, C[:, :, 0:DH]).then_inc(K["cp_out"].sem, 16)
                        sp.wait_ge(*K["cp_out"](h * 16 + 16))
                        if not last:
                            sp.wait_ge(*K["out_unit"](h * 24 + 24))
                            load(h + 1, 1)

                    for done in stored:
                        sp.wait_ge(*done)
                    with sp.Fori(0, H - 1) as h:
                        body(h, False)
                    body(H - 1, True)
                    sp.wait_ge(*state_kept(5))
                    sp.dma_start(O["conv_prompt"][0, 0], crow[0:3, :]).then_inc(states_stored.sem, 16)
                    sp.dma_start(O["conv_sample"].rearrange("l b j c -> (l b j) c"), crow[3:27, :]).then_inc(states_stored.sem, 16)
                    sp.dma_start(O["n_sample"].rearrange("l b h d -> (l b h) d"), nrow[:, :]).then_inc(states_stored.sem, 16)
                    sp.dma_start(O["n_prompt"].rearrange("l b h d -> (l b h) d"), nprow[:, :]).then_inc(states_stored.sem, 16)
                    sp.wait_ge(*states_stored(64))

                @block.gpsimd
                def _(pool):
                    own = pool_steps
                    pool.memset(vx[:, :, DH:DH + 1], 1.0).then_inc(K["ones_made"].sem, 1)
                    with pool.Fori(0, H) as h:
                        own.enter(h, NJ)
                        for p in range(NJ):
                            rows = place(p)[3]
                            pool.wait_ge(*K["var_ready"](h * NJ + p + 1))
                            pool.sem_inc(K["passed"].sem, 1)
                            pool.tensor_scalar(var[0:rows, 1:2], var[0:rows, 0:1], EPS, None, ALU.add).then_inc(*own.one())
                            pool.wait_ge(*own.now())
                            pool.tensor_tensor(var[0:rows, 1:2], var[0:rows, 1:2], M["half"][0:rows, 0:1], ALU.pow
                                               ).then_inc(K["rs_ready"].sem, 1)
                        own.leave(H)
                    for u in range(24):
                        sq.add(pool, u)

                @block.scalar
                def _(act):
                    def split(h, j):
                        pair, i = j // 2, j % 2
                        if i == 0:
                            act.wait_ge(*w_in_[pair % 2](h * 64 + 16 * (pair // 2) + 16))
                        rows = pair == 7
                        act.activation(pair_part(M, "hi", pair % 2, i, rows), pair_part(M, "raw", pair % 2, i, rows),
                                       ACT.Copy).then_inc(K["hi"].sem, 1)

                    def silu(h, j):
                        act.wait_ge(*K["conv"](h * 4 + j + 1))
                        t = (q, kk)[j // 2][:, j % 2, :]
                        act.activation(t, t, ACT.Silu).then_inc(K["qk_ready"].sem, 1)

                    def unit(h, u):
                        tile, n = divmod(u, 3)
                        t0, w = UNITS[n]
                        i = tile % 2
                        act.wait_ge(*K["step_unit"](h * 24 + u + 1))
                        if tile < 2:
                            dst = ob[:, i, t0:t0 + w]
                        else:
                            dst = tmp[:, u % 2, 0:w]
                            if u >= 8:
                                act.wait_ge(*K["step_mul"](h * 18 + u - 7))
                        f = ACT.Gelu_apprx_tanh if tile >= 6 else ACT.Sigmoid
                        act.activation(dst, ps[:, u % 3, 0:w], f).then_inc(K["step_act"].sem, 1)

                    def stage0(h, p):
                        chunk, c, t0, L, tt = place(p)
                        if chunk:
                            act.wait_ge(*K["kT"](h * NJ + c + 2))
                            if p:
                                act.wait_ge(*K["s1"](h * NJ + p))
                            act.activation(kw[:, :], ps[:, 4, 0:DH], ACT.Copy, scale=tk[:, tt, 1:2]).then_inc(K["kw_done"].sem, 1)
                        act.wait_ge(*K["e_ready"](h * NJ + p + 1))
                        act.activation(ex[0:L, 0:L], ex[0:L, 0:L], ACT.Exp, bias=tk[0:L, tt, 0:1]).then_inc(K["e_done"].sem, 1)

                    def stage1(h, p):
                        chunk, c, t0, L, tt = place(p)
                        if chunk:
                            act.wait_ge(*K["inter_mm"](h * 8 + c + 1))
                            act.activation(inter[:, :], ps[:, 4, 0:DH + 1], ACT.Copy, scale=tk[:, tt, 2:3]
                                           ).then_inc(K["inter_done"].sem, 1)

                    def stage2(h, p):
                        chunk, c, t0, L, tt = place(p)
                        act.wait_ge(*K["s2"](h * NJ + p + 1))
                        for i in range(2):
                            ins = act.activation(q[:, i, t0:t0 + L], ps[:, 4, 128 * i:128 * i + L], ACT.Copy, scale=ng[:, i:i + 1])
                        ins.then_inc(K["h_kept"].sem, 1)

                    def mixed_high(h, n):
                        t0, w = UNITS[n]
                        for i in range(2):
                            act.wait_ge(*K["mix_sum"](h * 6 + 2 * n + i + 1))
                            act.activation(mix_hi[:, i, t0:t0 + w], ub[:, i, t0:t0 + w], ACT.Copy).then_inc(K["mix_hi"].sem, 1)

                    def body(h, last):
                        for j in range(4):
                            for n, (t0, w) in enumerate(UNITS):
                                act.wait_ge(*K["qk_unit"](h * 12 + 3 * j + n + 1))
                                if n == 0 and j:
                                    act.wait_ge(*K["conv"](h * 4 + j))
                                if n < 2:
                                    act.activation(zc_out(n, w), ps[:, n, 0:w], ACT.Copy).then_inc(K["zc_kept"].sem, 1)
                                else:
                                    act.activation(zc_out(n, TAIL_P), ps[:, n, 0:TAIL_P], ACT.Copy)
                                    act.activation(zs[:, :, 3:3 + STOK], ps[:, n, TAIL_P:w].rearrange("p (b t) -> p b t", t=STOK),
                                                   ACT.Copy).then_inc(K["zc_kept"].sem, 1)
                                if n == 0:
                                    split(h, j + 2)
                                if n == 1 and j:
                                    silu(h, j - 1)
                        for t in range(NTT):
                            rows, r0 = (64, 64) if t == 8 else (P, 0)
                            act.wait_ge(*K["vm_unit"](h * NTT + t + 1))
                            act.activation(vx[0:rows, t, 0:DH], ps[r0:r0 + rows, t % 3, 0:DH], ACT.Copy).then_inc(K["vm_kept"].sem, 1)
                            if t == 1:
                                silu(h, 3)
                            if t in (3, 4):
                                split(h, t + 3)
                        act.wait_ge(*K["kT"](h * NJ + 1))
                        act.activation(kws[:, :], ps[0:64, 4, 0:DH], ACT.Copy, scale=tk[0:64, 8, 1:2]).then_inc(K["kw_done"].sem, 1)
                        for kind, a, s in EVENTS:
                            if kind == "stage":
                                (stage0, stage1, stage2)[s](h, a)
                                if (a, s) == (NJ - 1, 1):
                                    mixed_high(h, 1)
                            else:
                                unit(h, a)
                                if a % 3 == 1:
                                    split(h, a // 3 + 8)
                                if a == 21:
                                    mixed_high(h, 0)
                        mixed_high(h, 2)
                        if not last:
                            split(h + 1, 0)
                            split(h + 1, 1)

                    split(0, 0)
                    split(0, 1)
                    for done in stored:
                        act.wait_ge(*done)
                    with act.Fori(0, H - 1) as h:
                        body(h, False)
                    body(H - 1, True)
                    for s in range(2):
                        act.wait_ge(*c_out[s](H * 64))
                    for u in range(24):
                        act.wait_ge(*x_added(24 * (H - 1) + u + 1))
                        sq.square(act, u)
                        if u % 4 == 3 and u < 20:
                            q_ = u // 4
                            act.wait_ge(*state_turned(q_ + 1))
                            if q_ < 4:
                                act.activation(crow[:, 512 * q_:512 * q_ + 512], ps[0:27, 6 + q_ % 2, :], ACT.Copy).then_inc(state_kept.sem, 1)
                            else:
                                act.activation(nrow[:, :], ps[0:32, 6, 0:DH], ACT.Copy)
                                act.activation(nprow[:, :], ps[0:H, 6, DH:2 * DH], ACT.Copy).then_inc(state_kept.sem, 1)

                @block.vector
                def _(dve):
                    own = dve_steps

                    def link(ins):
                        ins.then_inc(*own.one())
                        dve.wait_ge(*own.now())

                    def split(h, j):
                        pair, i = j // 2, j % 2
                        rows = pair == 7
                        dve.wait_ge(*K["hi"](h * 16 + j + 1))
                        dve.tensor_tensor(pair_part(M, "lo", pair % 2, i, rows), pair_part(M, "raw", pair % 2, i, rows),
                                          pair_part(M, "hi", pair % 2, i, rows).bitcast(F32), ALU.subtract).then_inc(K["lo"].sem, 1)

                    def stage_head(h):
                        cwv = vT[:, V_CW:V_CW + 64].rearrange("p (j a t) -> p (j a) t", j=CW, a=2)
                        dve.tensor_copy(cw[:, :, :, :].rearrange("p j a i -> p (j a) i"), cwv[:, :, bass.ds(h * 2, 2)]).then_inc(*own.one())
                        dve.tensor_copy(cb[:, :, :], vT[:, V_CB:V_CB + 16].rearrange("p (a t) -> p a t", a=2)[:, :, bass.ds(h * 2, 2)]).then_inc(*own.one())
                        dve.tensor_copy(ng[:, :], vT[:, V_NORM:V_NORM + 8][:, bass.ds(h * 2, 2)]).then_inc(*own.one())
                        dve.tensor_copy(pads[:, :, :, :], M["conv_in"][:, :, bass.ds(h * 2, 2), :]).then_inc(*own.one())
                        dve.tensor_copy(tk[:, 0:8, :], M["tok"][:, 0:8, :, bass.ds(h, 1)].squeeze(3)).then_inc(*own.one())
                        dve.tensor_copy(tk[0:64, 8, :], M["tok"][0:64, 8, :, bass.ds(h, 1)].squeeze(2)).then_inc(*own.one())
                        dve.tensor_copy(sel[:, :], ident[0:H, bass.ds(h, 1)].broadcast_to([H, P])).then_inc(*own.one())
                        dve.tensor_copy(hn0[:, :, :], M["n_in"][:, :, :, bass.ds(h, 1)].squeeze(3)).then_inc(*own.one())
                        dve.memset(C[:, :, :], 0.0).then_inc(*own.one())
                        dve.wait_ge(*own.now())
                        dve.tensor_scalar(w_mask[:, :], M["seq_mask"][:, :], tk[0:64, 8, 2:3], None, ALU.mult).then_inc(K["staged"].sem, 1)

                    def conv(h, j):
                        a, i = divmod(j, 2)
                        dst = (q, kk)[a]
                        dve.tensor_copy(zs[:, :, 0:3], pads[:, a, i, :].rearrange("p (b t) -> p b t", t=3)).then_inc(*own.one())
                        link(dve.memset(zc[:, 0:3], 0.0))
                        dve.wait_ge(*K["zc_kept"](h * 12 + 3 * j + 3))
                        ds = dst[:, i, SEQ:T].rearrange("p (b t) -> p b t", t=STOK)
                        tails = M["tails"][:, bass.ds(h * 2 + (8 * a + i), 1), :].squeeze(1)
                        dve.tensor_copy(tails[:, 0:3], zc[:, SEQ:SEQ + 3]).then_inc(*own.one())
                        dve.tensor_copy(tails[:, 3:27].rearrange("p (b t) -> p b t", t=3), zs[:, :, STOK:STOK + 3]).then_inc(*own.one())
                        for w in range(CW):
                            for out, src in ((dst[:, i, 0:SEQ], zc[:, w:w + SEQ]), (ds, zs[:, :, w:w + STOK])):
                                if w == 0:
                                    ins = dve.tensor_scalar(out, src, cw[:, 0, a, i:i + 1], cb[:, a, i:i + 1], ALU.mult, ALU.add)
                                else:
                                    ins = dve.scalar_tensor_tensor(out=out, in0=src, scalar=cw[:, w, a, i:i + 1], in1=out,
                                                                   op0=ALU.mult, op1=ALU.add)
                                if w == CW - 1 and out is ds:
                                    ins.then_inc(K["conv"].sem, 1)
                                else:
                                    ins.then_inc(*own.one())
                            if w < CW - 1:
                                dve.wait_ge(*own.now())

                    def prep(h, b):
                        dve.tensor_copy(cs[:, b % 2, :, DH:DH + 1], hn0[:, :, b:b + 1]).then_inc(*own.one())
                        dve.tensor_scalar(vb[:, :], vx[0:64, 8, :], M["seq_mask"][:, b:b + 1], None, ALU.mult).then_inc(K["prep"].sem, 1)

                    def sequence(h, b):
                        dve.wait_ge(*K["seq_mm"](h * 8 + b + 1))
                        if b == 0:
                            dve.tensor_scalar(inter_s[:, :], ps[0:64, 7, 0:DH + 1], w_mask[:, 0:1], None, ALU.mult).then_inc(*own.one())
                        else:
                            dve.scalar_tensor_tensor(out=inter_s[:, :], in0=ps[0:64, 7, 0:DH + 1], scalar=w_mask[:, b:b + 1],
                                                     in1=inter_s[:, :], op0=ALU.mult, op1=ALU.add).then_inc(*own.one())
                        s = b % 2
                        dve.scalar_tensor_tensor(out=cs[:, s, :, DH:DH + 1], in0=cs[:, s, :, DH:DH + 1], scalar=ap_[:, 8 + b:9 + b],
                                                 in1=ps[:, 3, 300:302].unsqueeze(2), op0=ALU.mult, op1=ALU.add).then_inc(*own.one())
                        dve.scalar_tensor_tensor(out=cs[:, s, :, 0:DH], in0=cs[:, s, :, 0:DH], scalar=ap_[:, 8 + b:9 + b],
                                                 in1=ps[:, 6, 0:512].rearrange("p (i e) -> p i e", i=2), op0=ALU.mult,
                                                 op1=ALU.add).then_inc(K["seq_upd"].sem, 1)
                        dve.wait_ge(*own.now())
                        dve.tensor_copy(M["n_out"][:, :, b, bass.ds(h, 1)], cs[:, s, :, DH:DH + 1]).then_inc(*own.one())
                        if b + 1 < NSEQ:
                            prep(h, b + 1)

                    def stage0(h, p):
                        chunk, c, t0, L, tt = place(p)
                        dve.wait_ge(*K["s0"](h * NJ + p + 1))
                        mask = M["neg_mask"] if chunk else M["neg_diag"]
                        dve.tensor_tensor(ex[0:L, 0:L], mask[:, :], ps[0:L, 3, 128:128 + L], ALU.subtract).then_inc(K["e_ready"].sem, 1)
                        b = seq_at(p, 0)
                        if b is not None:
                            sequence(h, b)
                        dve.wait_ge(*K["e_done"](h * NJ + p + 1))
                        dve.scalar_tensor_tensor(out=st[0:L, 0:L], in0=ps[0:L, 3, 0:L], scalar=1.0 / 16, in1=ex[0:L, 0:L],
                                                 op0=ALU.mult, op1=ALU.mult).then_inc(K["st_done"].sem, 1)

                    def stage1(h, p):
                        chunk, c, t0, L, tt = place(p)
                        dve.wait_ge(*K["s1"](h * NJ + p + 1))
                        if chunk:
                            dve.wait_ge(*K["inter_done"](h * 8 + c + 1))
                        if p:
                            dve.wait_ge(*K["s2"](h * NJ + p))
                        src = inter if chunk else inter_s
                        ins = dve.tensor_tensor(num[0:L, :], src[0:L, :], ps[0:L, 5, 0:DH + 1], ALU.add)
                        if chunk:
                            ins.then_inc(*own.one())
                            dve.wait_ge(*own.now())
                        else:
                            ins.then_inc(K["b5_read"].sem, 1)
                            dve.wait_ge(*K["b5_read"](h * NJ + p + 1))
                        dve.tensor_scalar(den[0:L, 0:1], num[0:L, DH:DH + 1], -1.0, tk[0:L, tt, 3:4], ALU.mult, ALU.max
                                          ).then_inc(*own.one())
                        link(dve.bn_stats(hst[0:L, :], num[0:L, 0:DH]))
                        link(dve.tensor_scalar(den[0:L, 0:1], den[0:L, 0:1], num[0:L, DH:DH + 1], None, ALU.max))
                        dve.reciprocal(den[0:L, 1:2], den[0:L, 0:1]).then_inc(*own.one())
                        link(dve.bn_aggr(hmv[0:L, :], hst[0:L, :]))
                        dve.tensor_scalar(var[0:L, 0:1], hmv[0:L, 1:2], den[0:L, 1:2], den[0:L, 1:2], ALU.mult, ALU.mult
                                          ).then_inc(K["var_ready"].sem, 1)
                        if chunk:
                            dve.scalar_tensor_tensor(out=C[:, :, DH:DH + 1], in0=C[:, :, DH:DH + 1], scalar=ap_[:, c:c + 1],
                                                     in1=ps[:, 5, 300:302].unsqueeze(2), op0=ALU.mult, op1=ALU.add
                                                     ).then_inc(K["b5_read"].sem, 1)
                            dve.scalar_tensor_tensor(out=C[:, :, 0:DH], in0=C[:, :, 0:DH], scalar=ap_[:, c:c + 1],
                                                     in1=ps[:, 6, 0:512].rearrange("p (i e) -> p i e", i=2), op0=ALU.mult,
                                                     op1=ALU.add).then_inc(K["c_upd"].sem, 1)
                        dve.wait_ge(*K["rs_ready"](h * NJ + p + 1))
                        link(dve.tensor_scalar(den[0:L, 0:1], var[0:L, 1:2], den[0:L, 1:2], None, ALU.mult))
                        dve.tensor_scalar(num[0:L, 0:DH], num[0:L, 0:DH], hmv[0:L, 0:1], den[0:L, 0:1], ALU.subtract, ALU.mult
                                          ).then_inc(K["h_ready"].sem, 1)

                    def stage2(h, p):
                        b = seq_at(p, 2)
                        if b is not None:
                            sequence(h, b)

                    def unit(h, u):
                        tile, n = divmod(u, 3)
                        t0, w = UNITS[n]
                        i = tile % 2
                        if tile < 2:
                            return
                        dst = (ob, ub)[tile >= 4][:, i, t0:t0 + w]
                        dve.wait_ge(*K["step_act"](h * 24 + u + 1))
                        if u == 12:
                            dve.wait_ge(*K["ub_in"](h * 16 + 16))
                        dve.tensor_tensor(dst, dst, tmp[:, u % 2, 0:w], ALU.mult).then_inc(K["step_mul"].sem, 1)

                    dve.wait_ge(*K["ones_made"](1))
                    def mix(h, n):
                        t0, w = UNITS[n]
                        dve.wait_ge(*K["h_kept"](h * NJ + (3, 7, NJ)[n]))
                        for i in range(2):
                            dve.wait_ge(*K["step_mul"](h * 18 + 16 + n))
                            link(dve.tensor_tensor(ob[:, i, t0:t0 + w], ob[:, i, t0:t0 + w], q[:, i, t0:t0 + w], ALU.mult))
                            dve.tensor_tensor(ub[:, i, t0:t0 + w], ub[:, i, t0:t0 + w], ob[:, i, t0:t0 + w], ALU.add
                                              ).then_inc(K["mix_sum"].sem, 1)
                        for i in range(2):
                            dve.wait_ge(*K["mix_hi"](h * 6 + 2 * n + i + 1))
                            dve.tensor_tensor(mix_lo[:, i, t0:t0 + w], ub[:, i, t0:t0 + w], mix_hi[:, i, t0:t0 + w].bitcast(F32),
                                              ALU.subtract).then_inc(K["mix_lo"].sem, 1)

                    def body(h, last):
                        stage_head(h)
                        for j in range(4):
                            split(h, j + 2)
                            conv(h, j)
                        dve.wait_ge(*K["vm_kept"](h * NTT + 4))
                        split(h, 6)
                        split(h, 7)
                        dve.wait_ge(*K["ap_mm"](h + 1))
                        dve.tensor_copy(ap_[:, :], ps[:, 3, 0:16]).then_inc(K["ap_kept"].sem, 1)
                        dve.wait_ge(*K["ap_kept"](h + 1))
                        dve.wait_ge(*K["vm_kept"](h * NTT + NTT))
                        prep(h, 0)
                        for kind, a, s in EVENTS:
                            if kind == "stage":
                                (stage0, stage1, stage2)[s](h, a)
                                if (a, s) == (NJ - 1, 1):
                                    mix(h, 1)
                            else:
                                unit(h, a)
                                if a % 3 == 1:
                                    split(h, a // 3 + 8)
                                if a == 21:
                                    mix(h, 0)
                        dve.tensor_copy(M["np_out"][:, :, bass.ds(h, 1)], C[:, :, DH:DH + 1]).then_inc(*own.one())
                        mix(h, 2)
                        for u, (m, n) in enumerate(OUT_ORDER):
                            dve.wait_ge(*K["out_unit"](h * 24 + u + 1))
                            add_out(dve, own, m, n, u % 6, otmp[:, m % 4, :, :], x_added)
                            if not last and u in (9, 13):
                                split(h + 1, (u - 9) // 4)
                        dve.wait_ge(*K["cp_out"](h * 16 + 16))

                    split(0, 0)
                    split(0, 1)
                    for done in stored:
                        dve.wait_ge(*done)
                    with dve.Fori(0, H - 1) as h:
                        own.enter(h, HEAD_STEPS)
                        body(h, False)
                        own.leave(H - 1)
                    body(H - 1, True)

                @block.tensor
                def _(pe):
                    def operands(pair, i, t0, w):
                        wh, wl = (pair_part(M, kd, pair % 2, i) for kd in ("hi", "lo"))
                        return [(wh[:, k, :], wl[:, k, :], hhi[:, k, t0:t0 + w], hlo[:, k, t0:t0 + w]) for k in range(KT)]

                    def sequence(h, p, stage):
                        b = seq_at(p, stage)
                        if b is None:
                            return
                        s = b % 2
                        if stage == 2:
                            pe.wait_ge(*K["st_done"](h * NJ + p + 1))
                            pe.wait_ge(*K["seq_upd"](h * 8 + b))
                            state_n(h, b)
                        pe.wait_ge(*c_in[s](h * 64 + 16 * (b // 2 + 1)))
                        if b:
                            pe.wait_ge(*K["seq_upd"](h * 8 + b))
                        if stage == 0 and p:
                            pe.wait_ge(*K["c_upd"](h * 8 + p))
                        if stage == 2:
                            pe.wait_ge(*K["c_upd"](h * 8 + p + 1))
                        for i in range(2):
                            pe.matmul(ps[0:64, 7, 0:DH + 1], q[:, i, SEQ:T], cs[:, s, i, :], start=(i == 0), stop=(i == 1))
                        for i in range(2):
                            ins = pe.matmul(ps[:, 6, 256 * i:256 * i + 256], kws[:, 128 * i:128 * i + 128], vb[:, 0:DH],
                                            start=True, stop=True)
                        ins.then_inc(K["seq_mm"].sem, 1)

                    def state_n(h, b):
                        pe.wait_ge(*K["prep"](h * 8 + b + 1))
                        pe.wait_ge(*K["kw_done"](h * NJ + 1))
                        for i in range(2):
                            ins = pe.matmul(ps[:, 3, 300 + i:301 + i], kws[:, 128 * i:128 * i + 128], vb[:, DH:DH + 1],
                                            start=True, stop=True)
                        return ins

                    def stage0(h, p):
                        chunk, c, t0, L, tt = place(p)
                        if chunk:
                            if p:
                                pe.wait_ge(*K["h_kept"](h * NJ + p))
                            else:
                                pe.wait_ge(*K["kw_done"](h * NJ + 1))
                            for i in range(2):
                                ins = pe.transpose(ps[:, 4, 128 * i:128 * i + 128], kk[:, i, t0:t0 + L], ident[:, :])
                            ins.then_inc(K["kT"].sem, 1)
                        if p:
                            pe.wait_ge(*K["st_done"](h * NJ + p))
                            if p <= 4:
                                pe.wait_ge(*K["seq_upd"](h * 8 + 2 * p))
                        else:
                            pe.wait_ge(*K["ap_kept"](h + 1))
                        if not chunk:
                            pe.sem_inc(K["passed"].sem, 1)
                        for i in range(2):
                            pe.matmul(ps[0:L, 3, 0:L], kk[:, i, t0:t0 + L], q[:, i, t0:t0 + L], start=(i == 0), stop=(i == 1))
                        ins = pe.matmul(ps[0:L, 3, 128:128 + L], sel[:, 0:L], M["m_rows"][:, t0:t0 + L], start=True, stop=True)
                        if seq_at(p, 0) is not None:
                            ins = state_n(h, seq_at(p, 0))
                        ins.then_inc(K["s0"].sem, 1)
                        sequence(h, p, 0)

                    def stage1(h, p):
                        chunk, c, t0, L, tt = place(p)
                        if chunk:
                            pe.wait_ge(*K["kw_done"](h * NJ + c + 2))
                            if c:
                                pe.wait_ge(*K["c_upd"](h * 8 + c))
                            for i in range(2):
                                ins = pe.matmul(ps[:, 4, 0:DH + 1], q[:, i, t0:t0 + L], C[:, i, :], start=(i == 0), stop=(i == 1))
                            ins.then_inc(K["inter_mm"].sem, 1)
                        pe.wait_ge(*K["st_done"](h * NJ + p + 1))
                        if p:
                            pe.wait_ge(*K["b5_read"](h * NJ + p))
                        if not chunk:
                            pe.sem_inc(K["passed"].sem, 1)
                        ins = pe.matmul(ps[0:L, 5, 0:DH + 1], st[0:L, 0:L], vx[0:L, tt, :], start=True, stop=True)
                        if chunk:
                            for i in range(2):
                                pe.matmul(ps[:, 5, 300 + i:301 + i], kw[:, 128 * i:128 * i + 128], vx[:, tt, DH:DH + 1],
                                          start=True, stop=True)
                            if p < 4:
                                pe.wait_ge(*K["seq_upd"](h * 8 + 2 * p + 1))
                            for i in range(2):
                                ins = pe.matmul(ps[:, 6, 256 * i:256 * i + 256], kw[:, 128 * i:128 * i + 128], vx[:, tt, 0:DH],
                                                start=True, stop=True)
                        ins.then_inc(K["s1"].sem, 1)

                    def stage2(h, p):
                        chunk, c, t0, L, tt = place(p)
                        pe.wait_ge(*K["h_ready"](h * NJ + p + 1))
                        if chunk:
                            pe.wait_ge(*K["inter_done"](h * 8 + c + 1))
                        else:
                            pe.wait_ge(*K["h_kept"](h * NJ + p))
                        if not chunk:
                            pe.sem_inc(K["passed"].sem, 1)
                        for i in range(2):
                            ins = pe.transpose(ps[:, 4, 128 * i:128 * i + L], num[0:L, 128 * i:128 * i + 128], ident[0:L, 0:L])
                        ins.then_inc(K["s2"].sem, 1)
                        sequence(h, p, 2)

                    def unit(h, u):
                        tile, n = divmod(u, 3)
                        t0, w = UNITS[n]
                        if n == 0:
                            pe.wait_ge(*K["lo"](h * 16 + 6 + tile + 1))
                        if u < 3:
                            pe.wait_ge(*K["vm_kept"](h * NTT + 6 + u + 1))
                        else:
                            pe.wait_ge(*K["step_act"](h * 24 + u - 2))
                        ins = three(pe, ps[:, n, 0:w], operands(3 + tile // 2, tile % 2, t0, w))
                        ins.then_inc(K["step_unit"].sem, 1)

                    def body(h, last):
                        for j in range(4):
                            pe.wait_ge(*K["lo"](h * 16 + j + 1))
                            for n, (t0, w) in enumerate(UNITS):
                                if j:
                                    pe.wait_ge(*K["zc_kept"](h * 12 + 3 * (j - 1) + n + 1))
                                else:
                                    pe.wait_ge(*x_added(h * 24 - 5 + n))
                                three(pe, ps[:, n, 0:w], operands(j // 2, j % 2, t0, w)).then_inc(K["qk_unit"].sem, 1)
                        pe.wait_ge(*K["lo"](h * 16 + 6))
                        wh, wl = (M["w_" + kd][0][:, :].rearrange("p (k n) -> p k n", k=KT) for kd in ("hi", "lo"))
                        for t in range(NTT):
                            if t < 3:
                                pe.wait_ge(*K["zc_kept"](h * 12 + 9 + t + 1))
                            else:
                                pe.wait_ge(*K["vm_kept"](h * NTT + t - 2))
                            a = 128 * t if t < 8 else T - P
                            three(pe, ps[:, t % 3, 0:DH], [(hhi[:, k, a:a + P], hlo[:, k, a:a + P], wh[:, k, :], wl[:, k, :])
                                                           for k in range(KT)]).then_inc(K["vm_unit"].sem, 1)
                        pe.wait_ge(*K["staged"](h + 1))
                        pe.matmul(ps[:, 3, 0:16], sel[:, :], M["a_prev"][:, :], start=True, stop=True).then_inc(K["ap_mm"].sem, 1)
                        pe.wait_ge(*K["qk_ready"](h * 4 + 4))
                        pe.sem_inc(K["passed"].sem, 1)
                        for i in range(2):
                            ins = pe.transpose(ps[0:64, 4, 128 * i:128 * i + 128], kk[:, i, SEQ:T], ident[:, :])
                        ins.then_inc(K["kT"].sem, 1)
                        pe.wait_ge(*K["vm_kept"](h * NTT + NTT))
                        for kind, a, s in EVENTS:
                            if kind == "stage":
                                (stage0, stage1, stage2)[s](h, a)
                            else:
                                unit(h, a)
                        pe.wait_ge(*K["lo"](h * 16 + 16))
                        for u, (m, n) in enumerate(OUT_ORDER):
                            t0, w = UNITS[n]
                            if u < 3:
                                pe.wait_ge(*K["step_act"](h * 24 + 21 + u + 1))
                            elif u >= 6:
                                pe.wait_ge(*x_added(h * 24 + (u - 5)))
                            if m == 0:
                                pe.wait_ge(*K["mix_lo"](h * 6 + 2 * n + 2))
                            ms = slice(128 * m, 128 * m + 128)
                            three(pe, ps[:, u % 6, 0:w], [(pair_part(M, "hi", 1, i, True)[:, ms], pair_part(M, "lo", 1, i, True)[:, ms],
                                                           mix_hi[:, i, t0:t0 + w], mix_lo[:, i, t0:t0 + w]) for i in range(2)]
                                  ).then_inc(K["out_unit"].sem, 1)
                            if last and u % 4 == 1 and u < 20:
                                q_ = u // 4
                                if q_ >= 2:
                                    pe.wait_ge(*state_kept(q_ - 1))
                                for i in range(4 if q_ < 4 else 2):
                                    if q_ < 4:
                                        ins = pe.transpose(ps[0:27, 6 + q_ % 2, 128 * i:128 * i + 128], M["tails"][:, 4 * q_ + i, :], ident[:, :])
                                    else:
                                        pe.transpose(ps[0:32, 6, 128 * i:128 * i + 128],
                                                     M["n_out"][:, i, :, :].rearrange("p b h -> p (b h)"), ident[:, :])
                                        ins = pe.transpose(ps[0:H, 6, DH + 128 * i:DH + 128 * i + 128], M["np_out"][:, i, :], ident[:, :])
                                ins.then_inc(state_turned.sem, 1)

                    with pe.Fori(0, H - 1) as h:
                        body(h, False)
                    body(H - 1, True)
            sq.close()
            x_added.base += 24 * H

        def final_norm(norm):
            ar.at = work
            y = y_out
            row = ar.put("y_row", [P, 4, D])
            turned, kept = cnt("y_turned"), [cnt("y_kept_v"), cnt("y_kept_a")]
            out = [cnt(f"y_out{s}") for s in range(4)]
            with nc.Block() as block:
                @block.tensor
                def _(pe):
                    norm.means(pe)
                    for t in range(NTT):
                        n = 64 if t == 8 else P
                        if t % 3 == 0:
                            pe.wait_ge(*hi_done(KT * (t // 3 + 1)))
                        if t == 8:
                            pe.wait_ge(*hi_done(3 * KT + 1))
                        for hf in range(2):
                            u = 2 * t + hf
                            if t >= 4:
                                pe.wait_ge(*kept[hf](t - 3))
                            for f in range(4):
                                ins = pe.transpose(ps[0:n, u % 8, 128 * f:128 * f + 128], y[:, 4 * hf + f, 128 * t:128 * t + n], ident[:, :])
                            ins.then_inc(turned.sem, 1)

                def keep(eng, hf, t):
                    n = 64 if t == 8 else P
                    eng.wait_ge(*turned(2 * t + hf + 1))
                    if t >= 4:
                        eng.wait_ge(*out[t % 4](16 * (t // 4)))
                    dst, src = row[0:n, t % 4, 512 * hf:512 * hf + 512], ps[0:n, (2 * t + hf) % 8, :]
                    if hf == 0:
                        eng.tensor_copy(dst, src).then_inc(kept[0].sem, 1)
                    else:
                        eng.activation(dst, src, ACT.Copy).then_inc(kept[1].sem, 1)

                @block.vector
                def _(dve):
                    norm.factors(dve)
                    norm.unit(dve, 0)
                    norm.unit(dve, 1)
                    for t in range(3):
                        keep(dve, 0, t)
                    norm.unit(dve, 2)
                    norm.samples(dve)
                    for t in range(3, NTT):
                        keep(dve, 0, t)

                @block.scalar
                def _(act):
                    norm.roots(act)
                    for j in range(3 * KT):
                        norm.high(act, j)
                        if j == 2 * KT - 1:
                            for t in range(3):
                                keep(act, 1, t)
                    norm.high_samples(act)
                    for t in range(3, NTT):
                        keep(act, 1, t)

                @block.sync
                def _(sp):
                    for t in range(NTT):
                        n = 64 if t == 8 else P
                        sp.wait_ge(*kept[0](t + 1))
                        sp.wait_ge(*kept[1](t + 1))
                        dst = O["y_prompt"][0, 128 * t:128 * t + P, :] if t < 8 else O["y_sample"].rearrange("b t d -> (b t) d")
                        sp.dma_start(dst, row[0:n, t % 4, :]).then_inc(out[t % 4].sem, 16)
                    for s in range(4):
                        sp.wait_ge(*out[s](16 * (3 if s == 0 else 2)))
            norm.close()

        bring_in()
        ffn(I["w_ffn1_in"][0], I["w_ffn1_out"][0], Norm(V_FFN1, 0, 8, gate=16, factor=0.5), ada_first=12)
        M, after = mixer_memory()
        ar.at = after
        v = ar.put("v", [P, NTT, D])
        mixed_d = nc.dram_tensor("mixed", [D, T], F32, kind="Internal").ap()
        head_w_in = [cnt("h_w_in0"), cnt("h_w_in1")]
        S = gates_and_v(M, after, ar.at, v, Norm(V_MIX, 24, 32, gate=40, factor=1.0))
        stored = spatial(M, S, after + NTT * D * 4, v, mixed_d)
        heads(M, after, mixed_d, stored)
        ffn(I["w_ffn2_in"][0], I["w_ffn2_out"][0], Norm(V_FFN2, 48, 56, gate=64, factor=0.5))
        final_norm(Norm(V_FINAL, ADA_T, ADA_T + KT, final=True))


_INS = ['x_prompt', 'x_sample', 'c_prompt', 'c_sample', 'state_mlstm_C', 'state_mlstm_n', 'state_mlstm_m', 'state_conv',
        'w_ada', 'b_ada', 'g_ffn1', 'w_ffn1_in', 'w_ffn1_out', 'g_mix', 'w_in', 'b_gates', 'conv_w', 'conv_b',
        'gmlp_ln_g', 'gmlp_ln_b', 'gmlp_ws', 'gmlp_bs', 'mlstm_norm_g', 'w_out', 'g_ffn2', 'w_ffn2_in', 'w_ffn2_out',
        'w_ada_final', 'b_ada_final', 'g_final']
_OUTS = [("y_prompt", (1, SEQ, D)), ("y_sample", (NSEQ, STOK, D)), ("C_prompt", (1, 1, H, DH, DH)), ("n_prompt", (1, 1, H, DH)),
         ("m_prompt", (1, 1, H)), ("conv_prompt", (1, 1, CW - 1, 2 * D)), ("C_sample", (1, NSEQ, H, DH, DH)),
         ("n_sample", (1, NSEQ, H, DH)), ("m_sample", (1, NSEQ, H)), ("conv_sample", (1, NSEQ, CW - 1, 2 * D)),
         ("v_sample", (1, NSEQ, STOK, D))]


def kernel(**inputs):
    import numpy as _np
    import concourse.bacc as _bacc
    from concourse.bass_utils import run_bass_kernel_spmd as _run

    nc = _bacc.Bacc("TRN2", target_bir_lowering=False, num_devices=1, dynamic_dma_scratch_size=4096)
    arrays = {f"in_{n}": _np.ascontiguousarray(inputs[n]) for n in _INS}
    ins = {n: nc.dram_tensor(f"in_{n}", arrays[f"in_{n}"].shape, F32, kind="ExternalInput").ap() for n in _INS}
    outs = {n: nc.dram_tensor(f"out_{n}", s, F32, kind="ExternalOutput").ap() for n, s in _OUTS}
    layer(nc, ins, outs)
    r = _run(nc, [arrays], core_ids=[0])
    return tuple(r.results[0][f"out_{n}"] for n, _ in _OUTS)
```
